# Optimizing a Trainium2 kernel written in Bass

```python
import math
import jax
import jax.numpy as jnp
from jax import lax
import numpy as np

D_MODEL = 1024
BATCH = 1
SEQ = 256
DEPTH = 2

GRID_W = 64
CTX_LEN = 256
N_MOD = 6
RMS_EPS = 1e-6

ML_HEADS = 4
ML_DQK = D_MODEL // 8
ML_DV = D_MODEL // 4
ML_CHUNK = 128

SS_INNER = D_MODEL
SS_HEADDIM = 64
SS_HEADS = SS_INNER // SS_HEADDIM
SS_GROUPS = 2
SS_RPG = SS_HEADS // SS_GROUPS
SS_STATE = 128
SS_CHUNK = 64
SS_CONV_CH = SS_INNER + 2 * SS_GROUPS * SS_STATE

MIX_W = ML_HEADS * ML_DV + SS_INNER
AB_SIZES = (ML_HEADS * ML_DQK, ML_HEADS * ML_DQK, ML_HEADS * ML_DV, ML_HEADS * ML_DV, 4 * ML_HEADS,
            SS_INNER, SS_CONV_CH, 2 * SS_HEADS)
AB_COLS = sum(AB_SIZES)

RW_HEADSZ = 64
RW_HEADS = D_MODEL // RW_HEADSZ
RW_DECAY_LORA = 64
RW_ICLR_LORA = 64
RW_GATE_LORA = 160
RW_GN_EPS = 64e-5

N_EXPERTS = 16
EC_CAPACITY_FACTOR = 2
EXPERT_FF = 11 * D_MODEL // 8

kernel_name = 'hybrid_mlstm_ssd_rwkv7_ec_moe_dit'

def rmsnorm(x, g, eps=RMS_EPS):
    xf = x.astype(jnp.float32)
    y = xf * lax.rsqrt(jnp.mean(xf * xf, axis=-1, keepdims=True) + eps)
    return (y * g.astype(jnp.float32)).astype(x.dtype)

def modulate(h, shift, scale):
    return h * (1.0 + scale) + shift

def mlstm_scan(q, k, v, ig, fg, state):
    bsz, nh, t, dk = q.shape
    dv = v.shape[-1]
    L = ML_CHUNK
    nc = t // L
    q = q.reshape(bsz, nh, nc, L, dk)
    k = k.reshape(bsz, nh, nc, L, dk)
    v = v.reshape(bsz, nh, nc, L, dv)
    ig = ig.reshape(bsz, nh, nc, L)
    b = jnp.cumsum(jax.nn.log_sigmoid(fg).reshape(bsz, nh, nc, L), axis=-1)
    b_end = b[..., -1]
    lw = b_end[..., None] - b + ig
    m_loc = jnp.max(lw, axis=-1)
    wgt = jnp.exp(lw - m_loc[..., None])
    c_loc = jnp.einsum('bhcsv,bhcsk->bhcvk', v * wgt[..., None], k)
    n_loc = jnp.einsum('bhcs,bhcsk->bhck', wgt, k)

    def step(carry, inp):
        c_st, n_st, m_st = carry
        cl, nl, ml, be = inp
        m_new = jnp.maximum(be + m_st, ml)
        a = jnp.exp(be + m_st - m_new)
        g = jnp.exp(ml - m_new)
        c_new = a[..., None, None] * c_st + g[..., None, None] * cl
        n_new = a[..., None] * n_st + g[..., None] * nl
        return (c_new, n_new, m_new), (c_st, n_st, m_st)

    xs = tuple(jnp.moveaxis(u, 2, 0) for u in (c_loc, n_loc, m_loc, b_end))
    final, (c_prev, n_prev, m_prev) = lax.scan(step, state, xs)
    c_prev = jnp.moveaxis(c_prev, 0, 2)
    n_prev = jnp.moveaxis(n_prev, 0, 2)
    m_prev = jnp.moveaxis(m_prev, 0, 2)
    causal = jnp.tril(jnp.ones((L, L), dtype=bool))
    log_d = jnp.where(causal, b[..., :, None] - b[..., None, :] + ig[..., None, :], -jnp.inf)
    log_inter = b + m_prev[..., None]
    m_row = jnp.maximum(jnp.max(log_d, axis=-1), log_inter)
    s = jnp.einsum('bhcjk,bhcsk->bhcjs', q, k) * jnp.exp(log_d - m_row[..., None])
    w_inter = jnp.exp(log_inter - m_row)
    num = jnp.einsum('bhcjs,bhcsv->bhcjv', s, v) + w_inter[..., None] * jnp.einsum('bhcvk,bhcjk->bhcjv', c_prev, q)
    den = jnp.sum(s, axis=-1) + w_inter * jnp.einsum('bhck,bhcjk->bhcj', n_prev, q)
    h = num / jnp.maximum(jnp.abs(den), jnp.exp(-m_row))[..., None]
    return h.reshape(bsz, nh, t, dv), final

def mlstm_branch(parts_c, parts_l, gate_b, norm_g, ctx_out):
    def heads(parts):
        q, k, v, o, gates = parts
        bsz, t, _ = q.shape
        split = lambda u, dh: u.reshape(bsz, t, ML_HEADS, dh).transpose(0, 2, 1, 3)
        gates = (gates.reshape(bsz, t, 2, 2, ML_HEADS) + gate_b).transpose(2, 3, 0, 4, 1)
        return split(q, ML_DQK), split(k, ML_DQK) * (ML_DQK ** -0.5), split(v, ML_DV), gates, o

    def bidir(hp, init):
        q, k, v, g, _ = hp
        fl = lambda u: jnp.flip(u, axis=2)
        h_f, s_f = mlstm_scan(q, k, v, g[0, 0], g[0, 1], init[0])
        h_b, s_b = mlstm_scan(fl(q), fl(k), fl(v), fl(g[1, 0]), fl(g[1, 1]), init[1])
        return h_f + fl(h_b), (s_f, s_b)

    def post(h, o):
        bsz, _, t, _ = h.shape
        h = rmsnorm(jnp.swapaxes(h, 1, 2), norm_g.reshape(ML_HEADS, ML_DV))
        return h.reshape(bsz, t, ML_HEADS * ML_DV) * jax.nn.sigmoid(o)

    hc, hl = heads(parts_c), heads(parts_l)
    bsz = hc[0].shape[0]
    zero = (jnp.zeros((bsz, ML_HEADS, ML_DV, ML_DQK), jnp.float32),
            jnp.zeros((bsz, ML_HEADS, ML_DQK), jnp.float32),
            jnp.zeros((bsz, ML_HEADS), jnp.float32))
    y_c, ctx_states = bidir(hc, (zero, zero))
    y_l, _ = bidir(hl, ctx_states)
    return (post(y_c, hc[4]) if ctx_out else None), post(y_l, hl[4])

def depthwise_conv2d(u, w, bias, width):
    bsz, t, ch = u.shape
    img = u.reshape(bsz, t // width, width, ch)
    out = lax.conv_general_dilated(img, w.astype(u.dtype)[:, :, None, :], (1, 1), 'SAME',
                                   dimension_numbers=('NHWC', 'HWIO', 'NHWC'), feature_group_count=ch)
    return out.reshape(bsz, t, ch) + bias

def ssd_scan(xs, dt, a, bm, cm, h0):
    bsz, t, ng, nr, hp = xs.shape
    ns = bm.shape[-1]
    L = SS_CHUNK
    nc = t // L
    x = (xs * dt[..., None]).reshape(bsz, nc, L, ng, nr, hp)
    bc = bm.reshape(bsz, nc, L, ng, ns)
    cc = cm.reshape(bsz, nc, L, ng, ns)
    acum = jnp.cumsum((dt * a).reshape(bsz, nc, L, ng, nr), axis=2)
    a_end = acum[:, :, -1]
    s_loc = jnp.einsum('bclgrp,bclgn->bcgrpn', x * jnp.exp(a_end[:, :, None] - acum)[..., None], bc)

    def step(h, inp):
        sl, ae = inp
        return jnp.exp(ae)[..., None, None] * h + sl, h

    h_final, h_prev = lax.scan(step, h0, (jnp.moveaxis(s_loc, 1, 0), jnp.moveaxis(a_end, 1, 0)))
    h_prev = jnp.moveaxis(h_prev, 0, 1)
    causal = jnp.tril(jnp.ones((L, L), dtype=bool))[:, :, None, None]
    seg = jnp.exp(jnp.where(causal, acum[:, :, :, None] - acum[:, :, None, :], -jnp.inf))
    mmat = jnp.einsum('bcjgn,bcsgn->bcjsg', cc, bc)[..., None] * seg
    y = jnp.einsum('bcjsgr,bcsgrp->bcjgrp', mmat, x)
    y = y + jnp.einsum('bcjgn,bcgrpn->bcjgrp', cc, h_prev) * jnp.exp(acum)[..., None]
    return y.reshape(bsz, t, ng, nr, hp), h_final

def ssd_branch(parts_c, parts_l, conv_w, conv_b, dt_bias, a_log, d_skip, norm_g, ctx_out):
    a = -jnp.exp(a_log.astype(jnp.float32)).reshape(2, SS_GROUPS, SS_RPG)

    def prep(parts, width):
        z, xbc, dt = parts
        xbc = jax.nn.silu(depthwise_conv2d(xbc, conv_w, conv_b, width))
        xs, bm, cm = jnp.split(xbc, [SS_INNER, SS_INNER + SS_GROUPS * SS_STATE], axis=-1)
        bsz, t, _ = xs.shape
        xs = xs.reshape(bsz, t, SS_GROUPS, SS_RPG, SS_HEADDIM)
        bm = bm.reshape(bsz, t, SS_GROUPS, SS_STATE)
        cm = cm.reshape(bsz, t, SS_GROUPS, SS_STATE)
        dt = jax.nn.softplus(dt.reshape(bsz, t, 2, SS_HEADS) + dt_bias).reshape(bsz, t, 2, SS_GROUPS, SS_RPG)
        return z, xs, bm, cm, dt

    def bidir(pre, init):
        _, xs, bm, cm, dt = pre
        fl = lambda u: jnp.flip(u, axis=1)
        y_f, s_f = ssd_scan(xs, dt[:, :, 0], a[0], bm, cm, init[0])
        y_b, s_b = ssd_scan(fl(xs), fl(dt[:, :, 1]), a[1], fl(bm), fl(cm), init[1])
        y = y_f + fl(y_b) + d_skip.reshape(SS_GROUPS, SS_RPG)[..., None] * xs
        return y, (s_f, s_b)

    def post(pre, y):
        z = pre[0]
        bsz, t, _ = z.shape
        u = (y.reshape(bsz, t, SS_INNER) * jax.nn.silu(z)).reshape(bsz, t, SS_GROUPS, SS_INNER // SS_GROUPS)
        return rmsnorm(u, norm_g.reshape(SS_GROUPS, -1)).reshape(bsz, t, SS_INNER)

    pc = prep(parts_c, parts_c[0].shape[1])
    pl = prep(parts_l, GRID_W)
    bsz = pc[1].shape[0]
    zero = jnp.zeros((bsz, SS_GROUPS, SS_RPG, SS_HEADDIM, SS_STATE), jnp.float32)
    y_c, ctx_states = bidir(pc, (zero, zero))
    y_l, _ = bidir(pl, ctx_states)
    return (post(pc, y_c) if ctx_out else None), post(pl, y_l)

def mixer_ab(h_c, h_l, w_in, w_out, gate_b, ml_norm_g, conv_w, conv_b, dt_bias, a_log, d_skip, ss_norm_g, ctx_out):
    splits = np.cumsum(AB_SIZES)[:-1].tolist()
    pc = jnp.split((h_c @ w_in).astype(jnp.float32), splits, axis=-1)
    pl = jnp.split((h_l @ w_in).astype(jnp.float32), splits, axis=-1)
    ml_c, ml_l = mlstm_branch(pc[:5], pl[:5], gate_b, ml_norm_g, ctx_out)
    ss_c, ss_l = ssd_branch(pc[5:], pl[5:], conv_w, conv_b, dt_bias, a_log, d_skip, ss_norm_g, ctx_out)
    out_l = (jnp.concatenate([ml_l, ss_l], axis=-1) @ w_out).astype(h_l.dtype)
    out_c = (jnp.concatenate([ml_c, ss_c], axis=-1) @ w_out).astype(h_c.dtype) if ctx_out else None
    return out_c, out_l

def rwkv7_scan(r, w, k, v, a, b, s0, reverse):
    def step(s, inp):
        rt, wt, kt, vt, at, bt = inp
        sa = jnp.einsum('bhvk,bhk->bhv', s, at)
        s = s * wt[..., None, :] + sa[..., None] * bt[..., None, :] + vt[..., None] * kt[..., None, :]
        return s, jnp.einsum('bhvk,bhk->bhv', s, rt)

    xs = tuple(jnp.swapaxes(u, 0, 1) for u in (r, w, k, v, a, b))
    s_final, ys = lax.scan(step, s0, xs, reverse=reverse)
    return jnp.swapaxes(ys, 0, 1), s_final

def mixer_rwkv(h_c, h_l, mu, wr, wk, wv, wo, w0, w1, w2, a0, a1, a2, g1, g2, k_k, k_a, r_k, lnx_g, lnx_b, ctx_out):
    out_dtype = h_l.dtype

    def heads(u):
        return u.reshape(*u.shape[:-1], RW_HEADS, RW_HEADSZ)

    def prep(h):
        h = h.astype(jnp.float32)
        prev = jnp.pad(h[:, :-1], ((0, 0), (1, 0), (0, 0)))
        nxt = jnp.pad(h[:, 1:], ((0, 0), (0, 1), (0, 0)))
        xx = 0.5 * (prev + nxt) - h
        xr, xw, xk, xv, xa, xg = [h + xx * mu[n] for n in range(6)]
        r = xr @ wr
        k = xk @ wk
        v = xv @ wv
        lw = w0[:, None, None, :] + jnp.einsum('ebtr,erd->ebtd', jnp.tanh(jnp.einsum('btd,edr->ebtr', xw, w1)), w2)
        decay = jnp.exp(-jnp.exp(-jax.nn.softplus(-lw) - 0.5))
        a = jax.nn.sigmoid(a0 + (xa @ a1) @ a2)
        g = jax.nn.sigmoid(xg @ g1) @ g2
        kk = heads(k * k_k)
        kk = kk * lax.rsqrt(jnp.sum(kk * kk, axis=-1, keepdims=True) + 1e-12)
        k = k * (1.0 + (a - 1.0) * k_a)
        return heads(r), heads(decay), heads(k), heads(v), -kk, kk * heads(a), g

    def bidir(pre, init):
        r, decay, k, v, aa, bb, _ = pre
        y_f, s_f = rwkv7_scan(r, decay[0], k, v, aa, bb, init[0], False)
        y_b, s_b = rwkv7_scan(r, decay[1], k, v, aa, bb, init[1], True)
        return y_f + y_b, (s_f, s_b)

    def post(pre, y):
        r, _, k, v, _, _, g = pre
        bsz, t = y.shape[:2]
        mean = jnp.mean(y, axis=-1, keepdims=True)
        var = jnp.mean(jnp.square(y - mean), axis=-1, keepdims=True)
        y = ((y - mean) * lax.rsqrt(var + RW_GN_EPS)).reshape(bsz, t, D_MODEL) * lnx_g + lnx_b
        y = y + (jnp.sum(r * k * r_k, axis=-1, keepdims=True) * v).reshape(bsz, t, D_MODEL)
        return ((y * g) @ wo).astype(out_dtype)

    pc, pl = prep(h_c), prep(h_l)
    bsz = h_l.shape[0]
    zero = jnp.zeros((bsz, RW_HEADS, RW_HEADSZ, RW_HEADSZ), jnp.float32)
    y_c, ctx_states = bidir(pc, (zero, zero))
    y_l, _ = bidir(pl, ctx_states)
    return (post(pc, y_c) if ctx_out else None), post(pl, y_l)

def ec_moe(h, router_w, w1, w3, w2):
    bsz, n, d = h.shape
    cap = EC_CAPACITY_FACTOR * n // N_EXPERTS
    affinity = jax.nn.softmax((h @ router_w).astype(jnp.float32), axis=-1)
    gate, idx = lax.top_k(jnp.swapaxes(affinity, 1, 2), cap)
    xg = jax.vmap(lambda hb, ib: hb[ib])(h, idx)
    hid = jax.nn.silu(jnp.einsum('becd,edf->becf', xg, w1)) * jnp.einsum('becd,edf->becf', xg, w3)
    out = jnp.einsum('becf,efd->becd', hid, w2) * gate[..., None].astype(h.dtype)
    return jax.vmap(lambda ob, ib: jnp.zeros((n, d), ob.dtype).at[ib.reshape(-1)].add(ob.reshape(-1, d)))(out, idx)

def channel_sublayer(x, mod, ng, router_w, w1, w3, w2):
    h = modulate(rmsnorm(x, ng[2]), mod[3], mod[4])
    return x + mod[5] * rmsnorm(ec_moe(h, router_w, w1, w3, w2), ng[3])

def setup_inputs(seed: int = 0) -> dict:
    keys = jax.random.split(jax.random.key(seed), 48)
    counter = [0]

    def nxt():
        counter[0] += 1
        return keys[counter[0] - 1]

    def nrm(shape, scale):
        return jax.random.normal(nxt(), shape, jnp.float32) * scale

    def uni(shape, lo, hi):
        return jax.random.uniform(nxt(), shape, jnp.float32, lo, hi)

    d, e, f = D_MODEL, N_EXPERTS, EXPERT_FF
    ne, no = (DEPTH + 1) // 2, DEPTH // 2
    dt0 = jnp.exp(uni((ne, 2, SS_HEADS), math.log(1e-3), math.log(1e-1)))
    return {
        'x': nrm((BATCH, SEQ, d), 1.0),
        'c': nrm((BATCH, d), 1.0),
        'ctx': nrm((BATCH, CTX_LEN, d), 1.0),
        'c_ctx': nrm((d,), 1.0),
        'ada_w': nrm((DEPTH, d, N_MOD * d), 0.5 * d ** -0.5),
        'ada_b': nrm((DEPTH, N_MOD * d), 0.02),
        'norm_g': 1.0 + nrm((DEPTH, 4, d), 0.02),
        'router_w': nrm((DEPTH, d, e), d ** -0.5),
        'exp_w1': nrm((DEPTH, e, d, f), d ** -0.5),
        'exp_w3': nrm((DEPTH, e, d, f), d ** -0.5),
        'exp_w2': nrm((DEPTH, e, f, d), f ** -0.5),
        'ab_w_in': nrm((ne, d, AB_COLS), d ** -0.5),
        'ab_w_out': nrm((ne, MIX_W, d), MIX_W ** -0.5),
        'ml_gate_b': jnp.array([0.0, 3.0], jnp.float32)[None, None, :, None] + nrm((ne, 2, 2, ML_HEADS), 0.3),
        'ml_norm_g': 1.0 + nrm((ne, ML_HEADS * ML_DV), 0.02),
        'ss_conv_w': nrm((ne, 3, 3, SS_CONV_CH), 1.0 / 3.0),
        'ss_conv_b': nrm((ne, SS_CONV_CH), 0.02),
        'ss_dt_bias': dt0 + jnp.log(-jnp.expm1(-dt0)),
        'ss_A_log': jnp.log(uni((ne, 2, SS_HEADS), 1.0, 16.0)),
        'ss_D': 1.0 + nrm((ne, SS_HEADS), 0.1),
        'ss_norm_g': 1.0 + nrm((ne, SS_INNER), 0.02),
        'rw_mu': uni((no, 6, d), 0.0, 1.0),
        'rw_wr': nrm((no, d, d), d ** -0.5),
        'rw_wk': nrm((no, d, d), d ** -0.5),
        'rw_wv': nrm((no, d, d), d ** -0.5),
        'rw_wo': nrm((no, d, d), d ** -0.5),
        'rw_w0': uni((no, 2, d), -6.5, -1.5),
        'rw_w1': nrm((no, 2, d, RW_DECAY_LORA), d ** -0.5),
        'rw_w2': nrm((no, 2, RW_DECAY_LORA, d), 0.1 * RW_DECAY_LORA ** -0.5),
        'rw_a0': nrm((no, d), 0.1),
        'rw_a1': nrm((no, d, RW_ICLR_LORA), d ** -0.5),
        'rw_a2': nrm((no, RW_ICLR_LORA, d), 0.1 * RW_ICLR_LORA ** -0.5),
        'rw_g1': nrm((no, d, RW_GATE_LORA), d ** -0.5),
        'rw_g2': nrm((no, RW_GATE_LORA, d), RW_GATE_LORA ** -0.5),
        'rw_kk': 0.85 + nrm((no, d), 0.02),
        'rw_ka': 1.0 + nrm((no, d), 0.02),
        'rw_rk': nrm((no, RW_HEADS, RW_HEADSZ), 0.1),
        'rw_lnx_g': 1.0 + nrm((no, d), 0.02),
        'rw_lnx_b': nrm((no, d), 0.02),
    }

def reference(x, c, ctx, c_ctx, ada_w, ada_b, norm_g, router_w, exp_w1, exp_w3, exp_w2,
              ab_w_in, ab_w_out, ml_gate_b, ml_norm_g, ss_conv_w, ss_conv_b, ss_dt_bias, ss_A_log, ss_D, ss_norm_g,
              rw_mu, rw_wr, rw_wk, rw_wv, rw_wo, rw_w0, rw_w1, rw_w2, rw_a0, rw_a1, rw_a2, rw_g1, rw_g2,
              rw_kk, rw_ka, rw_rk, rw_lnx_g, rw_lnx_b):
    sc = jax.nn.silu(c)
    sc_ctx = jax.nn.silu(c_ctx)
    for i in range(DEPTH):
        last = i == DEPTH - 1
        j = i // 2
        ng = norm_g[i]
        mod_l = (sc @ ada_w[i] + ada_b[i]).reshape(x.shape[0], N_MOD, 1, D_MODEL).swapaxes(0, 1)
        mod_c = (sc_ctx @ ada_w[i] + ada_b[i]).reshape(N_MOD, 1, 1, D_MODEL)
        h_l = modulate(rmsnorm(x, ng[0]), mod_l[0], mod_l[1])
        h_c = modulate(rmsnorm(ctx, ng[0]), mod_c[0], mod_c[1])
        if i % 2 == 0:
            o_c, o_l = mixer_ab(h_c, h_l, ab_w_in[j], ab_w_out[j], ml_gate_b[j], ml_norm_g[j], ss_conv_w[j],
                                ss_conv_b[j], ss_dt_bias[j], ss_A_log[j], ss_D[j], ss_norm_g[j], not last)
        else:
            o_c, o_l = mixer_rwkv(h_c, h_l, rw_mu[j], rw_wr[j], rw_wk[j], rw_wv[j], rw_wo[j], rw_w0[j], rw_w1[j],
                                  rw_w2[j], rw_a0[j], rw_a1[j], rw_a2[j], rw_g1[j], rw_g2[j], rw_kk[j], rw_ka[j],
                                  rw_rk[j], rw_lnx_g[j], rw_lnx_b[j], not last)
        x = x + mod_l[2] * rmsnorm(o_l, ng[1])
        x = channel_sublayer(x, mod_l, ng, router_w[i], exp_w1[i], exp_w3[i], exp_w2[i])
        if not last:
            ctx = ctx + mod_c[2] * rmsnorm(o_c, ng[1])
            ctx = channel_sublayer(ctx, mod_c, ng, router_w[i], exp_w1[i], exp_w3[i], exp_w2[i])
    return x


_drawn_inputs = setup_inputs


def setup_inputs(seed=0):
    import zlib

    import numpy as np

    out = dict(_drawn_inputs(seed))
    spreads = {}
    factors = {'ml_norm_g': 4.054,
     'rw_w1': 3.939,
     'rw_w2': 4.298,
     'rw_lnx_b': 4.725,
     'rw_a2': 2.872,
     'rw_ka': 3.052,
     'rw_lnx_g': 3.87}
    for name, (base, spread) in spreads.items():
        noise = np.random.default_rng([zlib.crc32(name.encode()), seed]).standard_normal(out[name].shape)
        drawn = base * np.exp(spread * noise) if base else spread * noise
        out[name] = jnp.asarray(drawn.astype(out[name].dtype))
    for name, factor in factors.items():
        out[name] = (out[name] * factor).astype(out[name].dtype)
    return out
```

```python
from contextlib import ExitStack

import concourse.bass as bass
from concourse import mybir

F32 = mybir.dt.float32
U32 = mybir.dt.uint32
ALU = mybir.AluOpType
ACT = mybir.ActivationFunctionType
AX = mybir.AxisListType

P = 128
D = 1024
DC = D // P
SEG = 256
T = 2 * SEG
NT = T // P
NMOD = 6
ADA = NMOD * D
EPS = 1e-6
NEG = -1.0e30

ML_H, ML_DK, ML_DV = 4, 128, 256
SS_H, SS_HD, SS_G, SS_N = 16, 64, 2, 128
SS_HG = SS_H // SS_G
CONV = 1536
CT = CONV // P
GRID = 64
NE, FF, CAP = 16, 1408, 32
FC = FF // P
COL_Q, COL_K, COL_V, COL_O = 0, 512, 1024, 2048
COL_GATE = 3072
COL_Z = COL_GATE + 16
COL_X = COL_Z + 1024
COL_DT = COL_X + CONV

RW_H, RW_N = 16, 64
RW_EPS = 64e-5
LC = 64
NCH = T // LC


class Chain:

    def __init__(self, sem):
        self.sem, self.n, self.base = sem, 0, 0

    def do(self, ins):
        ins.then_inc(self.sem, 1)
        self.n += 1

    def join(self, eng):
        eng.wait_ge(self.sem, self.base + self.n)

    def step(self, eng, ins):
        self.do(ins)
        self.join(eng)

    def enter(self, i, per):
        self.start, self.n0 = (self.base, self.n)
        self.base, self.n = i * per + self.n, 0
        self.per = per

    def leave(self, passes):
        assert self.n == self.per, (self.n, self.per)
        self.base, self.n = 0, self.n0 + passes * self.per


class Env:
    pass


def setup(nc, ctx, a):
    g = Env()
    g.nc, g.a = nc, a
    g.names = 0
    g.rw_steps = 54

    g.passing = []

    def sem(name):
        g.names += 1
        g.passing.append(nc.alloc_semaphore(f"{name}_{g.names}"))
        return g.passing[-1]

    def place(scope, name, shape, dt=F32):
        g.names += 1
        return scope.enter_context(nc.sbuf_tensor(f"{name}_{g.names}", shape, dt))

    g.sem, g.place = sem, place
    g.dve, g.act, g.pool = Chain(sem("vector_done")), Chain(sem("scalar_done")), Chain(sem("gpsimd_done"))
    g.passing = []
    keep = lambda name, shape, dt=F32: ctx.enter_context(nc.sbuf_tensor(name, shape, dt))
    g.ident = keep("ident", [P, P])
    g.ones = keep("ones", [P, P])
    g.upper = keep("upper", [P, P])
    g.lower = keep("lower", [P, P])
    g.cols = keep("cols", [P, 512])
    g.x = keep("x_res", [P, NT, D])
    g.small = keep("small", [P, 64])
    g.ps = [ctx.enter_context(nc.psum_tensor(f"bank{i}", [P, 512], F32)) for i in range(8)]
    dram = lambda name, shape: nc.dram_tensor(name, shape, F32).ap()
    g.modraw = dram("mod_raw", [2, 2, ADA])
    g.modp = dram("mod_rows", [2, 2, ADA])
    return g


COL_MOD = (0, 96)
COL_P2, COL_P3, COL_P4 = 192, 304, 424


def mod_col(layer, stream, k, dc):
    return COL_MOD[layer] + stream * 48 + k * 8 + dc


def stage_constants_and_modulation(g):
    nc, a = g.nc, g.a
    HALF = ADA // 2
    RING = 4
    with ExitStack() as ctx:
        sb = lambda name, shape: g.place(ctx, name, shape)
        slab = sb("ada_slab", [P, RING, HALF])
        crow = sb("c_rows", [16, P])
        ccol = sb("c_cols", [P, 16])
        prow = [sb(f"param_rows{i}", [P, P]) for i in range(3)]
        mrow = sb("mod_evict", [66, 2, 2, 512])
        modr = sb("mod_r", [96, P])
        bias = sb("mod_bias", [96, 2, P])
        gains = sb("mod_gain", [96, 2, P])
        plus = sb("mod_plus", [96, P])
        ones16 = sb("ones16", [16, P])
        s_load, s_slab, s_used, s_mm = g.sem("rows_loaded"), [g.sem(f"slab{i}_loaded") for i in range(RING)], g.sem("slab_used"), g.sem("half_done")
        s_tr, s_trc, s_silu, s_const, s_evict = g.sem("transposed"), g.sem("tr_copied"), g.sem("silu_ready"), g.sem("consts_ready"), g.sem("half_evicted")
        s_raw, s_back, s_fin, s_set, s_rowout = [g.sem("raw_stored_even"), g.sem("raw_stored_odd")], g.sem("raw_back"), g.sem("mod_ready"), g.sem("fills_ready"), g.sem("mod_stored")
        s_one, s_x = g.sem("plus_placed"), g.sem("x_loaded")
        r2, r3, r4 = prow
        with nc.Block() as block:
            @block.sync
            def _(sp):
                sp.dma_start(crow[0:8, :], a["c"].rearrange("b (r p) -> (b r) p", p=P)).then_inc(s_load, 16)
                sp.dma_start(crow[8:16, :], a["c_ctx"].rearrange("(r p) -> r p", p=P)).then_inc(s_load, 16)
                at = 0
                for ap, n in ((a["rw_mu"].rearrange("o k (r p) -> (o k r) p", p=P), 48),
                              (a["rw_w0"].rearrange("o k (r p) -> (o k r) p", p=P), 16),
                              (a["rw_a0"].rearrange("o (r p) -> (o r) p", p=P), 8),
                              (a["rw_kk"].rearrange("o (r p) -> (o r) p", p=P), 8),
                              (a["rw_ka"].rearrange("o (r p) -> (o r) p", p=P), 8),
                              (a["rw_rk"].rearrange("o (r b) n -> (o r) (b n)", b=2), 8),
                              (a["rw_lnx_g"].rearrange("o (r p) -> (o r) p", p=P), 8),
                              (a["rw_lnx_b"].rearrange("o (r p) -> (o r) p", p=P), 8)):
                    sp.dma_start(r2[at:at + n, :], ap).then_inc(s_load, 16)
                    at += n
                sp.dma_start(r3[0:108, :], a["ss_conv_w"].rearrange("o i j (r p) -> (o i j r) p", p=P)).then_inc(s_load, 16)
                sp.dma_start(r3[108:120, :], a["ss_conv_b"].rearrange("o (r p) -> (o r) p", p=P)).then_inc(s_load, 16)
                sp.dma_start(r4[0:8, :], a["ml_norm_g"].rearrange("o (r p) -> (o r) p", p=P)).then_inc(s_load, 16)
                sp.dma_start(r4[8:16, :], a["ss_norm_g"].rearrange("o (r p) -> (o r) p", p=P)).then_inc(s_load, 16)
                sp.dma_start(r4[16:80, :], a["norm_g"].rearrange("l k (r p) -> (l k r) p", p=P)).then_inc(s_load, 16)
                n = 0
                for layer in range(2):
                    for half in range(2):
                        for dc in range(DC):
                            if n >= RING:
                                sp.wait_ge(s_used, n - RING + 1)
                            sp.dma_start(slab[:, n % RING, :],
                                         a["ada_w"][layer, dc * P:(dc + 1) * P, half * HALF:(half + 1) * HALF]
                                         ).then_inc(s_slab[n % RING], 16)
                            n += 1
                sp.dma_start(g.x[:, 0:2, :], a["ctx"].rearrange("b (t p) d -> p (b t) d", p=P)).then_inc(s_x, 16)
                sp.dma_start(g.x[:, 2:4, :], a["x"].rearrange("b (t p) d -> p (b t) d", p=P)).then_inc(s_x, 16)
                sp.wait_ge(s_x, 32)

            @block.gpsimd
            def _(pool):
                for m, v in ((g.ident, 0.0), (g.upper, 1.0), (g.lower, 1.0), (g.ones, 1.0)):
                    g.pool.do(pool.memset(m[:, :], v))
                g.pool.join(pool)
                pool.affine_select(out=g.ident[:, :], in_=g.ident[:, :], compare_op=ALU.not_equal, fill=1.0,
                                   base=0, pattern=[[-1, P]], channel_multiplier=1).then_inc(s_const, 1)
                pool.affine_select(out=g.upper[:, :], in_=g.upper[:, :], compare_op=ALU.is_ge, fill=0.0,
                                   base=0, pattern=[[1, P]], channel_multiplier=-1).then_inc(s_const, 1)
                pool.affine_select(out=g.lower[:, :], in_=g.lower[:, :], compare_op=ALU.is_ge, fill=0.0,
                                   base=0, pattern=[[-1, P]], channel_multiplier=1).then_inc(s_const, 1)

            @block.tensor
            def _(pe):
                pe.wait_ge(s_const, 1)
                pe.wait_ge(s_load, 16 * 15)
                pe.transpose(g.ps[4][:, 0:16], crow[:, :], g.ident[0:16, 0:16]).then_inc(s_tr, 1)
                pe.transpose(g.ps[5][:, 0:112], r2[0:112, :], g.ident[0:112, 0:112]).then_inc(s_tr, 1)
                pe.transpose(g.ps[6][:, 0:120], r3[0:120, :], g.ident[0:120, 0:120]).then_inc(s_tr, 1)
                pe.transpose(g.ps[7][:, 0:80], r4[0:80, :], g.ident[0:80, 0:80]).then_inc(s_tr, 1)
                pe.wait_ge(s_silu, 1)
                n = 0
                for h in range(4):
                    if h >= 2:
                        pe.wait_ge(s_evict, h - 1)
                    for dc in range(DC):
                        pe.wait_ge(s_slab[n % RING], 16 * (n // RING + 1))
                        for s in range(6):
                            j, b = s % 3, s // 3
                            mm = pe.matmul(g.ps[2 * (h % 2) + b][32 * j:32 * j + 2, :], ccol[:, dc::8],
                                           slab[:, n % RING, 512 * s:512 * s + 512],
                                           start=(dc == 0), stop=(dc == DC - 1))
                        mm.then_inc(s_used, 1)
                        n += 1
                for layer in range(2):
                    pe.wait_ge(s_fin, layer + 1)
                    pe.transpose(g.ps[4 + layer][:, 0:96], modr[:, :], g.ident[0:96, 0:96]).then_inc(s_tr, 1)

            @block.vector
            def _(dve):
                g.dve.do(dve.memset(gains[:, :, :], 1.0))
                g.dve.do(dve.memset(plus[:, :], 0.0))
                g.dve.do(dve.memset(ones16[:, :], 1.0))
                g.dve.join(dve)
                dve.sem_inc(s_set, 1) if False else dve.memset(g.small[:, :], 0.0).then_inc(s_set, 1)
                dve.wait_ge(s_tr, 4)
                dve.tensor_copy(g.cols[:, COL_P2:COL_P2 + 112], g.ps[5][:, 0:112]).then_inc(s_trc, 1)
                dve.tensor_copy(g.cols[:, COL_P3:COL_P3 + 120], g.ps[6][:, 0:120]).then_inc(s_trc, 1)
                dve.tensor_copy(g.cols[:, COL_P4:COL_P4 + 80], g.ps[7][:, 0:80]).then_inc(s_trc, 1)
                for h in range(4):
                    dve.wait_ge(s_used, DC * (h + 1))
                    if h >= 2:
                        dve.wait_ge(s_raw[h % 2], 16 * 6)
                    for j in range(3):
                        for b in range(2):
                            cp = dve.tensor_copy(mrow[32 * j:32 * j + 2, h % 2, b, :], g.ps[2 * (h % 2) + b][32 * j:32 * j + 2, :])
                            g.dve.do(cp)
                    g.dve.join(dve)
                    dve.memset(g.small[:, 0:1], 0.0).then_inc(s_evict, 1)
                for layer in range(2):
                    dve.wait_ge(s_back, 16 * (layer + 1))
                    dve.wait_ge(s_one, 16 * 16)
                    if layer:
                        dve.wait_ge(s_tr, 5)
                    g.dve.step(dve, dve.tensor_tensor(modr[:, :], modr[:, :], bias[:, layer, :], ALU.add))
                    g.dve.step(dve, dve.tensor_tensor(modr[:, :], modr[:, :], plus[:, :], ALU.add))
                    dve.tensor_tensor(modr[:, :], modr[:, :], gains[:, layer, :], ALU.mult).then_inc(s_fin, 1)
                    dve.wait_ge(s_tr, 5 + layer)
                    dve.tensor_copy(g.cols[:, COL_MOD[layer]:COL_MOD[layer] + 96], g.ps[4 + layer][:, 0:96]).then_inc(s_trc, 1)

            @block.scalar
            def _(act):
                act.wait_ge(s_tr, 1)
                act.activation(ccol[:, :], g.ps[4][:, 0:16], ACT.Silu).then_inc(s_silu, 1)
                act.wait_ge(s_set, 1)
                for layer in range(2):
                    for st in range(2):
                        act.dma_start(bias[48 * st:48 * st + 48, layer, :],
                                      a["ada_b"][layer].rearrange("(r p) -> r p", p=P)).then_inc(s_one, 16)
                        for k, norm in ((1, 0), (4, 2)):
                            act.dma_start(gains[48 * st + 8 * k:48 * st + 8 * k + 16, layer, :],
                                          a["norm_g"][layer, norm:norm + 2].rearrange("k (r p) -> (k r) p", p=P)).then_inc(s_one, 16)
                for st in range(2):
                    for k in (1, 4):
                        act.dma_start(plus[48 * st + 8 * k:48 * st + 8 * k + 8, :], ones16[0:8, :]).then_inc(s_one, 16)
                for h in range(4):
                    act.wait_ge(s_evict, h + 1)
                    layer, half = h // 2, h % 2
                    for s in range(6):
                        j, b = s % 3, s // 3
                        c0 = half * HALF + 512 * s
                        act.dma_start(g.modraw[layer, :, c0:c0 + 512], mrow[32 * j:32 * j + 2, h % 2, b, :]).then_inc(s_raw[h % 2], 16)
                    if half:
                        act.wait_ge(s_raw[0], 16 * 6 * (layer + 1))
                        act.wait_ge(s_raw[1], 16 * 6 * (layer + 1))
                        if layer:
                            act.wait_ge(s_rowout, 16)
                            act.wait_ge(s_tr, 5)
                        act.dma_start(modr[:, :], g.modraw[layer].rearrange("s (r p) -> (s r) p", p=P)).then_inc(s_back, 16)
                        act.wait_ge(s_fin, layer + 1)
                        act.dma_start(g.modp[layer].rearrange("s (r p) -> (s r) p", p=P), modr[:, :]).then_inc(s_rowout, 16)
                act.wait_ge(s_rowout, 32)


def stage_norm(g, layer, which, t0, ctx, need_xn):
    nc = g.nc
    nt = NT - t0
    with ExitStack() as own:
        sq = g.place(own, "norm_sq", [P, D])
        s_ss, s_root, s_xn, s_tp, s_ev = (g.sem(n) for n in ("squares_summed", "root_ready", "xn_ready", "xn_transposed", "hT_evicted"))
        ssq = g.small[:, 0:4]
        root = g.small[:, 4:8]
        rstd = g.small[:, 8:12]
        with nc.Block() as block:
            @block.scalar
            def _(act):
                for t in range(t0, NT):
                    if t > t0:
                        g.act.join(act)
                    g.act.do(act.activation(sq[:, :], g.x[:, t, :], ACT.Square, accum_out=ssq[:, t:t + 1]))
                g.act.join(act)
                act.activation(root[:, t0:NT], ssq[:, t0:NT], ACT.Sqrt, bias=g.eps[:, 0:1], scale=1.0 / D).then_inc(s_root, 1)
                n = 0
                for dc in range(DC):
                    act.wait_ge(s_tp, dc + 1)
                    for st, lo, hi in ((1, 0, 2 - t0), (0, 2 - t0, nt)):
                        if hi <= 0:
                            continue
                        lo = max(lo, 0)
                        col = mod_col(layer, st, which * 3 + 1, dc)
                        sh = mod_col(layer, st, which * 3, dc)
                        act.activation(g.hT[:, dc, (t0 + lo) * P:(t0 + hi) * P], g.ps[dc % 4][:, lo * P:hi * P],
                                       ACT.Identity, bias=g.cols[:, sh:sh + 1], scale=g.cols[:, col:col + 1]).then_inc(s_ev, 1)

            @block.vector
            def _(dve):
                dve.wait_ge(s_root, 1)
                g.dve.step(dve, dve.reciprocal(rstd[:, t0:NT], root[:, t0:NT]))
                for t in range(t0, NT):
                    dve.tensor_scalar(g.xn[:, t, :], g.x[:, t, :], rstd[:, t:t + 1], None, ALU.mult).then_inc(s_xn, 1)

            @block.tensor
            def _(pe):
                pe.wait_ge(s_xn, nt)
                segs = 2 if t0 == 0 else 1
                for dc in range(DC):
                    if dc >= 4:
                        pe.wait_ge(s_ev, segs * (dc - 3))
                    for t in range(nt):
                        mm = pe.transpose(g.ps[dc % 4][:, t * P:(t + 1) * P], g.xn[:, t0 + t, dc * P:(dc + 1) * P], g.ident[:, :])
                    mm.then_inc(s_tp, 1)


def stage_project(g):
    nc, a = g.nc, g.a
    RING = 2
    w = a["ab_w_in"]
    slabs = [("T", c, dst, t) for c, dst, t in ((COL_Q, g.qT, 0), (COL_K, g.kT, 0), (COL_X, g.xbc, 0), (COL_X + 512, g.xbc, 4), (COL_X + 1024, g.xbc, 8))]
    slabs += [("N", c, dst, t) for c, dst, t in ((COL_V, g.v, 0), (COL_V + 512, g.v, 1), (COL_O, g.o, 0), (COL_O + 512, g.o, 1), (COL_Z, g.z, 0), (COL_Z + 512, g.z, 1))]
    with ExitStack() as ctx:
        sb = lambda name, shape: g.place(ctx, name, shape)
        slab = sb("w_slab", [P, RING, DC, 512])
        wg = sb("w_gate_spread", [P, DC, 100])
        wd = sb("w_dt_spread", [P, DC, 48])
        s_w, s_small, s_spread = [g.sem(f"w_slab{i}") for i in range(RING)], g.sem("w_small"), g.sem("w_spread")
        s_mm, s_ev, s_slabfree, s_conv = g.sem("product_ready"), g.sem("product_out"), g.sem("slab_free"), g.sem("convolved")
        with nc.Block() as block:
            @block.sync
            def _(sp):
                for n, (_, c0, _, _) in enumerate(slabs):
                    if n >= RING:
                        sp.wait_ge(s_slabfree, n - RING + 1)
                    sp.dma_start(slab[:, n % RING, :, :], w[0, :, c0:c0 + 512].rearrange("(c p) n -> p c n", p=P)).then_inc(s_w[n % RING], 16)
                    if n == 1:
                        sp.wait_ge(s_spread, 1)
                        cols = lambda c0, m: w[0, :, c0:c0 + m].rearrange("(c p) n -> p c n", p=P)
                        for d in range(2):
                            for f in range(2):
                                sp.dma_start(wg[:, :, 64 * f + 32 * d:64 * f + 32 * d + 4], cols(COL_GATE + 8 * d + 4 * f, 4)).then_inc(s_small, 16)
                            sp.dma_start(wd[:, :, 32 * d:32 * d + 16], cols(COL_DT + 16 * d, 16)).then_inc(s_small, 16)

            @block.tensor
            def _(pe):
                k = 0
                def bank():
                    if k >= 8:
                        pe.wait_ge(s_ev, k - 7)
                    return g.ps[k % 8]
                for n, (kind, _, _, _) in enumerate(slabs):
                    pe.wait_ge(s_w[n % RING], 16 * (n // RING + 1))
                    for m in range(4):
                        ps = bank()
                        for dc in range(DC):
                            if kind == "T":
                                mm = pe.matmul(ps[:, :], slab[:, n % RING, dc, m * P:(m + 1) * P], g.hT[:, dc, :],
                                               start=(dc == 0), stop=(dc == DC - 1))
                            else:
                                mm = pe.matmul(ps[:, :], g.hT[:, dc, m * P:(m + 1) * P], slab[:, n % RING, dc, :],
                                               start=(dc == 0), stop=(dc == DC - 1))
                        if m == 3:
                            mm.then_inc(s_slabfree, 1)
                            pe.wait_ge(s_slabfree, n + 1)
                            pe.nop().then_inc(s_mm, 1)
                        else:
                            mm.then_inc(s_mm, 1)
                        k += 1
                pe.wait_ge(s_small, 96)
                for wt, m in ((wg, 100), (wd, 48)):
                    ps = bank()
                    for dc in range(DC):
                        mm = pe.matmul(ps[0:m, :], wt[:, dc, :], g.hT[:, dc, :], start=(dc == 0), stop=(dc == DC - 1))
                    mm.then_inc(s_mm, 1)
                    k += 1

            @block.gpsimd
            def _(pool):
                g.pool.do(pool.memset(wg[:, :, :], 0.0))
                g.pool.do(pool.memset(wd[:, :, :], 0.0))
                g.pool.do(pool.memset(g.v[:, :, :, ML_DV:ML_DV + 1], 1.0))
                g.pool.join(pool)
                pool.memset(g.small[:, 3:4], 0.0).then_inc(s_spread, 1)

            def evict(eng, copy, n, k, m):
                kind, _, dst, at = slabs[n]
                if kind == "T":
                    out = dst[:, at + m, :]
                elif dst is g.v:
                    out = dst[:, m, 2 * at:2 * at + 2, 0:ML_DV]
                else:
                    out = dst[:, m, 512 * at:512 * at + 512]
                src = g.ps[k % 8][:, :]
                if dst is g.v:
                    src = src.rearrange("p (h v) -> p h v", h=2)
                return copy(out, src, dst)

            n_t = 4 * sum(kind == "T" for kind, _, _, _ in slabs)

            @block.vector
            def _(dve):
                for k in range(0, n_t, 2):
                    n, m = k // 4, k % 4
                    dve.wait_ge(s_mm, k + 1)
                    if k:
                        dve.wait_ge(s_ev, k)
                    f = lambda o, i, dst: dve.tensor_scalar(o, i, ML_DK ** -0.5 if dst is g.kT else 1.0, None, ALU.mult)
                    evict(dve, f, n, k, m).then_inc(s_ev, 1)
                dve.wait_ge(s_ev, n_t)
                tap = lambda i, j, c: g.cols[:, COL_P3 + (3 * i + j) * CT + c:COL_P3 + (3 * i + j) * CT + c + 1]
                for c in range(CT):
                    g.dve.do(dve.tensor_scalar(g.xc[:, c, :], g.xbc[:, c, :], tap(1, 1, c),
                                               g.cols[:, COL_P3 + 108 + c:COL_P3 + 109 + c], ALU.mult, ALU.add))
                g.dve.join(dve)
                for j in (0, 2):
                    lo, hi = max(0, 1 - j), min(SEG, SEG + 1 - j)
                    for c in range(CT):
                        g.dve.do(dve.scalar_tensor_tensor(g.xc[:, c, lo:hi], g.xbc[:, c, lo + j - 1:hi + j - 1], tap(1, j, c),
                                                          g.xc[:, c, lo:hi], ALU.mult, ALU.add))
                    g.dve.join(dve)
                rows = SEG // GRID
                grid = lambda x, c: x[:, c, SEG:T].rearrange("p (r w) -> p r w", w=GRID)
                for i in range(3):
                    for j in range(3):
                        if (i, j) == (1, 1):
                            continue
                        r0, r1 = max(0, 1 - i), min(rows, rows + 1 - i)
                        lo, hi = max(0, 1 - j), min(GRID, GRID + 1 - j)
                        for c in range(CT):
                            acc = grid(g.xc, c)[:, r0:r1, lo:hi]
                            g.dve.do(dve.scalar_tensor_tensor(acc, grid(g.xbc, c)[:, r0 + i - 1:r1 + i - 1, lo + j - 1:hi + j - 1],
                                                              tap(i, j, c), acc, ALU.mult, ALU.add))
                        g.dve.join(dve)
                dve.memset(g.small[:, 0:1], 0.0).then_inc(s_conv, 1)

            @block.scalar
            def _(act):
                for k in range(4 * len(slabs)):
                    n, m = k // 4, k % 4
                    if k < n_t and k % 2 == 0:
                        continue
                    act.wait_ge(s_mm, k + 1)
                    act.wait_ge(s_ev, k)
                    f = lambda o, i, dst: act.activation(o, i, ACT.Copy, scale=ML_DK ** -0.5 if dst is g.kT else 1.0)
                    evict(act, f, n, k, m).then_inc(s_ev, 1)
                k = 4 * len(slabs)
                act.wait_ge(s_mm, k + 1)
                g.act.do(act.activation(g.ig[:, :], g.ps[k % 8][0:36, :], ACT.Copy))
                g.act.do(act.activation(g.fg[:, :], g.ps[k % 8][64:100, :], ACT.Copy))
                k += 1
                act.wait_ge(s_mm, k + 1)
                act.activation(g.dt[:, :], g.ps[k % 8][0:48, :], ACT.Copy)
                act.wait_ge(s_conv, 1)
                for c in range(CT):
                    act.activation(g.xc[:, c, :], g.xc[:, c, :], ACT.Silu)


def stage_mlstm(g):
    nc, a = g.nc, g.a
    ROW = lambda d, h: 32 * d + h
    FULL = [[[(1, 4)], [(2, 4)], [(3, 4)], []], [[(2, 4)], [(0, 1), (2, 4)], [], [(2, 3)]]]
    SEES = [[[0], [0, 1], [0, 1, 2], [0, 1, 2, 3]], [[0, 1], [1], [0, 1, 2, 3], [0, 1, 3]]]
    with ExitStack() as ctx:
        sb = lambda name, shape: g.place(ctx, name, shape)
        e = sb("ml_weights", [P, 2, NT, T])
        diag = sb("ml_diag", [P, 2, NT, P])
        mneg = sb("ml_mask", [P, 2, P])
        lf, b, gg, negm, enm = (sb(f"ml_{n}", [36, T]) for n in ("lf", "b", "g", "negm", "enm"))
        zero = sb("ml_zero", [36, T])
        gb = sb("ml_gate_bias", [36, 2])
        gcol, ecol = sb("ml_gcol", [P, NT, 36]), sb("ml_ecol", [P, NT, 36])
        den = sb("ml_den", [P, 2, 2])
        ssq = sb("ml_ssq", [P, 3, 16])
        ym = g.mixT[:, 8:16, :].rearrange("p a b -> p (a b)").rearrange("p (t d) -> p t d", t=NT)
        s_bias, s_zero, s_lin, s_ln, s_rows, s_cols, s_colsc = (g.sem(n) for n in ("gate_bias", "bias_zeroed", "forget_linear", "forget_log", "gate_rows", "gate_cols", "gate_cols_copied"))
        s_enm, s_score, s_bc, s_diag, s_exp, s_w, s_num, s_out = (g.sem(n) for n in ("enm", "scores", "m_spread", "diag_ready", "exp_ready", "weights_ready", "num_ready", "num_out"))
        s_sq, s_rt, s_sig, s_y, s_tp, s_ev = (g.sem(n) for n in ("ml_squares", "ml_root", "ml_sigmoid", "ml_y", "ml_transposed", "ml_evicted"))
        with nc.Block() as block:
            @block.sync
            def _(sp):
                sp.wait_ge(s_zero, 1)
                for d in range(2):
                    for f in range(2):
                        sp.dma_start(gb[32 * d:32 * d + 4, f:f + 1], a["ml_gate_b"][0, d, f, :].rearrange("(h o) -> h o", o=1)).then_inc(s_bias, 16)

            @block.vector
            def _(dve):
                g.dve.do(dve.memset(gb[:, :], 0.0))
                g.dve.do(dve.memset(zero[:, :], 0.0))
                g.dve.do(dve.tensor_scalar(mneg[:, 0, :], g.upper[:, :], 1.0, -NEG, ALU.subtract, ALU.mult))
                g.dve.do(dve.tensor_scalar(mneg[:, 1, :], g.lower[:, :], 1.0, -NEG, ALU.subtract, ALU.mult))
                g.dve.join(dve)
                dve.memset(g.small[:, 0:1], 0.0).then_inc(s_zero, 1)
                dve.wait_ge(s_bias, 64)
                g.dve.do(dve.tensor_scalar(g.ig[:, :], g.ig[:, :], gb[:, 0:1], None, ALU.add))
                g.dve.step(dve, dve.tensor_scalar(g.fg[:, :], g.fg[:, :], gb[:, 1:2], None, ALU.add))
                dve.tensor_scalar(lf[:, :], g.fg[:, :], 0.0, None, ALU.min).then_inc(s_lin, 1)
                dve.wait_ge(s_ln, 1)
                g.dve.step(dve, dve.tensor_tensor(lf[:, :], lf[:, :], enm[:, :], ALU.subtract))
                f, r = slice(0, 4), slice(32, 36)

                def scan(out, src, op):
                    other = (lambda x: x) if op == ALU.max else (lambda x: zero[:, :])
                    g.dve.do(dve.tensor_tensor_scan(out[f, :], src[f, :], src[f, :] if op == ALU.max else zero[f, :], 0.0, op, op))
                    back = lambda x, lo, hi: x[r, lo:hi][:, ::-1]
                    for lo, hi in ((0, SEG), (SEG, T)):
                        g.dve.step(dve, dve.tensor_tensor_scan(back(out, lo, hi), back(src, lo, hi), back(src if op == ALU.max else zero, lo, hi),
                                                               out[r, 0:1] if lo else 0.0, op, op))
                g.dve.do(dve.memset(b[:, :], 0.0))
                g.dve.do(dve.memset(negm[:, :], 0.0))
                g.dve.join(dve)
                scan(b, lf, ALU.add)
                g.dve.step(dve, dve.tensor_tensor(gg[:, :], g.ig[:, :], b[:, :], ALU.subtract))
                scan(negm, gg, ALU.max)
                g.dve.step(dve, dve.tensor_tensor(enm[:, :], b[:, :], negm[:, :], ALU.add))
                dve.tensor_scalar(negm[:, :], negm[:, :], -1.0, None, ALU.mult).then_inc(s_rows, 1)
                dve.wait_ge(s_cols, 4)
                dve.tensor_copy(gcol[:, :, :], g.ps[6][:, 0:144].rearrange("p (t r) -> p t r", t=NT)).then_inc(s_colsc, 1)
                dve.wait_ge(s_cols, 8)
                dve.tensor_copy(ecol[:, :, :], g.ps[7][:, 0:144].rearrange("p (t r) -> p t r", t=NT)).then_inc(s_colsc, 1)
                dve.wait_ge(s_colsc, 2)

                def diagonal(u):
                    h, d = u // 2, u % 2
                    dve.wait_ge(s_bc, u + 1)
                    if u >= 2:
                        dve.wait_ge(s_exp, u - 1)
                    for st in range(NT):
                        ins = dve.scalar_tensor_tensor(diag[:, d, st, :], g.ps[4 + d][:, st * P:(st + 1) * P],
                                                       gcol[:, st, ROW(d, h):ROW(d, h) + 1], mneg[:, d, :], ALU.add, ALU.add)
                    ins.then_inc(s_diag, 1)

                def weigh(u):
                    h, d = u // 2, u % 2
                    dve.wait_ge(s_exp, u + 1)
                    dve.wait_ge(s_score, h + 1)
                    for st in range(NT):
                        for lo, hi in [(st, st + 1)] + FULL[d][st]:
                            w = e[:, d, st, lo * P:hi * P]
                            ins = dve.tensor_tensor(w, g.ps[st][:, lo * P:hi * P], w, ALU.mult)
                            g.dve.do(ins)
                    g.dve.join(dve)
                    dve.memset(den[:, 0, 1:2], 0.0).then_inc(s_w, 1)

                def finish(u):
                    h, d = u // 2, u % 2
                    for jt in range(NT):
                        ps = g.ps[6 + jt % 2]
                        dve.wait_ge(s_num, NT * u + jt + 1)
                        c = ROW(d, h)
                        g.dve.step(dve, dve.tensor_scalar(den[:, 0, 0:1], ps[:, ML_DV:ML_DV + 1], ecol[:, jt, c:c + 1], None, ALU.max))
                        g.dve.step(dve, dve.scalar_tensor_tensor(den[:, 1, 0:1], ps[:, ML_DV:ML_DV + 1], -1.0, den[:, 0, 0:1], ALU.mult, ALU.max))
                        g.dve.step(dve, dve.reciprocal(den[:, 1, 1:2], den[:, 1, 0:1]))
                        y = ym[:, jt, h * ML_DV:(h + 1) * ML_DV]
                        if d == 0:
                            dve.tensor_scalar(y, ps[:, 0:ML_DV], den[:, 1, 1:2], None, ALU.mult).then_inc(s_out, 1)
                        else:
                            dve.scalar_tensor_tensor(y, ps[:, 0:ML_DV], den[:, 1, 1:2], y, ALU.mult, ALU.add).then_inc(s_out, 1)
                    dve.wait_ge(s_out, NT * (u + 1))

                diagonal(0)
                for u in range(2 * ML_H):
                    if u:
                        finish(u - 1)
                    if u + 1 < 2 * ML_H:
                        diagonal(u + 1)
                    weigh(u)
                finish(2 * ML_H - 1)
                dve.wait_ge(s_rt, 1)
                g.dve.step(dve, dve.reciprocal(ssq[:, 2, :], ssq[:, 1, :]))
                dve.wait_ge(s_sig, 1)
                for t in range(NT):
                    for h in range(ML_H):
                        y = ym[:, t, h * ML_DV:(h + 1) * ML_DV]
                        dve.scalar_tensor_tensor(y, y, ssq[:, 2, 4 * t + h:4 * t + h + 1], g.o[:, t, h * ML_DV:(h + 1) * ML_DV],
                                                 ALU.mult, ALU.mult).then_inc(s_y, 1)

            @block.scalar
            def _(act):
                act.wait_ge(s_lin, 1)
                g.act.step(act, act.activation(enm[:, :], g.fg[:, :], ACT.Abs))
                g.act.step(act, act.activation(enm[:, :], enm[:, :], ACT.Exp, scale=-1.0))
                act.activation(enm[:, :], enm[:, :], ACT.Ln, bias=1.0).then_inc(s_ln, 1)
                act.wait_ge(s_rows, 1)
                act.activation(enm[:, :], enm[:, :], ACT.Exp, scale=-1.0).then_inc(s_enm, 1)
                act.wait_ge(s_colsc, 2)
                for u in range(2 * ML_H):
                    h, d = u // 2, u % 2
                    act.wait_ge(s_diag, u + 1)
                    if u >= 2:
                        act.wait_ge(s_num, NT * (u - 1))
                    for st in range(NT):
                        g.act.do(act.activation(e[:, d, st, st * P:(st + 1) * P], diag[:, d, st, :], ACT.Exp))
                        for lo, hi in FULL[d][st]:
                            g.act.do(act.activation(e[:, d, st, lo * P:hi * P], g.ps[4 + d][:, lo * P:hi * P], ACT.Exp,
                                                    bias=gcol[:, st, ROW(d, h):ROW(d, h) + 1]))
                    g.act.join(act)
                    act.activation(g.small[:, 1:2], g.small[:, 2:3], ACT.Copy).then_inc(s_exp, 1)
                act.wait_ge(s_out, NT * 2 * ML_H)
                act.wait_ge(s_w, 2 * ML_H)
                for t in range(NT):
                    for h in range(ML_H):
                        g.act.do(act.activation(e[:, h % 2, t, 0:ML_DV], ym[:, t, h * ML_DV:(h + 1) * ML_DV], ACT.Square,
                                                accum_out=ssq[:, 0, 4 * t + h:4 * t + h + 1]))
                        if h % 2:
                            g.act.join(act)
                act.activation(ssq[:, 1, :], ssq[:, 0, :], ACT.Sqrt, bias=g.eps[:, 0:1], scale=1.0 / ML_DV).then_inc(s_rt, 1)
                act.activation(g.o[:, :, :], g.o[:, :, :], ACT.Sigmoid).then_inc(s_sig, 1)
                for c in range(DC):
                    act.wait_ge(s_tp, c + 1)
                    act.activation(g.mixT[:, c, :], g.ps[c % 4][:, :], ACT.Copy, scale=g.cols[:, COL_P4 + c:COL_P4 + c + 1]).then_inc(s_ev, 1)

            @block.tensor
            def _(pe):
                pe.wait_ge(s_rows, 1)
                for t in range(NT):
                    pe.transpose(g.ps[6][:, 36 * t:36 * t + 36], gg[:, t * P:(t + 1) * P], g.ident[0:36, 0:36]).then_inc(s_cols, 1)
                pe.wait_ge(s_enm, 1)
                for t in range(NT):
                    pe.transpose(g.ps[7][:, 36 * t:36 * t + 36], enm[:, t * P:(t + 1) * P], g.ident[0:36, 0:36]).then_inc(s_cols, 1)
                pe.wait_ge(s_colsc, 2)

                def spread(u):
                    h, d = u // 2, u % 2
                    if u >= 2:
                        pe.wait_ge(s_exp, u - 1)
                    r = ROW(d, h)
                    pe.matmul(g.ps[4 + d][:, :], g.ident[0:36, r:r + 1].broadcast_to([36, P]), negm[:, :], start=True, stop=True).then_inc(s_bc, 1)

                def scores(h):
                    if h:
                        pe.wait_ge(s_w, 2 * h)
                    for st in range(NT):
                        lo = 0 if st < 2 else SEG
                        mm = pe.matmul(g.ps[st][:, lo:T], g.kT[:, h, st * P:(st + 1) * P], g.qT[:, h, lo:T], start=True, stop=True)
                    mm.then_inc(s_score, 1)

                def numerators(u):
                    h, d = u // 2, u % 2
                    pe.wait_ge(s_w, u + 1)
                    for jt in range(NT):
                        n = NT * u + jt
                        if n >= 2:
                            pe.wait_ge(s_out, n - 1)
                        for st in SEES[d][jt]:
                            mm = pe.matmul(g.ps[6 + jt % 2][:, 0:ML_DV + 1], e[:, d, st, jt * P:(jt + 1) * P], g.v[:, st, h, :],
                                           start=(st == SEES[d][jt][0]), stop=(st == SEES[d][jt][-1]))
                        mm.then_inc(s_num, 1)

                spread(0)
                scores(0)
                for u in range(2 * ML_H):
                    if u + 1 < 2 * ML_H:
                        spread(u + 1)
                    if u % 2 == 1 and u + 1 < 2 * ML_H:
                        scores((u + 1) // 2)
                    numerators(u)
                for c in range(DC):
                    pe.wait_ge(s_y, NT * ML_H)
                    if c >= 4:
                        pe.wait_ge(s_ev, c - 3)
                    for t in range(NT):
                        mm = pe.transpose(g.ps[c % 4][:, t * P:(t + 1) * P], ym[:, t, c * P:(c + 1) * P], g.ident[:, :])
                    mm.then_inc(s_tp, 1)


def stage_ssd(g):
    nc, a = g.nc, g.a
    HW = SS_HG * SS_HD
    ROW = lambda d, h: 32 * d + h
    ORDER = ((0, 1, 2, 3), (1, 0, 3, 2))
    UNITS = [(d, h) for d in range(2) for h in range(SS_H)]
    with ExitStack() as ctx:
        sb = lambda name, shape: g.place(ctx, name, shape)
        xs = sb("ss_x", [P, NT, D])
        xd = sb("ss_xdt", [P, 2, NT, D])
        ys = sb("ss_y", [P, NT, D])
        bt = sb("ss_b", [P, NT, SS_G * SS_N])
        gm = sb("ss_gmask", [P, 2, SS_G, NT, P])
        e = sb("ss_exp", [P, 2, NT, P])
        w = sb("ss_w", [P, 2, NT, P])
        ac, wend, one, res = (sb(f"ss_{n}", [48, T]) for n in ("acum", "wend", "t1", "t2"))
        accol, dtcol, wcol, einc, eae = (sb(f"ss_{n}", [P, NT, 48]) for n in ("accol", "dtcol", "wcol", "einc", "eae"))
        aer = sb("ss_aend", [48, NT])
        bd = sb("ss_aend_diag", [48, NT, 48])
        par = sb("ss_par", [48, 4])
        dsk = sb("ss_dskip", [P, SS_H])
        hst = sb("ss_state", [P, SS_G, HW])
        tmp = sb("ss_tmp", [P, HW])
        ssq = sb("ss_ssq", [P, 3, 8])
        (s_par, s_z, s_abs, s_u, s_ln, s_wend, s_rows, s_col, s_colc, s_einc, s_ae) = (g.sem("ss_" + n) for n in (
            "params", "zeroed", "abs", "one_plus", "log", "wexp", "rows", "cols", "cols_out", "exps", "aend_spread"))
        (s_tp, s_tpv, s_tpa, s_g, s_gm, s_xd, s_yd, s_bc, s_df, s_ex, s_w, s_in, s_out) = (g.sem("ss_" + n) for n in (
            "x_transposed", "x_out_v", "x_out_a", "g_ready", "g_masked", "xdt", "y_init", "acum_spread", "diff", "exp", "weights", "intra", "intra_out"))
        (s_xp, s_loc, s_int, s_h, s_ya, s_silu, s_u2, s_sq, s_n, s_t2, s_e2) = (g.sem("ss_" + n) for n in (
            "xp", "local_state", "inter", "state", "inter_added", "silu", "gated", "squares", "normed", "y_transposed", "y_evicted"))
        with nc.Block() as block:
            @block.sync
            def _(sp):
                sp.wait_ge(s_z, 1)
                for d in range(2):
                    for k, n in enumerate(("ss_dt_bias", "ss_A_log")):
                        sp.dma_start(par[32 * d:32 * d + 16, k:k + 1], a[n][0, d, :].rearrange("(h o) -> h o", o=1)).then_inc(s_par, 16)
                sp.dma_start(dsk[:, :], a["ss_D"].broadcast_to([P, SS_H])).then_inc(s_par, 16)

            @block.vector
            def _(dve):
                dv = g.dve
                dv.do(dve.memset(par[:, :], 0.0))
                dv.do(dve.memset(ac[:, :], 0.0))
                dv.do(dve.memset(aer[:, :], 0.0))
                dv.join(dve)
                dve.memset(g.small[:, 0:1], 0.0).then_inc(s_z, 1)
                dve.wait_ge(s_par, 80)
                dve.tensor_scalar(g.dt[:, :], g.dt[:, :], par[:, 0:1], None, ALU.add).then_inc(s_abs, 1)
                dve.wait_ge(s_u, 1)
                dv.step(dve, dve.tensor_scalar(res[:, :], one[:, :], 1.0, None, ALU.add))
                dve.tensor_scalar(wend[:, :], res[:, :], 1.0, None, ALU.subtract).then_inc(s_u, 1)
                dve.wait_ge(s_u, 2)
                dve.wait_ge(s_ln, 1)
                dv.step(dve, dve.tensor_tensor(res[:, :], res[:, :], one[:, :], ALU.mult))
                dv.step(dve, dve.scalar_tensor_tensor(one[:, :], wend[:, :], 0.0, one[:, :], ALU.is_equal, ALU.mult))
                dv.step(dve, dve.tensor_scalar(wend[:, :], wend[:, :], 1.0e-30, None, ALU.max))
                dv.step(dve, dve.reciprocal(wend[:, :], wend[:, :]))
                dv.step(dve, dve.tensor_tensor(res[:, :], res[:, :], wend[:, :], ALU.mult))
                dv.step(dve, dve.tensor_tensor(res[:, :], res[:, :], one[:, :], ALU.add))
                dv.step(dve, dve.scalar_tensor_tensor(g.dt[:, :], g.dt[:, :], 0.0, res[:, :], ALU.max, ALU.add))
                dv.step(dve, dve.tensor_scalar(res[:, :], g.dt[:, :], par[:, 2:3], -1.0, ALU.mult, ALU.mult))
                dv.step(dve, dve.memset(one[:, :], 1.0))
                dv.do(dve.memset(one[0:16, 0::P], 0.0))
                dv.do(dve.memset(one[32:48, P - 1::P], 0.0))
                dv.join(dve)
                dv.do(dve.tensor_tensor_scan(ac[0:16, :], one[0:16, :], res[0:16, :], 0.0, ALU.mult, ALU.add))
                dv.do(dve.tensor_tensor_scan(ac[32:48, ::-1], one[32:48, ::-1], res[32:48, ::-1], 0.0, ALU.mult, ALU.add))
                dv.join(dve)
                dv.do(dve.tensor_copy(aer[0:16, :], ac[0:16, P - 1::P]))
                dv.do(dve.tensor_copy(aer[32:48, :], ac[32:48, 0::P]))
                dv.join(dve)
                for c in range(NT):
                    dv.do(dve.tensor_scalar(wend[:, c * P:(c + 1) * P], ac[:, c * P:(c + 1) * P], aer[:, c:c + 1], None, ALU.subtract))
                dv.join(dve)
                dve.tensor_tensor(bd[:, :, :], g.ident[0:48, 0:48].rearrange("p (o r) -> p o r", o=1).broadcast_to([48, NT, 48]),
                                  aer[:, :].rearrange("p (c o) -> p c o", o=1).broadcast_to([48, NT, 48]), ALU.mult).then_inc(s_rows, 1)
                for gr in range(SS_G):
                    dve.wait_ge(s_g, gr + 1)
                    for d, m in enumerate((g.upper, g.lower)):
                        dve.tensor_tensor(gm[:, d, gr, :, :], g.ps[gr][:, :].rearrange("p (c j) -> p c j", c=NT),
                                          m[:, :].rearrange("p (o j) -> p o j", o=1).broadcast_to([P, NT, P]), ALU.mult).then_inc(s_gm, 1)
                for k in range(0, 10, 2):
                    dve.wait_ge(s_tp, k + 1)
                    out = xs[:, k // 2, 0:512] if k < 8 else bt[:, 0:2, :]
                    dve.tensor_copy(out, g.ps[2 + k % 2][:, :] if k < 8 else g.ps[2][:, :].rearrange("p (c n) -> p c n", c=2)).then_inc(s_tpv, 1)
                for k, (dst, bank) in enumerate(((accol, 5), (dtcol, 6), (wcol, 7))):
                    dve.wait_ge(s_col, k + 1)
                    dve.tensor_copy(dst[:, :, :], g.ps[bank][:, 0:192].rearrange("p (c r) -> p c r", c=NT)).then_inc(s_colc, 1)
                dve.wait_ge(s_colc, 3)
                dve.wait_ge(s_tpv, 5)
                dve.wait_ge(s_tpa, 5)
                for t in range(NT):
                    dve.tensor_tensor(ys[:, t, :].rearrange("p (h k) -> p h k", h=SS_H), xs[:, t, :].rearrange("p (h k) -> p h k", h=SS_H),
                                      dsk[:, :].rearrange("p (h o) -> p h o", o=1).broadcast_to([P, SS_H, SS_HD]), ALU.mult).then_inc(s_yd, 1)
                dve.wait_ge(s_yd, NT)

                def difference(u):
                    d, h = UNITS[u]
                    dve.wait_ge(s_bc, u + 1)
                    if u >= 2:
                        dve.wait_ge(s_w, u - 1)
                    for c in range(NT):
                        ins = dve.tensor_scalar(e[:, u % 2, c, :], g.ps[u % 2][:, c * P:(c + 1) * P],
                                                accol[:, c, ROW(d, h):ROW(d, h) + 1], 0.0, ALU.subtract, ALU.min)
                    ins.then_inc(s_df, 1)

                def add_intra(u):
                    d, h = UNITS[u]
                    dve.wait_ge(s_in, u + 1)
                    if u >= SS_H:
                        dve.wait_ge(s_out, u - SS_H + 1)
                    y = ys[:, :, h * SS_HD:(h + 1) * SS_HD]
                    dve.tensor_tensor(y, g.ps[2 + u % 2][:, 0:NT * SS_HD].rearrange("p (c k) -> p c k", c=NT), y, ALU.add).then_inc(s_out, 1)

                for u in range(len(UNITS)):
                    difference(u)
                    if u:
                        add_intra(u - 1)
                add_intra(len(UNITS) - 1)
                dve.wait_ge(s_out, len(UNITS))
                heads = lambda x: x.rearrange("p (h k) -> p h k", h=SS_HG)
                spread = lambda x, c, d, gr: x[:, c, ROW(d, SS_HG * gr):ROW(d, SS_HG * gr) + SS_HG].rearrange("p (h o) -> p h o", o=1).broadcast_to([P, SS_HG, SS_HD])
                for d in range(2):
                    for k, c in enumerate(ORDER[d]):
                        n = 4 * d + k
                        if k < 3:
                            dve.wait_ge(s_loc, 3 * d + k + 1)
                            if k:
                                dve.wait_ge(s_int, 3 * d + k)
                                for gr in range(SS_G):
                                    dv.do(dve.tensor_tensor(heads(hst[:, gr, :]), heads(hst[:, gr, :]), spread(eae, c, d, gr), ALU.mult))
                                dv.join(dve)
                                for gr in range(SS_G):
                                    dv.do(dve.tensor_tensor(hst[:, gr, :], hst[:, gr, :], g.ps[4 + gr][:, :], ALU.add))
                            else:
                                if d:
                                    dve.wait_ge(s_int, 3)
                                for gr in range(SS_G):
                                    dv.do(dve.tensor_copy(hst[:, gr, :], g.ps[4 + gr][:, :]))
                            dv.join(dve)
                            dve.memset(g.small[:, 0:1], 0.0).then_inc(s_h, 1)
                        if k:
                            dve.wait_ge(s_int, 3 * d + k)
                            for gr in range(SS_G):
                                dv.step(dve, dve.tensor_tensor(heads(tmp[:, :]), heads(g.ps[6 + gr][:, :]), spread(einc, c, d, gr), ALU.mult))
                                y = ys[:, c, gr * HW:(gr + 1) * HW]
                                dv.step(dve, dve.tensor_tensor(y, tmp[:, :], y, ALU.add))
                            dve.memset(g.small[:, 0:1], 0.0).then_inc(s_ya, 1)
                dve.wait_ge(s_silu, 1)
                for t in range(NT):
                    dve.tensor_tensor(ys[:, t, :], ys[:, t, :], g.z[:, t, :], ALU.mult).then_inc(s_u2, 1)
                dve.wait_ge(s_sq, 1)
                dv.step(dve, dve.reciprocal(ssq[:, 2, :], ssq[:, 1, :]))
                for t in range(NT):
                    for gr in range(SS_G):
                        y = ys[:, t, gr * HW:(gr + 1) * HW]
                        dve.tensor_scalar(y, y, ssq[:, 2, 2 * t + gr:2 * t + gr + 1], None, ALU.mult).then_inc(s_n, 1)

            @block.scalar
            def _(act):
                ac_ = g.act
                act.wait_ge(s_abs, 1)
                ac_.step(act, act.activation(one[:, :], g.dt[:, :], ACT.Abs))
                act.activation(one[:, :], one[:, :], ACT.Exp, scale=-1.0).then_inc(s_u, 1)
                ac_.step(act, act.activation(par[:, 2:3], par[:, 1:2], ACT.Exp))
                act.wait_ge(s_u, 2)
                act.activation(res[:, :], res[:, :], ACT.Ln).then_inc(s_ln, 1)
                for k in range(1, 10, 2):
                    act.wait_ge(s_tp, k + 1)
                    out = xs[:, k // 2, 512:1024] if k < 8 else bt[:, 2:4, :]
                    act.activation(out, g.ps[3][:, :] if k < 8 else g.ps[3][:, :].rearrange("p (c n) -> p c n", c=2), ACT.Copy).then_inc(s_tpa, 1)
                act.wait_ge(s_rows, 1)
                act.activation(wend[:, :], wend[:, :], ACT.Exp, scale=-1.0).then_inc(s_wend, 1)
                act.wait_ge(s_colc, 1)
                act.activation(einc[:, :, :], accol[:, :, :], ACT.Exp).then_inc(s_einc, 1)
                act.wait_ge(s_ae, 1)
                act.activation(eae[:, :, :], g.ps[4][:, 0:192].rearrange("p (c r) -> p c r", c=NT), ACT.Exp).then_inc(s_einc, 1)
                for u in range(len(UNITS)):
                    act.wait_ge(s_df, u + 1)
                    act.activation(e[:, u % 2, :, :], e[:, u % 2, :, :], ACT.Exp).then_inc(s_ex, 1)
                act.activation(g.z[:, :, :], g.z[:, :, :], ACT.Silu).then_inc(s_silu, 1)
                act.wait_ge(s_in, len(UNITS))
                for t in range(NT):
                    act.wait_ge(s_u2, t + 1)
                    for gr in range(SS_G):
                        if t or gr:
                            ac_.join(act)
                        ac_.do(act.activation(e[:, 0, :, :].rearrange("p c j -> p (c j)"), ys[:, t, gr * HW:(gr + 1) * HW], ACT.Square,
                                              accum_out=ssq[:, 0, 2 * t + gr:2 * t + gr + 1]))
                ac_.join(act)
                act.activation(ssq[:, 1, :], ssq[:, 0, :], ACT.Sqrt, bias=g.eps[:, 0:1], scale=1.0 / HW).then_inc(s_sq, 1)
                for c in range(DC):
                    act.wait_ge(s_t2, c + 1)
                    act.activation(g.mixT[:, 8 + c, :], g.ps[c % 4][:, :], ACT.Copy, scale=g.cols[:, COL_P4 + 8 + c:COL_P4 + 9 + c]).then_inc(s_e2, 1)

            @block.gpsimd
            def _(pool):
                hd = lambda x: x.rearrange("p (h k) -> p h k", h=SS_H)
                sp_ = lambda x, c, d: x[:, c, 32 * d:32 * d + SS_H].rearrange("p (h o) -> p h o", o=1).broadcast_to([P, SS_H, SS_HD])
                pool.wait_ge(s_colc, 3)
                pool.wait_ge(s_tpv, 5)
                pool.wait_ge(s_tpa, 5)
                for d in range(2):
                    for t in range(NT):
                        pool.tensor_tensor(hd(xd[:, d, t, :]), hd(xs[:, t, :]), sp_(dtcol, t, d), ALU.mult).then_inc(s_xd, 1)
                pool.wait_ge(s_gm, 4)
                for u, (d, h) in enumerate(UNITS):
                    pool.wait_ge(s_ex, u + 1)
                    if u >= 2:
                        pool.wait_ge(s_in, u - 1)
                    pool.tensor_tensor(w[:, u % 2, :, :], e[:, u % 2, :, :], gm[:, d, h // SS_HG, :, :], ALU.mult).then_inc(s_w, 1)
                    if u < 8 and u % 2:
                        if u == 1:
                            pool.wait_ge(s_yd, NT)
                            pool.wait_ge(s_xd, 2 * NT)
                        t = u // 2
                        pool.tensor_tensor(hd(xs[:, t, :]), hd(xd[:, 0, t, :]), sp_(wcol, t, 0), ALU.mult).then_inc(s_xp, 1)
                pool.wait_ge(s_loc, 3)
                pool.wait_ge(s_xp, NT)
                for t in range(NT):
                    pool.tensor_tensor(hd(xs[:, t, :]), hd(xd[:, 1, t, :]), sp_(wcol, t, 1), ALU.mult).then_inc(s_xp, 1)

            @block.tensor
            def _(pe):
                for gr in range(SS_G):
                    for c in range(NT):
                        mm = pe.matmul(g.ps[gr][:, c * P:(c + 1) * P], g.xc[:, 8 + gr, c * P:(c + 1) * P], g.xc[:, 10 + gr, c * P:(c + 1) * P], start=True, stop=True)
                    mm.then_inc(s_g, 1)
                for k in range(10):
                    if k >= 2:
                        pe.wait_ge(s_tpa if k % 2 else s_tpv, k // 2)
                    for i in range(4):
                        if k < 8:
                            src = g.xc[:, 4 * (k % 2) + i, (k // 2) * P:(k // 2 + 1) * P]
                        else:
                            c = 2 * (k - 8) + i // 2
                            src = g.xc[:, 8 + i % 2, c * P:(c + 1) * P]
                        mm = pe.transpose(g.ps[2 + k % 2][:, i * P:(i + 1) * P], src, g.ident[:, :])
                    mm.then_inc(s_tp, 1)
                pe.wait_ge(s_rows, 1)
                cols = lambda bank, src: [pe.transpose(g.ps[bank][:, 48 * c:48 * c + 48], src[:, c * P:(c + 1) * P], g.ident[0:48, 0:48]) for c in range(NT)][-1]
                cols(5, ac).then_inc(s_col, 1)
                cols(6, g.dt).then_inc(s_col, 1)
                pe.matmul(g.ps[4][:, 0:192], g.ones[0:48, :], bd[:, :, :].rearrange("p c r -> p (c r)"), start=True, stop=True).then_inc(s_ae, 1)
                pe.wait_ge(s_wend, 1)
                cols(7, wend).then_inc(s_col, 1)

                def spread(u):
                    d, h = UNITS[u]
                    if u < 2:
                        pe.wait_ge(s_gm, 4)
                    else:
                        pe.wait_ge(s_df, u - 1)
                    r = ROW(d, h)
                    pe.matmul(g.ps[u % 2][:, :], g.ident[0:48, r:r + 1].broadcast_to([48, P]), ac[:, :], start=True, stop=True).then_inc(s_bc, 1)

                pe.wait_ge(s_tpv, 5)
                pe.wait_ge(s_tpa, 5)
                spread(0)
                for u, (d, h) in enumerate(UNITS):
                    if u + 1 < len(UNITS):
                        spread(u + 1)
                    pe.wait_ge(s_w, u + 1)
                    pe.wait_ge(s_xd, NT * (d + 1)) if h == 0 else None
                    if u >= 2:
                        pe.wait_ge(s_out, u - 1)
                    for c in range(NT):
                        mm = pe.matmul(g.ps[2 + u % 2][:, c * SS_HD:(c + 1) * SS_HD], w[:, u % 2, c, :], xd[:, d, c, h * SS_HD:(h + 1) * SS_HD], start=True, stop=True)
                    mm.then_inc(s_in, 1)
                pe.wait_ge(s_einc, 2)
                for d in range(2):
                    pe.wait_ge(s_xp, NT * (d + 1))
                    for k, c in enumerate(ORDER[d]):
                        if k:
                            pe.wait_ge(s_h, 3 * d + k)
                            if 3 * d + k >= 2:
                                pe.wait_ge(s_ya, 3 * d + k - 1)
                            for gr in range(SS_G):
                                mm = pe.matmul(g.ps[6 + gr][:, :], g.xc[:, 10 + gr, c * P:(c + 1) * P], hst[:, gr, :], start=True, stop=True)
                            mm.then_inc(s_int, 1)
                        if k < 3:
                            if 3 * d + k:
                                pe.wait_ge(s_h, 3 * d + k)
                            for gr in range(SS_G):
                                mm = pe.matmul(g.ps[4 + gr][:, :], bt[:, c, gr * SS_N:(gr + 1) * SS_N], xs[:, c, gr * HW:(gr + 1) * HW], start=True, stop=True)
                            mm.then_inc(s_loc, 1)
                pe.wait_ge(s_n, 8)
                for c in range(DC):
                    if c >= 4:
                        pe.wait_ge(s_e2, c - 3)
                    for t in range(NT):
                        mm = pe.transpose(g.ps[c % 4][:, t * P:(t + 1) * P], ys[:, t, c * P:(c + 1) * P], g.ident[:, :])
                    mm.then_inc(s_t2, 1)


class Tail:

    def __init__(self, g, ctx, layer, which, t0):
        self.g, self.layer, self.which, self.t0 = g, layer, which, t0
        sb = lambda name, shape: g.place(ctx, name, shape)
        self.gain = sb("tail_gain", [P, 2, D])
        self.tmp = sb("tail_tmp", [P, 2, 512])
        self.ssq = sb("tail_ssq", [P, 4, 8])
        (self.s_gain, self.s_ready, self.s_sq, self.s_sum, self.s_root, self.s_tmp, self.s_add) = (g.sem("tail_" + n) for n in (
            "gain_loaded", "product_ready", "squared", "summed", "root", "scaled", "added"))

    def load(self, eng):
        for st in range(2):
            if st == 1 and self.t0:
                continue
            eng.dma_start(self.gain[:, st, :], self.g.modp[self.layer, st:st + 1, self.which * D:(self.which + 1) * D].broadcast_to([P, D])).then_inc(self.s_gain, 16)

    def scalar(self, act):
        g, t0 = self.g, self.t0
        for t in range(t0, NT):
            act.wait_ge(self.s_ready, t - t0 + 1)
            for h in range(2):
                if t > t0 or h:
                    g.act.join(act)
                g.act.do(act.activation(self.tmp[:, 0, :], g.ps[2 * (t - t0) + h][:, :], ACT.Square, accum_out=self.ssq[:, 0, 2 * t + h:2 * t + h + 1]))
        g.act.join(act)
        act.activation(self.ssq[:, 1, 0:1], self.ssq[:, 0, 2 * t0:2 * t0 + 1], ACT.Copy).then_inc(self.s_sq, 1)
        act.wait_ge(self.s_sum, 1)
        act.activation(self.ssq[:, 2, t0:NT], self.ssq[:, 1, t0:NT], ACT.Sqrt, bias=g.eps[:, 0:1], scale=1.0 / D).then_inc(self.s_root, 1)

    def vector(self, dve):
        g, t0 = self.g, self.t0
        dve.wait_ge(self.s_sq, 1)
        halves = self.ssq[:, 0, :].rearrange("p (t h) -> p t h", h=2)
        dve.tensor_tensor(self.ssq[:, 1, t0:NT], halves[:, t0:NT, 0], halves[:, t0:NT, 1], ALU.add).then_inc(self.s_sum, 1)
        dve.wait_ge(self.s_root, 1)
        g.dve.step(dve, dve.reciprocal(self.ssq[:, 3, t0:NT], self.ssq[:, 2, t0:NT]))
        dve.wait_ge(self.s_gain, 16 * (1 if t0 else 2))
        n = 0
        for t in range(t0, NT):
            for h in range(2):
                if n >= 2:
                    dve.wait_ge(self.s_add, n - 1)
                dve.scalar_tensor_tensor(self.tmp[:, n % 2, :], g.ps[2 * (t - t0) + h][:, :], self.ssq[:, 3, t:t + 1],
                                         self.gain[:, 1 if t < 2 else 0, 512 * h:512 * h + 512], ALU.mult, ALU.mult).then_inc(self.s_tmp, 1)
                n += 1

    def gpsimd(self, pool):
        n = 0
        for t in range(self.t0, NT):
            for h in range(2):
                x = self.g.x[:, t, 512 * h:512 * h + 512]
                pool.wait_ge(self.s_tmp, n + 1)
                pool.tensor_tensor(x, self.tmp[:, n % 2, :], x, ALU.add).then_inc(self.s_add, 1)
                n += 1


def stage_out(g, layer, w, kc, src, t0):
    nc = g.nc
    RING = 4
    with ExitStack() as ctx:
        slab = g.place(ctx, "wo_slab", [P, RING, D])
        tail = Tail(g, ctx, layer, 2, t0)
        s_w, s_used = [g.sem(f"wo_slab{i}") for i in range(RING)], g.sem("wo_used")
        with nc.Block() as block:
            @block.sync
            def _(sp):
                for k in range(kc):
                    if k >= RING:
                        sp.wait_ge(s_used, k - RING + 1)
                    sp.dma_start(slab[:, k % RING, :], w[k * P:(k + 1) * P, :]).then_inc(s_w[k % RING], 16)
                tail.load(sp)

            @block.tensor
            def _(pe):
                for k in range(kc):
                    pe.wait_ge(s_w[k % RING], 16 * (k // RING + 1))
                    for t in range(t0, NT):
                        for h in range(2):
                            mm = pe.matmul(g.ps[2 * (t - t0) + h][:, :], src[:, k, t * P:(t + 1) * P], slab[:, k % RING, 512 * h:512 * h + 512],
                                           start=(k == 0), stop=(k == kc - 1))
                        if k == kc - 1 and t < NT - 1:
                            mm.then_inc(tail.s_ready, 1)
                    mm.then_inc(tail.s_ready if k == kc - 1 else s_used, 1)

            @block.scalar
            def _(act):
                tail.scalar(act)

            @block.vector
            def _(dve):
                tail.vector(dve)

            @block.gpsimd
            def _(pool):
                tail.gpsimd(pool)


def stage_moe(g, layer, t0, out=None):
    nc, a = g.nc, g.a
    segs = (1,) if t0 else (0, 1)
    ns = len(segs)
    M = CAP * ns
    RA, RB = 6, 6
    SL = [(0, 512), (512, 1024), (1024, FF)]
    w1, w3, w2 = (a[n][layer] for n in ("exp_w1", "exp_w3", "exp_w2"))
    visits_a = lambda s: len(range(s, DC, RA))
    visits_b = lambda s: len(range(s, FC, RB))
    with ExitStack() as ctx:
        sb = lambda name, shape: g.place(ctx, name, shape)
        wa = sb("moe_w13", [P, RA, 2, FF])
        wb = sb("moe_w2", [P, RB, D])
        hm = sb("moe_h", [P, NT, D])
        oe = sb("moe_rows", [P, 2, NE // 4, D])
        selt = sb("moe_put", [P, 2, NE // 4, SEG])
        sel = sb("moe_pick", [P, 2, 2, NE * CAP + CAP])
        xg = sb("moe_xT", [P, 2, DC, M])
        s1 = sb("moe_silu", [M, FF])
        hidt = sb("moe_hidT", [P, FC, M])
        tail = Tail(g, ctx, layer, 5, t0)
        hid = s1
        g.hT = oe[:, :, :, :].rearrange("p s b d -> p (s b d)")[:, 0:DC * T].rearrange("p (c t) -> p c t", c=DC)
        g.xn = hm
        stage_norm(g, layer, 1, t0, ctx, True)
        with ExitStack() as rt:
            sr = lambda name, shape, dt=F32: g.place(rt, name, shape, dt)
            rw = sr("router_w", [P, DC, NE])
            aff = sr("affinity", [P, 2, 48])
            lg = sr("router_tmp", [P, 4, NE])
            st8 = sr("router_stat", [P, 4, 4])
            atr = sr("affinity_rows", [48, SEG])
            mx = sr("top_values", [48, 8])
            ix = sr("top_index", [48, CAP], U32)
            ixf = sr("top_index_f", [48, CAP])
            own = sr("own_expert", [48, NE])
            bdx = sr("index_diag", [48, NE, CAP])
            tok = sr("token_number", [P, 2])
            wsel = sr("weighed_pick", [P, 2, NE * CAP])
            (s_rw, s_lg, s_max, s_e, s_aff, s_at, s_row, s_bd, s_bc, s_own, s_sel, s_ws, s_st, s_sto, s_hb, s_hbo) = (g.sem("route_" + n) for n in (
                "weights", "logits", "max", "exp", "affinity", "rows", "diag", "diag2", "spread", "own", "pick", "weighed", "put", "put_out", "h_back", "h_out"))
            with nc.Block() as block:
                @block.sync
                def _(sp):
                    sp.dma_start(rw[:, :, :], a["router_w"][layer].rearrange("(c p) e -> p c e", p=P)).then_inc(s_rw, 16)

                @block.gpsimd
                def _(pool):
                    g.pool.do(pool.memset(own[:, :], 0.0))
                    g.pool.do(pool.iota(tok[:, :], [[P, 2]], base=0, channel_multiplier=1, allow_small_or_imprecise_dtypes=True))
                    g.pool.join(pool)
                    for r in (0, 32):
                        g.pool.step(pool, pool.affine_select(out=own[:, :], in_=own[:, :], compare_op=ALU.not_equal, fill=1.0, base=-r, pattern=[[-1, NE]], channel_multiplier=1))
                    pool.memset(sel[:, :, :, NE * CAP:], 0.0).then_inc(s_own, 1)

                @block.tensor
                def _(pe):
                    pe.wait_ge(s_rw, 16)
                    for t in range(t0, NT):
                        for dc in range(DC):
                            mm = pe.matmul(g.ps[4][:, t * NE:(t + 1) * NE], g.hT[:, dc, t * P:(t + 1) * P], rw[:, dc, :], start=(dc == 0), stop=(dc == DC - 1))
                    mm.then_inc(s_lg, 1)
                    k = 0
                    for t in range(t0, NT):
                        for h in range(2):
                            if k >= 2:
                                pe.wait_ge(s_hbo, k - 1)
                            for i in range(4):
                                mm = pe.transpose(g.ps[6 + k % 2][:, i * P:(i + 1) * P], g.hT[:, 4 * h + i, t * P:(t + 1) * P], g.ident[:, :])
                            mm.then_inc(s_hb, 1)
                            k += 1
                    pe.wait_ge(s_aff, 1)
                    for j in range(2):
                        mm = pe.transpose(g.ps[5][0:48, j * P:(j + 1) * P], aff[:, j, :], g.ident[:, :])
                    mm.then_inc(s_at, 1)
                    pe.wait_ge(s_bd, 1)
                    for n, s in enumerate(segs):
                        pe.matmul(g.ps[n][:, :], g.ones[32 * s:32 * s + 16, :], bdx[32 * s:32 * s + 16, :, :].rearrange("r e c -> r (e c)"), start=True, stop=True).then_inc(s_bc, 1)
                    k = 0
                    for s in segs:
                        for j in range(2):
                            pe.wait_ge(s_ws, k + 1)
                            if k >= 2:
                                pe.wait_ge(s_sto, k - 1)
                            for b in range(4):
                                mm = pe.transpose(g.ps[2 + k % 2][:, b * P:(b + 1) * P], wsel[:, k % 2, b * P:(b + 1) * P], g.ident[:, :])
                            mm.then_inc(s_st, 1)
                            k += 1

                @block.scalar
                def _(act):
                    act.wait_ge(s_max, 1)
                    act.activation(lg[:, t0:NT, :], lg[:, t0:NT, :], ACT.Exp).then_inc(s_e, 1)
                    k = 0
                    for t in range(t0, NT):
                        for h in range(2):
                            act.wait_ge(s_hb, k + 1)
                            act.activation(hm[:, t, 512 * h:512 * h + 512], g.ps[6 + k % 2][:, :], ACT.Copy).then_inc(s_hbo, 1)
                            k += 1
                    for k in range(2 * ns):
                        act.wait_ge(s_st, k + 1)
                        s, j = segs[k // 2], k % 2
                        act.activation(selt[:, s, :, j * P:(j + 1) * P], g.ps[2 + k % 2][:, :].rearrange("p (b t) -> p b t", b=4), ACT.Copy).then_inc(s_sto, 1)

                @block.vector
                def _(dve):
                    dv = g.dve
                    n = NT - t0
                    dv.do(dve.memset(aff[:, :, :], 0.0))
                    dve.wait_ge(s_lg, 1)
                    psl = g.ps[4][:, t0 * NE:NT * NE].rearrange("p (t e) -> p t e", e=NE)
                    wide = lambda x: x.rearrange("p (t o) -> p t o", o=1).broadcast_to([P, n, NE])
                    dv.step(dve, dve.tensor_reduce(st8[:, 0, t0:NT], psl, AX.X, ALU.max))
                    dve.tensor_tensor(lg[:, t0:NT, :], psl, wide(st8[:, 0, t0:NT]), ALU.subtract).then_inc(s_max, 1)
                    dve.wait_ge(s_e, 1)
                    dv.step(dve, dve.tensor_reduce(st8[:, 1, t0:NT], lg[:, t0:NT, :], AX.X, ALU.add))
                    dv.step(dve, dve.reciprocal(st8[:, 2, t0:NT], st8[:, 1, t0:NT]))
                    for s in segs:
                        dv.do(dve.tensor_tensor(aff[:, :, 32 * s:32 * s + NE], lg[:, 2 * s:2 * s + 2, :],
                                                st8[:, 2, 2 * s:2 * s + 2].rearrange("p (t o) -> p t o", o=1).broadcast_to([P, 2, NE]), ALU.mult))
                    dv.join(dve)
                    dve.memset(g.small[:, 0:1], 0.0).then_inc(s_aff, 1)
                    dve.wait_ge(s_at, 1)
                    dv.step(dve, dve.tensor_copy(atr[:, :], g.ps[5][0:48, 0:SEG]))
                    for k in range(CAP // 8):
                        dv.step(dve, dve.max(mx[:, :], atr[:, :]))
                        dv.step(dve, dve.max_index(ix[:, 8 * k:8 * k + 8], mx[:, :], atr[:, :]))
                        if k < CAP // 8 - 1:
                            dv.step(dve, dve.match_replace(atr[:, :], mx[:, :], atr[:, :], -1.0))
                    dv.step(dve, dve.tensor_copy(ixf[:, :], ix[:, :]))
                    dve.wait_ge(s_own, 1)
                    dve.tensor_tensor(bdx[:, :, :], own[:, :].rearrange("r (e o) -> r e o", o=1).broadcast_to([48, NE, CAP]),
                                      ixf[:, :].rearrange("r (o c) -> r o c", o=1).broadcast_to([48, NE, CAP]), ALU.mult).then_inc(s_bd, 1)
                    k = 0
                    for n_, s in enumerate(segs):
                        dve.wait_ge(s_bc, n_ + 1)
                        for j in range(2):
                            dv.step(dve, dve.tensor_scalar(sel[:, s, j, 0:NE * CAP], g.ps[n_][:, :], tok[:, j:j + 1], None, ALU.is_equal))
                            if k >= 2:
                                dve.wait_ge(s_st, k - 1)
                            dve.tensor_tensor(wsel[:, k % 2, :].rearrange("p (e c) -> p e c", e=NE), sel[:, s, j, 0:NE * CAP].rearrange("p (e c) -> p e c", e=NE),
                                              aff[:, j, 32 * s:32 * s + NE].rearrange("p (e o) -> p e o", o=1).broadcast_to([P, NE, CAP]), ALU.mult).then_inc(s_ws, 1)
                            k += 1
        s_wa, s_wb = [g.sem(f"moe_w13_{i}") for i in range(RA)], [g.sem(f"moe_w2_{i}") for i in range(RB)]
        (s_ua, s_ub, s_h, s_s, s_hid, s_ht, s_hto, s_y, s_o, s_gt, s_x, s_store, s_apart) = (g.sem("moe_" + n) for n in (
            "w13_used", "w2_used", "h_ready", "silu_ready", "hid_ready", "hidT_ready", "hidT_out", "rows_ready", "rows_out", "picked", "xT_ready", "stored", "waits_apart"))
        NB = NE // 4
        with nc.Block() as block:
            @block.sync
            def _(sp):
                tail.load(sp)

                def weights(i, j, first):
                    e = 4 * i + j if isinstance(i, int) else None
                    pick = lambda x: x[e] if e is not None else x[bass.ds(i * 4 + j, 1)].rearrange("o p f -> (o p) f")
                    for c in range(DC):
                        n = j * DC + c - RA
                        former = j * DC + max(x for x in range(-DC, c) if x % DC % RA == c % RA and x < c)
                        if not (first and former < 0):
                            sp.wait_ge(s_ua, i * 4 * DC + former + 1)
                        for k, w in enumerate((w1, w3)):
                            sp.dma_start(wa[:, c % RA, k, :], pick(w)[c * P:(c + 1) * P, :]).then_inc(s_wa[c % RA], 16)
                    for c in range(FC):
                        former = j * FC + max(x for x in range(-FC, c) if x % FC % RB == c % RB and x < c)
                        if not (first and former < 0):
                            sp.wait_ge(s_ub, i * 4 * FC + former + 1)
                        sp.dma_start(wb[:, c % RB, :], pick(w2)[c * P:(c + 1) * P, :]).then_inc(s_wb[c % RB], 16)

                for j in range(4):
                    weights(0, j, True)
                with sp.Fori(1, NB) as i:
                    for j in range(4):
                        weights(i, j, False)
                if out is not None:
                    for t in range(t0, NT):
                        sp.wait_ge(tail.s_add, 2 * (t - t0) + 2)
                        sp.dma_start(out[0, (t - t0) * P:(t - t0 + 1) * P, :], g.x[:, t, :]).then_inc(s_store, 16)
                    sp.wait_ge(s_store, 16 * (NT - t0))

            @block.tensor
            def _(pe):
                def pick(e, wait):
                    if wait is not None:
                        pe.wait_ge(s_x, wait)
                    for dc in range(DC):
                        for n, s in enumerate(segs):
                            for j in range(2):
                                c0 = e * CAP
                                cols = slice(c0, c0 + CAP) if isinstance(e, int) else bass.ds(c0, CAP)
                                mm = pe.matmul(g.ps[7][:, dc * M + n * CAP:dc * M + (n + 1) * CAP], hm[:, 2 * s + j, dc * P:(dc + 1) * P],
                                               sel[:, s, j, cols], start=(j == 0), stop=(j == 1))
                    mm.then_inc(s_gt, 1)

                def expert(i, j, first):
                    e = i * 4 + j
                    pe.wait_ge(s_x, e + 1)
                    if not first:
                        pe.wait_ge(s_hid, e)
                    for c in range(DC):
                        v = j * visits_a(c % RA) + c // RA + 1
                        pe.wait_ge(s_wa[c % RA], (i * (4 * visits_a(c % RA)) + v) * 32)
                        for k, (lo, hi) in enumerate(SL):
                            for m in range(2):
                                mm = pe.matmul(g.ps[k][64 * m:64 * m + M, 0:hi - lo], xg[:, j % 2, c, :], wa[:, c % RA, m, lo:hi], start=(c == 0), stop=(c == DC - 1))
                        mm.then_inc(s_ua, 1)
                    pick(e + 1, e + 1)
                    pe.wait_ge(s_hid, e + 1)
                    if not first:
                        pe.wait_ge(s_hto, 2 * e)
                    pe.sem_inc(s_apart, 1)
                    for c in range(FC):
                        mm = pe.transpose(g.ps[3 + c // 8][:, (c % 8) * M:(c % 8 + 1) * M], hid[:, c * P:(c + 1) * P], g.ident[0:M, 0:M])
                        if c in (7, FC - 1):
                            mm.then_inc(s_ht, 1)
                    if not first:
                        pe.wait_ge(s_o, e)
                    for c in range(FC):
                        if c in (0, 8):
                            pe.wait_ge(s_hto, 2 * e + 1 + c // 8)
                        v = j * visits_b(c % RB) + c // RB + 1
                        pe.wait_ge(s_wb[c % RB], (i * (4 * visits_b(c % RB)) + v) * 16)
                        for m in range(2):
                            mm = pe.matmul(g.ps[5 + m][64 * m:64 * m + M, :], hidt[:, c, :], wb[:, c % RB, 512 * m:512 * m + 512], start=(c == 0), stop=(c == FC - 1))
                        mm.then_inc(s_ub, 1)

                pick(0, None)
                for j in range(4):
                    expert(0, j, j == 0)
                with pe.Fori(1, NB) as i:
                    for j in range(4):
                        expert(i, j, False)
                pe.wait_ge(s_o, NE)
                for t in range(t0, NT):
                    s = t // 2
                    for h in range(2):
                        for b in range(NB):
                            mm = pe.matmul(g.ps[2 * (t - t0) + h][:, :], selt[:, s, b, (t % 2) * P:(t % 2 + 1) * P], oe[:, s, b, 512 * h:512 * h + 512],
                                           start=(b == 0), stop=(b == NB - 1))
                    mm.then_inc(tail.s_ready, 1)

            @block.scalar
            def _(act):
                def expert(i, j, first):
                    e = i * 4 + j
                    act.wait_ge(s_ua, (e + 1) * DC)
                    if not first:
                        act.wait_ge(s_ht, 2 * e)
                    for k, (lo, hi) in enumerate(SL):
                        ins = act.activation(s1[:, lo:hi], g.ps[k][0:M, 0:hi - lo], ACT.Silu)
                        ins.then_inc(s_s, 1)
                    if not first:
                        act.wait_ge(s_ub, e * FC)
                    for k, (lo, hi) in enumerate(((0, 8), (8, FC))):
                        act.wait_ge(s_ht, 2 * e + 1 + k)
                        act.activation(hidt[:, lo:hi, :], g.ps[3 + k][:, 0:(hi - lo) * M].rearrange("p (c m) -> p c m", m=M), ACT.Copy).then_inc(s_hto, 1)

                for j in range(4):
                    expert(0, j, j == 0)
                with act.Fori(1, NB) as i:
                    for j in range(4):
                        expert(i, j, False)
                tail.scalar(act)

            @block.vector
            def _(dve):
                def rows_in(i, j, wait):
                    e = i * 4 + j
                    dve.wait_ge(s_gt, e + 1)
                    if wait is not None:
                        dve.wait_ge(s_ua, wait)
                    dve.tensor_copy(xg[:, j % 2, :, :], g.ps[7][:, 0:DC * M].rearrange("p (c m) -> p c m", m=M)).then_inc(s_x, 1)

                def expert(i, j, first):
                    e = i * 4 + j
                    rows_in(i, j + 1, (e * DC) if not first else None)
                    for k, (lo, hi) in enumerate(SL):
                        dve.wait_ge(s_s, 3 * e + k + 1)
                        ins = dve.tensor_tensor(hid[:, lo:hi], g.ps[k][64:64 + M, 0:hi - lo], s1[:, lo:hi], ALU.mult)
                    ins.then_inc(s_hid, 1)
                    dve.wait_ge(s_ub, (e + 1) * FC)
                    at = slice(i, i + 1) if isinstance(i, int) else bass.ds(i, 1)
                    for n, s in enumerate(segs):
                        for m in range(2):
                            ins = dve.tensor_copy(oe[32 * j:32 * j + 32, s, at, 512 * m:512 * m + 512],
                                                  g.ps[5 + m][64 * m + 32 * n:64 * m + 32 * n + 32, :].rearrange("p (o d) -> p o d", o=1))
                    ins.then_inc(s_o, 1)

                rows_in(0, 0, None)
                for j in range(4):
                    expert(0, j, j == 0)
                with dve.Fori(1, NB) as i:
                    for j in range(4):
                        expert(i, j, False)
                tail.vector(dve)

            @block.gpsimd
            def _(pool):
                tail.gpsimd(pool)


def stage_rwkv_project(g):
    nc, a = g.nc, g.a
    RING = 2
    MU = COL_P2
    order = ((1, "w"), (4, "a"), (5, "g"), (2, "k"), (3, "v"), (0, "r"))
    lo_of = {"g": SEG, "r": SEG}
    W = {"k": a["rw_wk"], "v": a["rw_wv"], "r": a["rw_wr"]}
    with ExitStack() as ctx:
        sb = lambda name, shape: g.place(ctx, name, shape)
        xx = sb("shift", [P, DC, T])
        mix = sb("mixture", [P, 2, DC, T])
        slab = sb("rw_slab", [P, RING, DC, 256])
        lora = sb("rw_lora", [P, DC, 128 + 64 + 160])
        s_lora, s_slab, s_free, s_mix, s_used, s_mm, s_ev = g.sem("lora_loaded"), [g.sem(f"rw_slab{i}") for i in range(RING)], g.sem("rw_slab_free"), g.sem("mixed"), g.sem("mix_used"), g.sem("rw_product"), g.sem("rw_out")
        jobs = []
        with nc.Block() as block:
            @block.sync
            def _(sp):
                for d in range(2):
                    sp.dma_start(lora[:, :, 64 * d:64 * d + 64], a["rw_w1"][0, d].rearrange("(c p) r -> p c r", p=P)).then_inc(s_lora, 16)
                sp.dma_start(lora[:, :, 128:192], a["rw_a1"][0].rearrange("(c p) r -> p c r", p=P)).then_inc(s_lora, 16)
                sp.dma_start(lora[:, :, 192:352], a["rw_g1"][0].rearrange("(c p) r -> p c r", p=P)).then_inc(s_lora, 16)
                sp.dma_start(g.w2[0:64, :], a["rw_w2"][0, 0]).then_inc(s_lora, 16)
                sp.dma_start(g.w2[64:128, :], a["rw_w2"][0, 1]).then_inc(s_lora, 16)
                sp.dma_start(g.a2[:, :], a["rw_a2"][0]).then_inc(s_lora, 16)
                sp.dma_start(g.g2[:, 0, :], a["rw_g2"][0, 0:P, :]).then_inc(s_lora, 16)
                sp.dma_start(g.g2[0:32, 1, :], a["rw_g2"][0, P:160, :]).then_inc(s_lora, 16)
                n = 0
                for name in "kvr":
                    for q in range(4):
                        if n >= RING:
                            sp.wait_ge(s_free, n - RING + 1)
                        sp.dma_start(slab[:, n % RING, :, :], W[name][0, :, 256 * q:256 * q + 256].rearrange("(c p) n -> p c n", p=P)).then_inc(s_slab[n % RING], 16)
                        n += 1

            @block.vector
            def _(dve):
                for s in range(2):
                    lo, hi = SEG * s, SEG * (s + 1)
                    for c in range(DC):
                        g.dve.do(dve.tensor_tensor(xx[:, c, lo + 1:hi - 1], g.hT[:, c, lo:hi - 2], g.hT[:, c, lo + 2:hi], ALU.add))
                        g.dve.do(dve.tensor_copy(xx[:, c, lo:hi:SEG - 1], g.hT[:, c, lo + 1:hi - 1:SEG - 3]))
                g.dve.join(dve)
                for c in range(DC):
                    g.dve.do(dve.scalar_tensor_tensor(xx[:, c, :], xx[:, c, :], 0.5, g.hT[:, c, :], ALU.mult, ALU.subtract))
                g.dve.join(dve)
                for n, (m, name) in enumerate(order):
                    lo = lo_of.get(name, 0)
                    if n >= 2:
                        dve.wait_ge(s_used, n - 1)
                    for c in range(DC):
                        ins = dve.scalar_tensor_tensor(mix[:, n % 2, c, lo:T], xx[:, c, lo:T], g.cols[:, MU + 8 * m + c:MU + 8 * m + c + 1], g.hT[:, c, lo:T], ALU.mult, ALU.add)
                    ins.then_inc(s_mix, 1)

            @block.tensor
            def _(pe):
                k = 0
                pe.wait_ge(s_lora, 144)
                for n, (m, name) in enumerate(order):
                    lo = lo_of.get(name, 0)
                    pe.wait_ge(s_mix, n + 1)
                    parts = {"w": [(0, 128)], "a": [(128, 192)], "g": [(192, 320), (320, 352)]}.get(name, [None] * 8)
                    for q, part in enumerate(parts):
                        if k >= 8:
                            pe.wait_ge(s_ev, k - 7)
                        if part is None:
                            ns = 4 * (n - 3) + q // 2
                            if q % 2 == 0:
                                pe.wait_ge(s_slab[ns % RING], 16 * (ns // RING + 1))
                        rows = part[1] - part[0] if part else P
                        for c in range(DC):
                            lhs = lora[:, c, part[0]:part[1]] if part else slab[:, ns % RING, c, P * (q % 2):P * (q % 2) + P]
                            mm = pe.matmul(g.ps[k % 8][0:rows, 0:T - lo], lhs, mix[:, n % 2, c, lo:T], start=(c == 0), stop=(c == DC - 1))
                        mm.then_inc(s_mm, 1)
                        k += 1
                        pe.wait_ge(s_mm, k)
                        if part is None and q % 2:
                            pe.nop().then_inc(s_free, 1)
                    pe.nop().then_inc(s_used, 1)

            @block.scalar
            def _(act):
                act.wait_ge(s_mm, 1)
                act.activation(g.tw[:, :], g.ps[0][:, :], ACT.Tanh).then_inc(s_ev, 1)
                act.wait_ge(s_mm, 2)
                act.activation(g.ta[:, :], g.ps[1][0:64, :], ACT.Copy).then_inc(s_ev, 1)
                act.wait_ge(s_mm, 3)
                act.activation(g.tg[:, 0, :], g.ps[2][:, 0:SEG], ACT.Sigmoid).then_inc(s_ev, 1)
                act.wait_ge(s_mm, 4)
                act.activation(g.tg[0:32, 1, :], g.ps[3][0:32, 0:SEG], ACT.Sigmoid).then_inc(s_ev, 1)
                for k in range(4, 28):
                    q = (k - 4) % 8
                    dst = (g.kT, g.vT, g.rT)[(k - 4) // 8]
                    act.wait_ge(s_mm, k + 1)
                    act.activation(dst[:, q, :], g.ps[k % 8][:, 0:SEG] if dst is g.rT else g.ps[k % 8][:, :], ACT.Copy).then_inc(s_ev, 1)


def stage_rwkv_masks(g):
    nc = g.nc
    s_a, s_b = g.sem("mask_filled"), g.sem("mask_cut")
    with nc.Block() as block:
        @block.gpsimd
        def _(pool):
            pool.memset(g.lev[:, :, :, :], 0.0)
            pool.memset(g.i64[:, :], 0.0)
            pool.memset(g.bones[:, :], 0.0)
            pool.memset(g.inc[:, :, :], 1.0)
            pool.memset(g.strict[:, :, :], 1.0).then_inc(s_a, 1)
            pool.wait_ge(s_a, 1)
            n = 0
            for h in range(2):
                r = slice(64 * h, 64 * h + 64)
                ins = [pool.memset(g.bones[r, 64 * h:64 * h + 64], 1.0),
                       pool.affine_select(out=g.i64[r, :], in_=g.i64[r, :], compare_op=ALU.not_equal, fill=1.0, base=0, pattern=[[-1, 64]], channel_multiplier=1)]
                for d, sgn in ((0, 1), (1, -1)):
                    ins.append(pool.affine_select(out=g.inc[r, d, :], in_=g.inc[r, d, :], compare_op=ALU.is_ge, fill=0.0, base=0, pattern=[[sgn, 64]], channel_multiplier=-sgn))
                    ins.append(pool.affine_select(out=g.strict[r, d, :], in_=g.strict[r, d, :], compare_op=ALU.is_gt, fill=0.0, base=0, pattern=[[sgn, 64]], channel_multiplier=-sgn))
                for i in ins:
                    i.then_inc(s_b, 1)
                n += len(ins)
                for lv in range(6):
                    m = 1 << lv
                    for k in range(2):
                        view = g.lev[r, k, lv, :].rearrange("p (b h r) -> p b h r", h=2, r=m)[:, :, 1 - k, :]
                        pool.memset(view, 1.0).then_inc(s_b, 1)
                        n += 1
                        pool.wait_ge(s_b, n)
                        pool.affine_select(out=view, in_=view, compare_op=ALU.is_ge, fill=0.0, base=-k * m, pattern=[[-2 * m, 32 // m], [0, m]], channel_multiplier=1).then_inc(s_b, 1)
                        n += 1
                        pool.wait_ge(s_b, n)
                        pool.affine_select(out=view, in_=view, compare_op=ALU.is_ge, fill=0.0, base=k * m + m - 1, pattern=[[2 * m, 32 // m], [0, m]], channel_multiplier=-1).then_inc(s_b, 1)
                        n += 1


def stage_rwkv(g):
    nc = g.nc
    K = 0.6065306597126334
    C3 = lambda x: x.rearrange("p (c t) -> p c t", t=LC)
    ORDER = ((0, 1, 2, 3, 4, 5, 6, 7), (3, 2, 1, 0, 7, 6, 5, 4))
    LAT = NCH // 2
    HALF = (slice(0, 64), slice(64, 128))
    with ExitStack() as ctx:
        sb = lambda name, shape: g.place(ctx, name, shape)
        two = lambda name, shape: [sb(f"{name}{d}", shape) for d in range(2)]
        par = sb("pair_cols", [P, 8])
        w2s, a2s, g2s = sb("w2_pair", [P, P]), sb("a2_pair", [64, P]), sb("g2_pair", [P, 2, P])
        k0, v0, r0 = sb("k_pair", [P, T]), sb("v_pair", [P, T]), sb("r_pair", [P, SEG])
        kk, al, bb, km, t2 = (sb(n, [P, T]) for n in ("kk", "iclr", "bvec", "kmod", "rw_t2"))
        gp, bon = sb("gate_pair", [P, SEG]), sb("bonus", [P, SEG])
        one = sb("chunk_starts", [P, 2, T])
        sg, cs, ex = two("rw_sig", [P, T]), two("rw_cum", [P, T]), two("rw_exc", [P, T])
        em, ep = sg, cs
        ah, bh, kh, bbar, kbar = (two(n, [P, T]) for n in ("a_hat", "b_hat", "k_hat", "b_bar", "k_bar"))
        rh = two("r_hat", [P, SEG])
        ecl = two("e_cend", [P, NCH])
        nt, x, xt, pp, nk = (two(n, [P, NCH, LC]) for n in ("n_t", "x_inv", "x_inv_t", "p_prod", "nk_t"))
        t1 = nt[0][:, :, :].rearrange("p c t -> p (c t)")
        nlev = two("n_levels", [P, 2, NCH, LC])
        rb = two("r_products", [P, 2 * LAT, LC])
        rhs = two("a_and_nkv", [P, NCH, 2, LC])
        au = [n[:, :, :, :].rearrange("p l c t -> p (l c t)").rearrange("p (c k t) -> p c k t", k=2, t=LC) for n in nlev]
        bt, kt, st = (two(n, [P, NCH, LC]) for n in ("b_tok", "k_tok", "state"))
        gt, dg, rt = x, nt, [p[:, 0:LAT, :] for p in pp]
        vt = sb("v_tok", [P, NCH, LC])
        yn, ysq = rhs[0][:, 0:2, :, :].rearrange("p a b t -> p (a b) t"), rhs[1][:, 0:2, :, :].rearrange("p a b t -> p (a b) t")
        ystat = sb("y_stat", [P, 4, LAT])
        yc = sb("y_chan", [P, SEG])
        names = ("apart", "pass_end", "staged", "lora_mm", "sig", "iclr", "gate", "kksq", "kksum", "kkroot", "kmod", "bonus_in", "bonus_mm", "cum", "exps", "hats", "bars",
                 "mm1", "nt", "x0", "mask", "nlev", "pmm", "pcopy", "xmm", "xadd", "tokmm", "tok", "nkvmm", "nkv", "aumm", "au", "gmm", "gt", "dg", "smm", "scopy", "ymm", "ystat1", "ysq", "yvar", "yroot", "yn", "ytmm", "yout")
        S = {n: g.sem("rw_" + n) for n in names}
        with nc.Block() as block:
            def W(eng, name, i, per, k):
                eng.wait_ge(S[name], i * per + k)

            @block.gpsimd
            def _(pool):
                g.pool.do(pool.memset(one[:, :, :], 1.0))
                g.pool.join(pool)
                g.pool.do(pool.memset(one[:, 0, 0::LC], 0.0))
                g.pool.do(pool.memset(one[:, 1, LC - 1::LC], 0.0))
                g.pool.join(pool)
                with pool.Fori(0, DC) as i:
                    pool.tensor_copy(w2s[:, :], g.w2[:, bass.ds(i * P, P)]).then_inc(S["staged"], 1)
                    pool.tensor_copy(a2s[:, :], g.a2[:, bass.ds(i * P, P)]).then_inc(S["staged"], 1)
                    pool.tensor_copy(g2s[:, 0, :], g.g2[:, 0, bass.ds(i * P, P)]).then_inc(S["staged"], 1)
                    pool.tensor_copy(g2s[0:32, 1, :], g.g2[0:32, 1, bass.ds(i * P, P)]).then_inc(S["staged"], 1)
                    for d in range(2):
                        W(pool, "hats", i, 2, d + 1)
                        e3 = lambda: ecl[d][:, :].rearrange("p (c o) -> p c o", o=1).broadcast_to([P, NCH, LC])
                        pool.tensor_tensor(C3(bbar[d][:, :]), C3(bh[d][:, :]), e3(), ALU.mult).then_inc(S["bars"], 1)
                        pool.tensor_tensor(C3(kbar[d][:, :]), C3(kh[d][:, :]), e3(), ALU.mult).then_inc(S["bars"], 1)
                    for lv in range(5):
                        for d in range(2):
                            if lv == 0:
                                W(pool, "nt", i, 2, d + 1)
                            if lv >= 2:
                                W(pool, "pmm", i, 10, 2 * (lv - 2) + d + 1)
                            pool.tensor_tensor(nlev[d][:, lv % 2, :, :], nt[d][:, :, :], g.lev[:, d, lv + 1, :].rearrange("p (o t) -> p o t", o=1).broadcast_to([P, NCH, LC]), ALU.mult).then_inc(S["nlev"], 1)
                    W(pool, "nlev", i, 10, 10)
                    W(pool, "x0", i, 2, 2)
                    for d in range(2):
                        pool.tensor_tensor(dg[d][:, :, :], g.i64[:, :].rearrange("p (o t) -> p o t", o=1).broadcast_to([P, NCH, LC]),
                                           ecl[d][:, :].rearrange("p (c o) -> p c o", o=1).broadcast_to([P, NCH, LC]), ALU.mult).then_inc(S["dg"], 1)
                    pool.wait_ge(S["pass_end"], i + 1)

            @block.vector
            def _(dve):
                dv = g.dve
                inc8 = lambda m, n: m.rearrange("p (o t) -> p o t", o=1).broadcast_to([P, n, LC])
                def body(i):
                    dv.do(dve.tensor_copy(par[:, :].rearrange("p (k o) -> p k o", o=1), g.cols[:, COL_P2 + 48:COL_P2 + 112].rearrange("p (k r) -> p k r", r=8)[:, :, bass.ds(i, 1)]))
                    dv.do(dve.tensor_copy(k0[:, :].rearrange("p (o t) -> p o t", o=1), g.kT[:, bass.ds(i, 1), :]))
                    dv.do(dve.tensor_copy(v0[:, :].rearrange("p (o t) -> p o t", o=1), g.vT[:, bass.ds(i, 1), :]))
                    dv.do(dve.tensor_copy(r0[:, :].rearrange("p (o t) -> p o t", o=1), g.rT[:, bass.ds(i, 1), :]))
                    dv.join(dve)
                    dve.tensor_scalar(kk[:, :], k0[:, :], par[:, 3:4], None, ALU.mult).then_inc(S["cum"], 1)
                    for d in range(2):
                        W(dve, "sig", i, 2, d + 1)
                        order = slice(None) if d == 0 else slice(None, None, -1)
                        dv.step(dve, dve.tensor_tensor_scan(cs[d][:, order], one[:, d, order], sg[d][:, order], 0.0, ALU.mult, ALU.add))
                        dve.tensor_tensor(ex[d][:, :], cs[d][:, :], sg[d][:, :], ALU.subtract).then_inc(S["cum"], 1)
                    W(dve, "iclr", i, 1, 1)
                    dv.step(dve, dve.tensor_scalar(t1[:, :], al[:, :], 1.0, par[:, 4:5], ALU.subtract, ALU.mult))
                    dv.step(dve, dve.scalar_tensor_tensor(km[:, :], t1[:, :], 1.0, k0[:, :], ALU.add, ALU.mult))
                    dv.step(dve, dve.tensor_tensor(bon[:, :], r0[:, :], km[:, SEG:T], ALU.mult))
                    dve.tensor_scalar(bon[:, :], bon[:, :], par[:, 5:6], None, ALU.mult).then_inc(S["bonus_in"], 1)
                    W(dve, "kkroot", i, 1, 1)
                    dv.step(dve, dve.reciprocal(t2[:, :], t2[:, :]))
                    dv.step(dve, dve.tensor_tensor(kk[:, :], kk[:, :], t2[:, :], ALU.mult))
                    dv.step(dve, dve.tensor_tensor(bb[:, :], kk[:, :], al[:, :], ALU.mult))
                    for d in range(2):
                        W(dve, "exps", i, 2, d + 1)
                        end = ep[d][:, LC - 1::LC] if d == 0 else ep[d][:, 0::LC]
                        dv.do(dve.tensor_copy(ecl[d][:, :], end))
                        dv.do(dve.scalar_tensor_tensor(ah[d][:, :], kk[:, :], -1.0, ex[d][:, :], ALU.mult, ALU.mult))
                        dv.do(dve.tensor_tensor(bh[d][:, :], bb[:, :], em[d][:, :], ALU.mult))
                        dv.do(dve.tensor_tensor(kh[d][:, :], km[:, :], em[d][:, :], ALU.mult))
                        dv.do(dve.tensor_tensor(rh[d][:, :], r0[:, :], ep[d][:, SEG:T], ALU.mult))
                        dv.join(dve)
                        dve.memset(g.small[:, 0:1], 0.0).then_inc(S["hats"], 1)
                    W(dve, "bonus_mm", i, 1, 1)
                    dv.step(dve, dve.tensor_tensor(bon[:, :], g.ps[5][:, 0:SEG], v0[:, SEG:T], ALU.mult))
                    dve.memset(g.small[:, 0:1], 0.0).then_inc(S["kmod"], 1)
                    for d in range(2):
                        B = 4 * d
                        W(dve, "nt", i, 2, d + 1)
                        W(dve, "mm1", i, 8, 4 * d + 2)
                        dv.do(dve.tensor_tensor(x[d][:, :, :], C3(g.ps[B + 1][:, :]), inc8(g.lev[:, 1 - d, 0, :], NCH), ALU.mult))
                        dv.do(dve.tensor_tensor(xt[d][:, :, :], nt[d][:, :, :], inc8(g.lev[:, d, 0, :], NCH), ALU.mult))
                        dv.join(dve)
                        dv.do(dve.tensor_tensor(x[d][:, :, :], x[d][:, :, :], inc8(g.i64[:, :], NCH), ALU.add))
                        dv.do(dve.tensor_tensor(xt[d][:, :, :], xt[d][:, :, :], inc8(g.i64[:, :], NCH), ALU.add))
                        dv.join(dve)
                        dve.memset(g.small[:, 0:1], 0.0).then_inc(S["x0"], 1)
                        W(dve, "mm1", i, 8, 4 * d + 4)
                        dve.tensor_tensor(nk[d][:, :, :], C3(g.ps[B + 2][:, :]), inc8(g.strict[:, d, :], NCH), ALU.mult).then_inc(S["mask"], 1)
                        dve.tensor_tensor(rb[d][:, :, :], C3(g.ps[B + 3][:, :]), inc8(g.inc[:, d, :], 2 * LAT), ALU.mult).then_inc(S["mask"], 1)
                    for lv in range(5):
                        for d in range(2):
                            B = 4 * d
                            W(dve, "xmm", i, 10, 2 * lv + d + 1)
                            if lv < 4:
                                dv.do(dve.tensor_tensor(x[d][:, :, :], C3(g.ps[B + 1][:, :]), x[d][:, :, :], ALU.add))
                            dv.do(dve.tensor_tensor(xt[d][:, :, :], C3(g.ps[B + 2][:, :]), xt[d][:, :, :], ALU.add))
                            dv.join(dve)
                            dve.memset(g.small[:, 0:1], 0.0).then_inc(S["xadd"], 1)
                    for d in range(2):
                        B = 4 * d
                        W(dve, "aumm", i, 2, d + 1)
                        dve.tensor_copy(au[d][:, LAT:NCH, :, :], g.ps[B + 1][:, :].rearrange("p (c k t) -> p c k t", k=2, t=LC)).then_inc(S["au"], 1)
                    for d in range(2):
                        B = 4 * d
                        W(dve, "gmm", i, 2, d + 1)
                        W(dve, "dg", i, 2, d + 1)
                        dve.tensor_tensor(gt[d][:, :, :], C3(g.ps[B + 2][:, :]), dg[d][:, :, :], ALU.add).then_inc(S["gt"], 1)
                        dve.tensor_tensor(rt[d][:, :, :], C3(g.ps[B + 3][:, 0:SEG]), C3(rh[d][:, :]), ALU.add).then_inc(S["gt"], 1)
                    for k in range(NCH - 1):
                        c = ORDER[0][k + 1]
                        W(dve, "smm", i, 14, 2 * k + 1)
                        dve.tensor_copy(st[0][:, c, :], g.ps[0][:, k * LC:(k + 1) * LC]).then_inc(S["scopy"], 1)
                    W(dve, "ymm", i, 1, 1)
                    y = C3(g.ps[3][:, 0:SEG])
                    wide = lambda v: v.rearrange("p (c o) -> p c o", o=1).broadcast_to([P, LAT, LC])
                    dv.step(dve, dve.tensor_reduce(ystat[:, 0, :], y, AX.X, ALU.add))
                    dv.step(dve, dve.tensor_scalar(ystat[:, 0, :], ystat[:, 0, :], 1.0 / LC, None, ALU.mult))
                    dve.tensor_tensor(yn[:, :, :], y, wide(ystat[:, 0, :]), ALU.subtract).then_inc(S["ystat1"], 1)
                    W(dve, "ysq", i, 1, 1)
                    dve.tensor_reduce(ystat[:, 1, :], ysq[:, :, :], AX.X, ALU.add).then_inc(S["yvar"], 1)
                    W(dve, "yroot", i, 1, 1)
                    dv.step(dve, dve.reciprocal(ystat[:, 3, :], ystat[:, 2, :]))
                    dve.tensor_tensor(yn[:, :, :], yn[:, :, :], wide(ystat[:, 3, :]), ALU.mult).then_inc(S["yn"], 1)
                    W(dve, "ytmm", i, 1, 1)
                    dv.step(dve, dve.tensor_scalar(yc[:, :], g.ps[2][:, 0:SEG], par[:, 6:7], par[:, 7:8], ALU.mult, ALU.add))
                    dv.step(dve, dve.tensor_tensor(yc[:, :], yc[:, :], bon[:, :], ALU.add))
                    W(dve, "gate", i, 1, 1)
                    dve.tensor_tensor(g.yT[:, bass.ds(i, 1), :], yc[:, :].rearrange("p (o t) -> p o t", o=1), gp[:, :].rearrange("p (o t) -> p o t", o=1), ALU.mult).then_inc(S["pass_end"], 1)
                    dve.wait_ge(S["pass_end"], i + 1)

                with dve.Fori(0, DC) as i:
                    dv.enter(i, g.rw_steps)
                    body(i)
                    print("rw steps", dv.n) if dv.n != g.rw_steps else None
                    dv.leave(DC)

            @block.scalar
            def _(act):
                with act.Fori(0, DC) as i:
                    W(act, "cum", i, 3, 1)
                    act.activation(t2[:, :], kk[:, :], ACT.Square).then_inc(S["kksq"], 1)
                    for d in range(2):
                        W(act, "lora_mm", i, 4, d + 1)
                        act.activation(sg[d][:, :], g.ps[d][:, :], ACT.Sigmoid, bias=par[:, d:d + 1]).then_inc(S["sig"], 1)
                    W(act, "lora_mm", i, 4, 3)
                    act.activation(al[:, :], g.ps[2][:, :], ACT.Sigmoid, bias=par[:, 2:3]).then_inc(S["iclr"], 1)
                    W(act, "lora_mm", i, 4, 4)
                    act.activation(gp[:, :], g.ps[3][:, 0:SEG], ACT.Copy).then_inc(S["gate"], 1)
                    W(act, "kksum", i, 1, 1)
                    act.activation(t2[:, :], g.ps[4][:, :], ACT.Sqrt, bias=g.eps2[:, 0:1]).then_inc(S["kkroot"], 1)
                    for d in range(2):
                        W(act, "cum", i, 3, 2 + d)
                        act.activation(em[d][:, :], cs[d][:, :], ACT.Exp, scale=K)
                        act.activation(ep[d][:, :], cs[d][:, :], ACT.Exp, scale=-K)
                        act.activation(ex[d][:, :], ex[d][:, :], ACT.Exp, scale=-K).then_inc(S["exps"], 1)
                    for d in range(2):
                        W(act, "mm1", i, 8, 4 * d + 1)
                        act.activation(nt[d][:, :, :], C3(g.ps[4 * d][:, :]), ACT.Copy).then_inc(S["nt"], 1)
                    def tok(k, dst, bank):
                        W(act, "tokmm", i, 7, k)
                        act.activation(dst, C3(g.ps[bank][:, :]), ACT.Copy).then_inc(S["tok"], 1)

                    def pcopy(lv):
                        for d in range(2):
                            W(act, "pmm", i, 10, 2 * lv + d + 1)
                            act.activation(pp[d][:, :, :], C3(g.ps[4 * d][:, :]), ACT.Copy).then_inc(S["pcopy"], 1)

                    tok(1, vt[:, :, :], 3)
                    tok(2, rhs[0][:, :, 0, :], 7)
                    pcopy(0)
                    tok(3, rhs[1][:, :, 0, :], 3)
                    tok(4, bt[0][:, :, :], 7)
                    pcopy(1)
                    tok(5, bt[1][:, :, :], 3)
                    tok(6, kt[0][:, :, :], 7)
                    pcopy(2)
                    tok(7, kt[1][:, :, :], 3)
                    pcopy(3)
                    for d in range(2):
                        W(act, "nkvmm", i, 2, d + 1)
                        act.activation(rhs[d][:, :, 1, :], C3(g.ps[4 * d + 3][:, :]), ACT.Copy).then_inc(S["nkv"], 1)
                    pcopy(4)
                    for d in range(2):
                        W(act, "aumm", i, 2, d + 1)
                        act.activation(au[d][:, 0:LAT, :, :], g.ps[4 * d][:, :].rearrange("p (c k t) -> p c k t", k=2, t=LC), ACT.Copy).then_inc(S["au"], 1)
                    for k in range(NCH - 1):
                        c = ORDER[1][k + 1]
                        W(act, "smm", i, 14, 2 * k + 2)
                        act.activation(st[1][:, c, :], g.ps[4][:, k * LC:(k + 1) * LC], ACT.Copy).then_inc(S["scopy"], 1)
                    W(act, "ystat1", i, 1, 1)
                    act.activation(ysq[:, :, :], yn[:, :, :], ACT.Square).then_inc(S["ysq"], 1)
                    W(act, "yvar", i, 1, 1)
                    act.activation(ystat[:, 2, :], ystat[:, 1, :], ACT.Sqrt, bias=g.eps[:, 1:2], scale=1.0 / LC).then_inc(S["yroot"], 1)
                    act.wait_ge(S["pass_end"], i + 1)

            @block.tensor
            def _(pe):
                def apart():
                    pe.sem_inc(S["apart"], 1)

                def each(bank, col0, lhs, rhs_, chunks, width=LC, start=True, stop=True, cols=None):
                    apart()
                    for n, c in enumerate(chunks):
                        for h in HALF:
                            o = col0 + (n if cols is None else cols[n]) * width
                            mm = pe.matmul(g.ps[bank][h, o:o + width], lhs(c, h), rhs_(c, h), start=start, stop=stop)
                    return mm

                tk = lambda x: (lambda c, h: x[h, c * LC:(c + 1) * LC])
                lat = lambda x: (lambda c, h: x[h, (c - LAT) * LC:(c - LAT + 1) * LC])
                ch = lambda x: (lambda c, h: x[h, c, :])
                ALL, LATS = range(NCH), range(LAT, NCH)
                eye = lambda c, h: g.ident[h, h]
                with pe.Fori(0, DC) as i:
                    W(pe, "staged", i, 4, 4)
                    for d in range(2):
                        pe.matmul(g.ps[d][:, :], w2s[HALF[d], :], g.tw[HALF[d], :], start=True, stop=True).then_inc(S["lora_mm"], 1)
                    pe.matmul(g.ps[2][:, :], a2s[:, :], g.ta[:, :], start=True, stop=True).then_inc(S["lora_mm"], 1)
                    pe.matmul(g.ps[3][:, 0:SEG], g2s[:, 0, :], g.tg[:, 0, :], start=True, stop=False)
                    pe.matmul(g.ps[3][:, 0:SEG], g2s[0:32, 1, :], g.tg[0:32, 1, :], start=False, stop=True).then_inc(S["lora_mm"], 1)
                    W(pe, "kksq", i, 1, 1)
                    pe.matmul(g.ps[4][:, :], g.bones[:, :], t2[:, :], start=True, stop=True).then_inc(S["kksum"], 1)
                    W(pe, "bonus_in", i, 1, 1)
                    pe.matmul(g.ps[5][:, 0:SEG], g.bones[:, :], bon[:, :], start=True, stop=True).then_inc(S["bonus_mm"], 1)
                    W(pe, "kmod", i, 1, 1)
                    W(pe, "gate", i, 1, 1)
                    W(pe, "kkroot", i, 1, 1)
                    for d in range(2):
                        B = 4 * d
                        W(pe, "hats", i, 2, d + 1)
                        each(B, 0, tk(bh[d]), tk(ah[d]), ALL).then_inc(S["mm1"], 1)
                        each(B + 1, 0, tk(ah[d]), tk(bh[d]), ALL).then_inc(S["mm1"], 1)
                        each(B + 2, 0, tk(kh[d]), tk(ah[d]), ALL).then_inc(S["mm1"], 1)
                        each(B + 3, 0, tk(bh[d]), lat(rh[d]), LATS)
                        each(B + 3, SEG, tk(kh[d]), lat(rh[d]), LATS).then_inc(S["mm1"], 1)

                    def pmm(lv):
                        for d in range(2):
                            if lv:
                                W(pe, "xadd", i, 10, 2 * (lv - 1) + d + 1)
                            else:
                                W(pe, "x0", i, 2, d + 1)
                            W(pe, "nlev", i, 10, 2 * lv + d + 1)
                            each(4 * d, 0, lambda c, h: nlev[d][h, lv % 2, c, :], ch(x[d]), ALL).then_inc(S["pmm"], 1)

                    def xmm(lv):
                        for d in range(2):
                            W(pe, "pcopy", i, 10, 2 * lv + d + 1)
                            if lv == 0:
                                W(pe, "mask", i, 4, 2 * d + 1)
                            if lv < 4:
                                each(4 * d + 1, 0, ch(xt[d]), ch(pp[d]), ALL)
                            each(4 * d + 2, 0, ch(pp[d]), ch(xt[d]), ALL).then_inc(S["xmm"], 1)

                    def tok(src, bank, former):
                        if former is not None:
                            W(pe, "tok", i, 7, former)
                        each(bank, 0, tk(src), eye, ALL).then_inc(S["tokmm"], 1)

                    W(pe, "mask", i, 4, 2)
                    tok(v0, 3, None)
                    W(pe, "mask", i, 4, 4)
                    tok(ah[0], 7, None)
                    pmm(0)
                    W(pe, "bars", i, 4, 4)
                    tok(ah[1], 3, 1)
                    tok(bbar[0], 7, 2)
                    xmm(0)
                    pmm(1)
                    tok(bbar[1], 3, 3)
                    tok(kbar[0], 7, 4)
                    xmm(1)
                    pmm(2)
                    tok(kbar[1], 3, 5)
                    xmm(2)
                    pmm(3)
                    W(pe, "tok", i, 7, 7)
                    for d in range(2):
                        each(4 * d + 3, 0, ch(nk[d]), ch(vt), ALL).then_inc(S["nkvmm"], 1)
                    xmm(3)
                    pmm(4)
                    xmm(4)
                    for d in range(2):
                        B = 4 * d
                        W(pe, "xadd", i, 10, 8 + d + 1)
                        W(pe, "nkv", i, 2, d + 1)
                        wide = lambda c, h: rhs[d][h, c, :, :].rearrange("p k t -> p (k t)")
                        each(B, 0, ch(xt[d]), wide, range(LAT), width=2 * LC)
                        each(B + 1, 0, ch(xt[d]), wide, LATS, width=2 * LC).then_inc(S["aumm"], 1)
                    for d in range(2):
                        B = 4 * d
                        W(pe, "au", i, 4, 4)
                        each(B + 2, 0, lambda c, h: au[d][h, c, 0, :], ch(bt[d]), ALL)
                        each(B + 3, 0, lambda c, h: au[d][h, c, 0, :], lambda c, h: rb[d][h, c - LAT, :], LATS).then_inc(S["gmm"], 1)
                    W(pe, "gt", i, 4, 4)
                    apart()
                    for k in range(NCH - 1):
                        for d in range(2):
                            c = ORDER[d][k]
                            if k:
                                W(pe, "scopy", i, 14, 2 * k)
                                apart()
                            for h in HALF:
                                o = g.ps[4 * d][h, k * LC:(k + 1) * LC]
                                pe.matmul(o, bt[d][h, c, :], au[d][h, c, 1, :], start=True, stop=False)
                                mm = pe.matmul(o, kt[d][h, c, :], vt[h, c, :], start=False, stop=(k == 0))
                                if k:
                                    mm = pe.matmul(o, gt[d][h, c, :], st[d][h, c, :], start=False, stop=True)
                            mm.then_inc(S["smm"], 1)
                    W(pe, "scopy", i, 14, 14)
                    apart()
                    for c in LATS:
                        for h in HALF:
                            o = g.ps[3][h, (c - LAT) * LC:(c - LAT + 1) * LC]
                            for d in range(2):
                                pe.matmul(o, rt[d][h, c - LAT, :], st[d][h, c, :], start=(d == 0), stop=False)
                                pe.matmul(o, rb[d][h, c - LAT, :], au[d][h, c, 1, :], start=False, stop=False)
                                mm = pe.matmul(o, rb[d][h, c, :], vt[h, c, :], start=False, stop=(d == 1))
                    mm.then_inc(S["ymm"], 1)
                    W(pe, "yn", i, 1, 1)
                    each(2, 0, lambda c, h: yn[h, c, :], eye, range(LAT)).then_inc(S["ytmm"], 1)
                    pe.wait_ge(S["pass_end"], i + 1)


def program(nc, a, out, stop=99, dump=None):
    with ExitStack() as ctx:
        g = setup(nc, ctx, a)
        g.eps = g.place(ctx, "eps", [P, 2])
        g.eps2 = g.place(ctx, "eps_kk", [P, 1])
        with nc.Block() as block:
            @block.vector
            def _(dve):
                dve.memset(g.eps[:, 0:1], EPS)
                dve.memset(g.eps[:, 1:2], RW_EPS)
                dve.memset(g.eps2[:, 0:1], 1.0e-12)
        stage_constants_and_modulation(g)
        if stop == 0:
            return dump and dump(g)
        if stop < 100:
            layer0(g, stop, dump)
        if stop <= 20:
            return
        nc.clear_and_free_semaphores(g.passing)
        nc.all_engine_barrier()
        layer1(g, out, stop, dump)


def layer0(g, stop, dump):
    nc = g.nc
    with ExitStack() as ctx:
        sb = lambda name, shape: g.place(ctx, name, shape)
        g.mixT = sb("mixT", [P, 16, T])
        g.z = sb("z_gate", [P, NT, D])
        g.dt = sb("dt_raw", [48, T])
        g.xc = sb("conv_out", [P, CT, T])
        g.hT = g.mixT[:, 0:8, :]
        with ExitStack() as ml:
            sb = lambda name, shape: g.place(ml, name, shape)
            g.o = sb("o_gate", [P, NT, D])
            g.v = sb("v_ext", [P, NT, ML_H, ML_DV + 1])
            g.qT = sb("qT", [P, ML_H, T])
            g.kT = sb("kT", [P, ML_H, T])
            g.ig, g.fg = sb("ig", [36, T]), sb("fg", [36, T])
            g.xn = g.o
            stage_norm(g, 0, 0, 0, ctx, False)
            if stop <= 1:
                return dump(g)
            with nc.sbuf_tensor("conv_in", [P, CT, T], F32) as g.xbc:
                stage_project(g)
            if stop <= 2:
                return dump(g)
            stage_mlstm(g)
            if stop <= 3:
                return dump(g)
        stage_ssd(g)
        if stop <= 4:
            return dump(g)
        stage_out(g, 0, g.a["ab_w_out"][0], 16, g.mixT, 0)
        if stop <= 5:
            return dump(g)
    stage_moe(g, 0, 0)
    if stop <= 6:
        return dump(g)


def layer1(g, out, stop, dump):
    stop = stop - 100 if stop > 100 else stop
    nc = g.nc
    with ExitStack() as ctx:
        sb = lambda name, shape: g.place(ctx, name, shape)
        g.yT = sb("rwkv_out", [P, DC, SEG])
        with ExitStack() as rw:
            sb = lambda name, shape: g.place(rw, name, shape)
            g.kT, g.vT, g.rT = sb("rw_k", [P, DC, T]), sb("rw_v", [P, DC, T]), sb("rw_r", [P, DC, SEG])
            g.tw, g.ta, g.tg = sb("rw_tanh", [P, T]), sb("rw_a_in", [64, T]), sb("rw_g_in", [P, 2, SEG])
            g.w2, g.a2, g.g2 = sb("rw_w2", [P, D]), sb("rw_a2", [64, D]), sb("rw_g2", [P, 2, D])
            with ExitStack() as pr:
                g.hT = g.place(pr, "rw_hT", [P, DC, T])
                with ExitStack() as nr:
                    g.xn = g.place(nr, "rw_xn", [P, NT, D])
                    stage_norm(g, 1, 0, 0, nr, False)
                stage_rwkv_project(g)
            if stop <= 21:
                return dump(g)
            with ExitStack() as mk:
                m = lambda name, shape: g.place(mk, name, shape)
                g.lev, g.i64, g.bones = m("level_masks", [P, 2, 6, LC]), m("eye64", [P, LC]), m("block_ones", [P, P])
                g.inc, g.strict = m("mask_inc", [P, 2, LC]), m("mask_strict", [P, 2, LC])
                stage_rwkv_masks(g)
                stage_rwkv(g)
        if stop <= 22:
            return dump(g)
        stage_out(g, 1, g.a["rw_wo"][0], DC, g.yT if False else LatOnly(g.yT), 2)
    if stop <= 23:
        return dump(g)
    stage_moe(g, 1, 2, out)
    if dump:
        dump(g)


class LatOnly:

    def __init__(self, x):
        self.x = x

    def __getitem__(self, at):
        p, k, t = at
        return self.x[p, k, t.start - SEG:t.stop - SEG]


_INS = ["x", "c", "ctx", "c_ctx", "ada_w", "ada_b", "norm_g", "router_w", "exp_w1", "exp_w3", "exp_w2",
        "ab_w_in", "ab_w_out", "ml_gate_b", "ml_norm_g", "ss_conv_w", "ss_conv_b", "ss_dt_bias", "ss_A_log", "ss_D", "ss_norm_g",
        "rw_mu", "rw_wr", "rw_wk", "rw_wv", "rw_wo", "rw_w0", "rw_w1", "rw_w2", "rw_a0", "rw_a1", "rw_a2", "rw_g1", "rw_g2",
        "rw_kk", "rw_ka", "rw_rk", "rw_lnx_g", "rw_lnx_b"]


def kernel(**inputs):
    import numpy as _np
    import concourse.bacc as _bacc
    from concourse import mybir as _mybir
    from concourse.bass_utils import run_bass_kernel_spmd as _run

    nc = _bacc.Bacc("TRN2", target_bir_lowering=False, num_devices=1)
    arrays, args = {}, {}
    for name in _INS:
        a = _np.ascontiguousarray(inputs[name])
        arrays[f"in_{name}"] = a
        args[name] = nc.dram_tensor(f"in_{name}", a.shape, _mybir.dt.from_np(a.dtype), kind="ExternalInput").ap()
    out = nc.dram_tensor("out_0", (1, SEG, D), F32, kind="ExternalOutput").ap()
    program(nc, args, out)
    r = _run(nc, [arrays], core_ids=[0])
    return r.results[0]["out_0"]
```

```python
from contextlib import ExitStack

import concourse.bass as bass
from concourse import mybir

F32 = mybir.dt.float32
U32 = mybir.dt.uint32
ALU = mybir.AluOpType
ACT = mybir.ActivationFunctionType
AX = mybir.AxisListType

P = 128
D = 1024
DC = D // P
SEG = 256
T = 2 * SEG
NT = T // P
NMOD = 6
ADA = NMOD * D
EPS = 1e-6
NEG = -1.0e30

ML_H, ML_DK, ML_DV = 4, 128, 256
SS_H, SS_HD, SS_G, SS_N = 16, 64, 2, 128
SS_HG = SS_H // SS_G
CONV = 1536
CT = CONV // P
GRID = 64
NE, FF, CAP = 16, 1408, 32
FC = FF // P
COL_Q, COL_K, COL_V, COL_O = 0, 512, 1024, 2048
COL_GATE = 3072
COL_Z = COL_GATE + 16
COL_X = COL_Z + 1024
COL_DT = COL_X + CONV

RW_H, RW_N = 16, 64
RW_EPS = 64e-5
RING_B = 6
LC = 64
NCH = T // LC


class Chain:

    def __init__(self, sem):
        self.sem, self.n, self.base = sem, 0, 0

    def do(self, ins):
        ins.then_inc(self.sem, 1)
        self.n += 1

    def join(self, eng):
        eng.wait_ge(self.sem, self.base + self.n)

    def step(self, eng, ins):
        self.do(ins)
        self.join(eng)

    def enter(self, i, per):
        self.start, self.n0 = (self.base, self.n)
        self.base, self.n = i * per + self.n, 0
        self.per = per

    def leave(self, passes):
        assert self.n == self.per, (self.n, self.per)
        self.base, self.n = 0, self.n0 + passes * self.per


class Env:
    pass


def setup(nc, ctx, a):
    g = Env()
    g.nc, g.a = nc, a
    g.names = 0
    g.rw_steps = 45

    g.passing = []

    def sem(name):
        g.names += 1
        g.passing.append(nc.alloc_semaphore(f"{name}_{g.names}"))
        return g.passing[-1]

    def place(scope, name, shape, dt=F32):
        g.names += 1
        return scope.enter_context(nc.sbuf_tensor(f"{name}_{g.names}", shape, dt))

    g.sem, g.place = sem, place
    g.dve, g.act, g.pool = Chain(sem("vector_done")), Chain(sem("scalar_done")), Chain(sem("gpsimd_done"))
    g.passing = []
    keep = lambda name, shape, dt=F32: ctx.enter_context(nc.sbuf_tensor(name, shape, dt))
    g.ident = keep("ident", [P, P])
    g.ones = keep("ones", [P, P])
    g.upper = keep("upper", [P, P])
    g.lower = keep("lower", [P, P])
    g.cols = keep("cols", [P, 512])
    g.x = keep("x_res", [P, NT, D])
    g.small = keep("small", [P, 64])
    g.ps = [ctx.enter_context(nc.psum_tensor(f"bank{i}", [P, 512], F32)) for i in range(8)]
    dram = lambda name, shape: nc.dram_tensor(name, shape, F32).ap()
    g.modraw = dram("mod_raw", [2, 2, ADA])
    g.modp = dram("mod_rows", [2, 2, ADA])
    g.rwk, g.rwv, g.rwr = dram("rwkv_k", [P, DC, T]), dram("rwkv_v", [P, DC, T]), dram("rwkv_r", [P, DC, SEG])
    return g


COL_MOD = (0, 96)
COL_P2, COL_P3, COL_P4 = 192, 304, 424


def mod_col(layer, stream, k, dc):
    return COL_MOD[layer] + stream * 48 + k * 8 + dc


def stage_constants_and_modulation(g):
    nc, a = g.nc, g.a
    HALF = ADA // 2
    RING = 4
    with ExitStack() as ctx:
        sb = lambda name, shape: g.place(ctx, name, shape)
        slab = sb("ada_slab", [P, RING, HALF])
        crow = sb("c_rows", [16, P])
        ccol = sb("c_cols", [P, 16])
        prow = [sb(f"param_rows{i}", [P, P]) for i in range(3)]
        mrow = sb("mod_evict", [66, 2, 2, 512])
        modr = sb("mod_r", [96, P])
        bias = sb("mod_bias", [96, 2, P])
        gains = sb("mod_gain", [96, 2, P])
        plus = sb("mod_plus", [96, P])
        ones16 = sb("ones16", [16, P])
        s_load, s_slab, s_used, s_mm = g.sem("rows_loaded"), [g.sem(f"slab{i}_loaded") for i in range(RING)], g.sem("slab_used"), g.sem("half_done")
        s_tr, s_trc, s_silu, s_const, s_evict = g.sem("transposed"), g.sem("tr_copied"), g.sem("silu_ready"), g.sem("consts_ready"), g.sem("half_evicted")
        s_raw, s_back, s_fin, s_set, s_rowout = [g.sem("raw_stored_even"), g.sem("raw_stored_odd")], g.sem("raw_back"), g.sem("mod_ready"), g.sem("fills_ready"), g.sem("mod_stored")
        s_one, s_x = g.sem("plus_placed"), g.sem("x_loaded")
        r2, r3, r4 = prow
        with nc.Block() as block:
            @block.sync
            def _(sp):
                sp.dma_start(crow[0:8, :], a["c"].rearrange("b (r p) -> (b r) p", p=P)).then_inc(s_load, 16)
                sp.dma_start(crow[8:16, :], a["c_ctx"].rearrange("(r p) -> r p", p=P)).then_inc(s_load, 16)
                at = 0
                for ap, n in ((a["rw_mu"].rearrange("o k (r p) -> (o k r) p", p=P), 48),
                              (a["rw_w0"].rearrange("o k (r p) -> (o k r) p", p=P), 16),
                              (a["rw_a0"].rearrange("o (r p) -> (o r) p", p=P), 8),
                              (a["rw_kk"].rearrange("o (r p) -> (o r) p", p=P), 8),
                              (a["rw_ka"].rearrange("o (r p) -> (o r) p", p=P), 8),
                              (a["rw_rk"].rearrange("o (r b) n -> (o r) (b n)", b=2), 8),
                              (a["rw_lnx_g"].rearrange("o (r p) -> (o r) p", p=P), 8),
                              (a["rw_lnx_b"].rearrange("o (r p) -> (o r) p", p=P), 8)):
                    sp.dma_start(r2[at:at + n, :], ap).then_inc(s_load, 16)
                    at += n
                sp.dma_start(r3[0:108, :], a["ss_conv_w"].rearrange("o i j (r p) -> (o i j r) p", p=P)).then_inc(s_load, 16)
                sp.dma_start(r3[108:120, :], a["ss_conv_b"].rearrange("o (r p) -> (o r) p", p=P)).then_inc(s_load, 16)
                sp.dma_start(r4[0:8, :], a["ml_norm_g"].rearrange("o (r p) -> (o r) p", p=P)).then_inc(s_load, 16)
                sp.dma_start(r4[8:16, :], a["ss_norm_g"].rearrange("o (r p) -> (o r) p", p=P)).then_inc(s_load, 16)
                sp.dma_start(r4[16:80, :], a["norm_g"].rearrange("l k (r p) -> (l k r) p", p=P)).then_inc(s_load, 16)
                n = 0
                for layer in range(2):
                    for half in range(2):
                        for dc in range(DC):
                            if n >= RING:
                                sp.wait_ge(s_used, n - RING + 1)
                            sp.dma_start(slab[:, n % RING, :],
                                         a["ada_w"][layer, dc * P:(dc + 1) * P, half * HALF:(half + 1) * HALF]
                                         ).then_inc(s_slab[n % RING], 16)
                            n += 1
                sp.dma_start(g.x[:, 0:2, :], a["ctx"].rearrange("b (t p) d -> p (b t) d", p=P)).then_inc(s_x, 16)
                sp.dma_start(g.x[:, 2:4, :], a["x"].rearrange("b (t p) d -> p (b t) d", p=P)).then_inc(s_x, 16)
                sp.wait_ge(s_x, 32)

            @block.gpsimd
            def _(pool):
                for m, v in ((g.ident, 0.0), (g.upper, 1.0), (g.lower, 1.0), (g.ones, 1.0)):
                    g.pool.do(pool.memset(m[:, :], v))
                g.pool.join(pool)
                pool.affine_select(out=g.ident[:, :], in_=g.ident[:, :], compare_op=ALU.not_equal, fill=1.0,
                                   base=0, pattern=[[-1, P]], channel_multiplier=1).then_inc(s_const, 1)
                pool.affine_select(out=g.upper[:, :], in_=g.upper[:, :], compare_op=ALU.is_ge, fill=0.0,
                                   base=0, pattern=[[1, P]], channel_multiplier=-1).then_inc(s_const, 1)
                pool.affine_select(out=g.lower[:, :], in_=g.lower[:, :], compare_op=ALU.is_ge, fill=0.0,
                                   base=0, pattern=[[-1, P]], channel_multiplier=1).then_inc(s_const, 1)

            @block.tensor
            def _(pe):
                pe.wait_ge(s_const, 1)
                pe.wait_ge(s_load, 16 * 15)
                pe.transpose(g.ps[4][:, 0:16], crow[:, :], g.ident[0:16, 0:16]).then_inc(s_tr, 1)
                pe.transpose(g.ps[5][:, 0:112], r2[0:112, :], g.ident[0:112, 0:112]).then_inc(s_tr, 1)
                pe.transpose(g.ps[6][:, 0:120], r3[0:120, :], g.ident[0:120, 0:120]).then_inc(s_tr, 1)
                pe.transpose(g.ps[7][:, 0:80], r4[0:80, :], g.ident[0:80, 0:80]).then_inc(s_tr, 1)
                pe.wait_ge(s_silu, 1)
                n = 0
                for h in range(4):
                    if h >= 2:
                        pe.wait_ge(s_evict, h - 1)
                    for dc in range(DC):
                        pe.wait_ge(s_slab[n % RING], 16 * (n // RING + 1))
                        for s in range(6):
                            j, b = s % 3, s // 3
                            mm = pe.matmul(g.ps[2 * (h % 2) + b][32 * j:32 * j + 2, :], ccol[:, dc::8],
                                           slab[:, n % RING, 512 * s:512 * s + 512],
                                           start=(dc == 0), stop=(dc == DC - 1))
                        mm.then_inc(s_used, 1)
                        n += 1
                for layer in range(2):
                    pe.wait_ge(s_fin, layer + 1)
                    pe.transpose(g.ps[4 + layer][:, 0:96], modr[:, :], g.ident[0:96, 0:96]).then_inc(s_tr, 1)

            @block.vector
            def _(dve):
                g.dve.do(dve.memset(gains[:, :, :], 1.0))
                g.dve.do(dve.memset(plus[:, :], 0.0))
                g.dve.do(dve.memset(ones16[:, :], 1.0))
                g.dve.join(dve)
                dve.memset(g.small[:, :], 0.0).then_inc(s_set, 1)
                dve.wait_ge(s_tr, 4)
                dve.tensor_copy(g.cols[:, COL_P2:COL_P2 + 112], g.ps[5][:, 0:112]).then_inc(s_trc, 1)
                dve.tensor_copy(g.cols[:, COL_P3:COL_P3 + 120], g.ps[6][:, 0:120]).then_inc(s_trc, 1)
                dve.tensor_copy(g.cols[:, COL_P4:COL_P4 + 80], g.ps[7][:, 0:80]).then_inc(s_trc, 1)
                for h in range(4):
                    dve.wait_ge(s_used, DC * (h + 1))
                    if h >= 2:
                        dve.wait_ge(s_raw[h % 2], 16 * 6)
                    for j in range(3):
                        for b in range(2):
                            cp = dve.tensor_copy(mrow[32 * j:32 * j + 2, h % 2, b, :], g.ps[2 * (h % 2) + b][32 * j:32 * j + 2, :])
                            g.dve.do(cp)
                    g.dve.join(dve)
                    dve.memset(g.small[:, 0:1], 0.0).then_inc(s_evict, 1)
                for layer in range(2):
                    dve.wait_ge(s_back, 16 * (layer + 1))
                    dve.wait_ge(s_one, 16 * 16)
                    if layer:
                        dve.wait_ge(s_tr, 5)
                    g.dve.step(dve, dve.tensor_tensor(modr[:, :], modr[:, :], bias[:, layer, :], ALU.add))
                    g.dve.step(dve, dve.tensor_tensor(modr[:, :], modr[:, :], plus[:, :], ALU.add))
                    dve.tensor_tensor(modr[:, :], modr[:, :], gains[:, layer, :], ALU.mult).then_inc(s_fin, 1)
                    dve.wait_ge(s_tr, 5 + layer)
                    dve.tensor_copy(g.cols[:, COL_MOD[layer]:COL_MOD[layer] + 96], g.ps[4 + layer][:, 0:96]).then_inc(s_trc, 1)

            @block.scalar
            def _(act):
                act.wait_ge(s_tr, 1)
                act.activation(ccol[:, :], g.ps[4][:, 0:16], ACT.Silu).then_inc(s_silu, 1)
                act.wait_ge(s_set, 1)
                for layer in range(2):
                    for st in range(2):
                        act.dma_start(bias[48 * st:48 * st + 48, layer, :],
                                      a["ada_b"][layer].rearrange("(r p) -> r p", p=P)).then_inc(s_one, 16)
                        for k, norm in ((1, 0), (4, 2)):
                            act.dma_start(gains[48 * st + 8 * k:48 * st + 8 * k + 16, layer, :],
                                          a["norm_g"][layer, norm:norm + 2].rearrange("k (r p) -> (k r) p", p=P)).then_inc(s_one, 16)
                for st in range(2):
                    for k in (1, 4):
                        act.dma_start(plus[48 * st + 8 * k:48 * st + 8 * k + 8, :], ones16[0:8, :]).then_inc(s_one, 16)
                for h in range(4):
                    act.wait_ge(s_evict, h + 1)
                    layer, half = h // 2, h % 2
                    for s in range(6):
                        j, b = s % 3, s // 3
                        c0 = half * HALF + 512 * s
                        act.dma_start(g.modraw[layer, :, c0:c0 + 512], mrow[32 * j:32 * j + 2, h % 2, b, :]).then_inc(s_raw[h % 2], 16)
                    if half:
                        act.wait_ge(s_raw[0], 16 * 6 * (layer + 1))
                        act.wait_ge(s_raw[1], 16 * 6 * (layer + 1))
                        if layer:
                            act.wait_ge(s_rowout, 16)
                            act.wait_ge(s_tr, 5)
                        act.dma_start(modr[:, :], g.modraw[layer].rearrange("s (r p) -> (s r) p", p=P)).then_inc(s_back, 16)
                        act.wait_ge(s_fin, layer + 1)
                        act.dma_start(g.modp[layer].rearrange("s (r p) -> (s r) p", p=P), modr[:, :]).then_inc(s_rowout, 16)
                act.wait_ge(s_rowout, 32)


def stage_norm(g, layer, which, t0, ctx):
    nc = g.nc
    nt = NT - t0
    with ExitStack() as own:
        sq = g.place(own, "norm_sq", [P, D])
        s_ss, s_root, s_xn, s_tp, s_ev = (g.sem(n) for n in ("squares_summed", "root_ready", "xn_ready", "xn_transposed", "hT_evicted"))
        ssq = g.small[:, 0:4]
        root = g.small[:, 4:8]
        rstd = g.small[:, 8:12]
        with nc.Block() as block:
            @block.scalar
            def _(act):
                for t in range(t0, NT):
                    if t > t0:
                        g.act.join(act)
                    g.act.do(act.activation(sq[:, :], g.x[:, t, :], ACT.Square, accum_out=ssq[:, t:t + 1]))
                g.act.join(act)
                act.activation(root[:, t0:NT], ssq[:, t0:NT], ACT.Sqrt, bias=g.eps[:, 0:1], scale=1.0 / D).then_inc(s_root, 1)
                n = 0
                for dc in range(DC):
                    act.wait_ge(s_tp, dc + 1)
                    for st, lo, hi in ((1, 0, 2 - t0), (0, 2 - t0, nt)):
                        if hi <= 0:
                            continue
                        lo = max(lo, 0)
                        col = mod_col(layer, st, which * 3 + 1, dc)
                        sh = mod_col(layer, st, which * 3, dc)
                        act.activation(g.hT[:, dc, (t0 + lo) * P:(t0 + hi) * P], g.ps[dc % 4][:, lo * P:hi * P],
                                       ACT.Identity, bias=g.cols[:, sh:sh + 1], scale=g.cols[:, col:col + 1]).then_inc(s_ev, 1)

            @block.vector
            def _(dve):
                dve.wait_ge(s_root, 1)
                g.dve.step(dve, dve.reciprocal(rstd[:, t0:NT], root[:, t0:NT]))
                for t in range(t0, NT):
                    dve.tensor_scalar(g.xn[:, t, :], g.x[:, t, :], rstd[:, t:t + 1], None, ALU.mult).then_inc(s_xn, 1)

            @block.tensor
            def _(pe):
                pe.wait_ge(s_xn, nt)
                segs = 2 if t0 == 0 else 1
                for dc in range(DC):
                    if dc >= 4:
                        pe.wait_ge(s_ev, segs * (dc - 3))
                    for t in range(nt):
                        mm = pe.transpose(g.ps[dc % 4][:, t * P:(t + 1) * P], g.xn[:, t0 + t, dc * P:(dc + 1) * P], g.ident[:, :])
                    mm.then_inc(s_tp, 1)


def stage_project(g):
    nc, a = g.nc, g.a
    RING = 2
    w = a["ab_w_in"]
    slabs = [("T", c, dst, t) for c, dst, t in ((COL_Q, g.qT, 0), (COL_K, g.kT, 0), (COL_X, g.xbc, 0), (COL_X + 512, g.xbc, 4), (COL_X + 1024, g.xbc, 8))]
    slabs += [("N", c, dst, t) for c, dst, t in ((COL_V, g.v, 0), (COL_V + 512, g.v, 1), (COL_O, g.o, 0), (COL_O + 512, g.o, 1), (COL_Z, g.z, 0), (COL_Z + 512, g.z, 1))]
    with ExitStack() as ctx:
        sb = lambda name, shape: g.place(ctx, name, shape)
        slab = sb("w_slab", [P, RING, DC, 512])
        wg = sb("w_gate_spread", [P, DC, 100])
        wd = sb("w_dt_spread", [P, DC, 48])
        s_w, s_small, s_spread = [g.sem(f"w_slab{i}") for i in range(RING)], g.sem("w_small"), g.sem("w_spread")
        s_mm, s_ev, s_slabfree, s_conv = g.sem("product_ready"), g.sem("product_out"), g.sem("slab_free"), g.sem("convolved")
        with nc.Block() as block:
            @block.sync
            def _(sp):
                for n, (_, c0, _, _) in enumerate(slabs):
                    if n >= RING:
                        sp.wait_ge(s_slabfree, n - RING + 1)
                    sp.dma_start(slab[:, n % RING, :, :], w[0, :, c0:c0 + 512].rearrange("(c p) n -> p c n", p=P)).then_inc(s_w[n % RING], 16)
                    if n == 1:
                        sp.wait_ge(s_spread, 1)
                        cols = lambda c0, m: w[0, :, c0:c0 + m].rearrange("(c p) n -> p c n", p=P)
                        for d in range(2):
                            for f in range(2):
                                sp.dma_start(wg[:, :, 64 * f + 32 * d:64 * f + 32 * d + 4], cols(COL_GATE + 8 * d + 4 * f, 4)).then_inc(s_small, 16)
                            sp.dma_start(wd[:, :, 32 * d:32 * d + 16], cols(COL_DT + 16 * d, 16)).then_inc(s_small, 16)

            @block.tensor
            def _(pe):
                k = 0
                def bank():
                    if k >= 8:
                        pe.wait_ge(s_ev, k - 7)
                    return g.ps[k % 8]
                for n, (kind, _, _, _) in enumerate(slabs):
                    pe.wait_ge(s_w[n % RING], 16 * (n // RING + 1))
                    for m in range(4):
                        ps = bank()
                        for dc in range(DC):
                            if kind == "T":
                                mm = pe.matmul(ps[:, :], slab[:, n % RING, dc, m * P:(m + 1) * P], g.hT[:, dc, :],
                                               start=(dc == 0), stop=(dc == DC - 1))
                            else:
                                mm = pe.matmul(ps[:, :], g.hT[:, dc, m * P:(m + 1) * P], slab[:, n % RING, dc, :],
                                               start=(dc == 0), stop=(dc == DC - 1))
                        if m == 3:
                            mm.then_inc(s_slabfree, 1)
                            pe.wait_ge(s_slabfree, n + 1)
                            pe.nop().then_inc(s_mm, 1)
                        else:
                            mm.then_inc(s_mm, 1)
                        k += 1
                pe.wait_ge(s_small, 96)
                for wt, m in ((wg, 100), (wd, 48)):
                    ps = bank()
                    for dc in range(DC):
                        mm = pe.matmul(ps[0:m, :], wt[:, dc, :], g.hT[:, dc, :], start=(dc == 0), stop=(dc == DC - 1))
                    mm.then_inc(s_mm, 1)
                    k += 1

            @block.gpsimd
            def _(pool):
                g.pool.do(pool.memset(wg[:, :, :], 0.0))
                g.pool.do(pool.memset(wd[:, :, :], 0.0))
                g.pool.do(pool.memset(g.v[:, :, :, ML_DV:ML_DV + 1], 1.0))
                g.pool.join(pool)
                pool.memset(g.small[:, 3:4], 0.0).then_inc(s_spread, 1)

            def evict(eng, copy, n, k, m):
                kind, _, dst, at = slabs[n]
                if kind == "T":
                    out = dst[:, at + m, :]
                elif dst is g.v:
                    out = dst[:, m, 2 * at:2 * at + 2, 0:ML_DV]
                else:
                    out = dst[:, m, 512 * at:512 * at + 512]
                src = g.ps[k % 8][:, :]
                if dst is g.v:
                    src = src.rearrange("p (h v) -> p h v", h=2)
                return copy(out, src, dst)

            n_t = 4 * sum(kind == "T" for kind, _, _, _ in slabs)

            @block.vector
            def _(dve):
                for k in range(0, n_t, 2):
                    n, m = k // 4, k % 4
                    dve.wait_ge(s_mm, k + 1)
                    if k:
                        dve.wait_ge(s_ev, k)
                    f = lambda o, i, dst: dve.tensor_scalar(o, i, ML_DK ** -0.5 if dst is g.kT else 1.0, None, ALU.mult)
                    evict(dve, f, n, k, m).then_inc(s_ev, 1)
                dve.wait_ge(s_ev, n_t)
                tap = lambda i, j, c: g.cols[:, COL_P3 + (3 * i + j) * CT + c:COL_P3 + (3 * i + j) * CT + c + 1]
                for c in range(CT):
                    g.dve.do(dve.tensor_scalar(g.xc[:, c, :], g.xbc[:, c, :], tap(1, 1, c),
                                               g.cols[:, COL_P3 + 108 + c:COL_P3 + 109 + c], ALU.mult, ALU.add))
                g.dve.join(dve)
                for j in (0, 2):
                    lo, hi = max(0, 1 - j), min(SEG, SEG + 1 - j)
                    for c in range(CT):
                        g.dve.do(dve.scalar_tensor_tensor(g.xc[:, c, lo:hi], g.xbc[:, c, lo + j - 1:hi + j - 1], tap(1, j, c),
                                                          g.xc[:, c, lo:hi], ALU.mult, ALU.add))
                    g.dve.join(dve)
                rows = SEG // GRID
                grid = lambda x, c: x[:, c, SEG:T].rearrange("p (r w) -> p r w", w=GRID)
                for i in range(3):
                    for j in range(3):
                        if (i, j) == (1, 1):
                            continue
                        r0, r1 = max(0, 1 - i), min(rows, rows + 1 - i)
                        lo, hi = max(0, 1 - j), min(GRID, GRID + 1 - j)
                        for c in range(CT):
                            acc = grid(g.xc, c)[:, r0:r1, lo:hi]
                            g.dve.do(dve.scalar_tensor_tensor(acc, grid(g.xbc, c)[:, r0 + i - 1:r1 + i - 1, lo + j - 1:hi + j - 1],
                                                              tap(i, j, c), acc, ALU.mult, ALU.add))
                        g.dve.join(dve)
                dve.memset(g.small[:, 0:1], 0.0).then_inc(s_conv, 1)

            @block.scalar
            def _(act):
                for k in range(4 * len(slabs)):
                    n, m = k // 4, k % 4
                    if k < n_t and k % 2 == 0:
                        continue
                    act.wait_ge(s_mm, k + 1)
                    act.wait_ge(s_ev, k)
                    f = lambda o, i, dst: act.activation(o, i, ACT.Copy, scale=ML_DK ** -0.5 if dst is g.kT else 1.0)
                    evict(act, f, n, k, m).then_inc(s_ev, 1)
                k = 4 * len(slabs)
                act.wait_ge(s_mm, k + 1)
                g.act.do(act.activation(g.ig[:, :], g.ps[k % 8][0:36, :], ACT.Copy))
                g.act.do(act.activation(g.fg[:, :], g.ps[k % 8][64:100, :], ACT.Copy))
                k += 1
                act.wait_ge(s_mm, k + 1)
                act.activation(g.dt[:, :], g.ps[k % 8][0:48, :], ACT.Copy)
                act.wait_ge(s_conv, 1)
                for c in range(CT):
                    act.activation(g.xc[:, c, :], g.xc[:, c, :], ACT.Silu)


def stage_mlstm(g):
    nc, a = g.nc, g.a
    ROW = lambda d, h: 32 * d + h
    FULL = [[[(1, 4)], [(2, 4)], [(3, 4)], []], [[(2, 4)], [(0, 1), (2, 4)], [], [(2, 3)]]]
    SEES = [[[0], [0, 1], [0, 1, 2], [0, 1, 2, 3]], [[0, 1], [1], [0, 1, 2, 3], [0, 1, 3]]]
    with ExitStack() as ctx:
        sb = lambda name, shape: g.place(ctx, name, shape)
        e = sb("ml_weights", [P, 2, NT, T])
        diag = sb("ml_diag", [P, 2, NT, P])
        mneg = sb("ml_mask", [P, 2, P])
        lf, b, gg, enm = (sb(f"ml_{n}", [36, T]) for n in ("lf", "b", "g", "enm"))
        negw = sb("ml_negm", [P, T])
        negm = negw[0:36, :]
        zero = sb("ml_zero", [36, T])
        gb = sb("ml_gate_bias", [36, 2])
        gcol, ecol = sb("ml_gcol", [P, NT, 36]), sb("ml_ecol", [P, NT, 36])
        den = sb("ml_den", [P, 2, 2])
        ssq = sb("ml_ssq", [P, 3, 16])
        ym = g.mixT[:, 8:16, :].rearrange("p a b -> p (a b)").rearrange("p (t d) -> p t d", t=NT)
        s_bias, s_zero, s_lin, s_ln, s_rows, s_cols, s_colsc = (g.sem(n) for n in ("gate_bias", "bias_zeroed", "forget_linear", "forget_log", "gate_rows", "gate_cols", "gate_cols_copied"))
        s_enm, s_score, s_bc, s_diag, s_exp, s_w, s_num, s_out = (g.sem(n) for n in ("enm", "scores", "m_spread", "diag_ready", "exp_ready", "weights_ready", "num_ready", "num_out"))
        s_sq, s_rt, s_sig, s_y, s_tp, s_ev = (g.sem(n) for n in ("ml_squares", "ml_root", "ml_sigmoid", "ml_y", "ml_transposed", "ml_evicted"))
        with nc.Block() as block:
            @block.sync
            def _(sp):
                sp.wait_ge(s_zero, 1)
                for d in range(2):
                    for f in range(2):
                        sp.dma_start(gb[32 * d:32 * d + 4, f:f + 1], a["ml_gate_b"][0, d, f, :].rearrange("(h o) -> h o", o=1)).then_inc(s_bias, 16)

            @block.vector
            def _(dve):
                g.dve.do(dve.memset(gb[:, :], 0.0))
                g.dve.do(dve.memset(zero[:, :], 0.0))
                g.dve.do(dve.tensor_scalar(mneg[:, 0, :], g.upper[:, :], 1.0, -NEG, ALU.subtract, ALU.mult))
                g.dve.do(dve.tensor_scalar(mneg[:, 1, :], g.lower[:, :], 1.0, -NEG, ALU.subtract, ALU.mult))
                g.dve.join(dve)
                dve.memset(g.small[:, 0:1], 0.0).then_inc(s_zero, 1)
                dve.wait_ge(s_bias, 64)
                g.dve.do(dve.tensor_scalar(g.ig[:, :], g.ig[:, :], gb[:, 0:1], None, ALU.add))
                g.dve.step(dve, dve.tensor_scalar(g.fg[:, :], g.fg[:, :], gb[:, 1:2], None, ALU.add))
                dve.tensor_scalar(lf[:, :], g.fg[:, :], 0.0, None, ALU.min).then_inc(s_lin, 1)
                dve.wait_ge(s_ln, 1)
                g.dve.step(dve, dve.tensor_tensor(lf[:, :], lf[:, :], enm[:, :], ALU.subtract))
                f, r = slice(0, 4), slice(32, 36)

                def scan(out, src, op):
                    other = (lambda x: x) if op == ALU.max else (lambda x: zero[:, :])
                    g.dve.do(dve.tensor_tensor_scan(out[f, :], src[f, :], src[f, :] if op == ALU.max else zero[f, :], 0.0, op, op))
                    back = lambda x, lo, hi: x[r, lo:hi][:, ::-1]
                    for lo, hi in ((0, SEG), (SEG, T)):
                        g.dve.step(dve, dve.tensor_tensor_scan(back(out, lo, hi), back(src, lo, hi), back(src if op == ALU.max else zero, lo, hi),
                                                               out[r, 0:1] if lo else 0.0, op, op))
                g.dve.do(dve.memset(b[:, :], 0.0))
                g.dve.do(dve.memset(negw[:, :], 0.0))
                g.dve.join(dve)
                scan(b, lf, ALU.add)
                g.dve.step(dve, dve.tensor_tensor(gg[:, :], g.ig[:, :], b[:, :], ALU.subtract))
                scan(negm, gg, ALU.max)
                g.dve.step(dve, dve.tensor_tensor(enm[:, :], b[:, :], negm[:, :], ALU.add))
                dve.tensor_scalar(negm[:, :], negm[:, :], -1.0, None, ALU.mult).then_inc(s_rows, 1)
                dve.wait_ge(s_cols, 4)
                dve.tensor_copy(gcol[:, :, :], g.ps[6][:, 0:144].rearrange("p (t r) -> p t r", t=NT)).then_inc(s_colsc, 1)
                dve.wait_ge(s_cols, 8)
                dve.tensor_copy(ecol[:, :, :], g.ps[7][:, 0:144].rearrange("p (t r) -> p t r", t=NT)).then_inc(s_colsc, 1)
                dve.wait_ge(s_colsc, 2)

                def diagonal(u):
                    h, d = u // 2, u % 2
                    dve.wait_ge(s_bc, u + 1)
                    if u >= 2:
                        dve.wait_ge(s_exp, u - 1)
                    for st in range(NT):
                        ins = dve.scalar_tensor_tensor(diag[:, d, st, :], g.ps[4 + d][:, st * P:(st + 1) * P],
                                                       gcol[:, st, ROW(d, h):ROW(d, h) + 1], mneg[:, d, :], ALU.add, ALU.add)
                    ins.then_inc(s_diag, 1)

                def weigh(u):
                    h, d = u // 2, u % 2
                    dve.wait_ge(s_exp, u + 1)
                    dve.wait_ge(s_score, h + 1)
                    for st in range(NT):
                        for lo, hi in [(st, st + 1)] + FULL[d][st]:
                            w = e[:, d, st, lo * P:hi * P]
                            ins = dve.tensor_tensor(w, g.ps[st][:, lo * P:hi * P], w, ALU.mult)
                            g.dve.do(ins)
                    g.dve.join(dve)
                    dve.memset(den[:, 0, 1:2], 0.0).then_inc(s_w, 1)

                def finish(u):
                    h, d = u // 2, u % 2
                    for jt in range(NT):
                        ps = g.ps[6 + jt % 2]
                        dve.wait_ge(s_num, NT * u + jt + 1)
                        c = ROW(d, h)
                        g.dve.step(dve, dve.tensor_scalar(den[:, 0, 0:1], ps[:, ML_DV:ML_DV + 1], ecol[:, jt, c:c + 1], None, ALU.max))
                        g.dve.step(dve, dve.scalar_tensor_tensor(den[:, 1, 0:1], ps[:, ML_DV:ML_DV + 1], -1.0, den[:, 0, 0:1], ALU.mult, ALU.max))
                        g.dve.step(dve, dve.reciprocal(den[:, 1, 1:2], den[:, 1, 0:1]))
                        y = ym[:, jt, h * ML_DV:(h + 1) * ML_DV]
                        if d == 0:
                            dve.tensor_scalar(y, ps[:, 0:ML_DV], den[:, 1, 1:2], None, ALU.mult).then_inc(s_out, 1)
                        else:
                            dve.scalar_tensor_tensor(y, ps[:, 0:ML_DV], den[:, 1, 1:2], y, ALU.mult, ALU.add).then_inc(s_out, 1)
                    dve.wait_ge(s_out, NT * (u + 1))

                diagonal(0)
                for u in range(2 * ML_H):
                    if u:
                        finish(u - 1)
                    if u + 1 < 2 * ML_H:
                        diagonal(u + 1)
                    weigh(u)
                finish(2 * ML_H - 1)
                dve.wait_ge(s_rt, 1)
                g.dve.step(dve, dve.reciprocal(ssq[:, 2, :], ssq[:, 1, :]))
                dve.wait_ge(s_sig, 1)
                for t in range(NT):
                    for h in range(ML_H):
                        y = ym[:, t, h * ML_DV:(h + 1) * ML_DV]
                        dve.scalar_tensor_tensor(y, y, ssq[:, 2, 4 * t + h:4 * t + h + 1], g.o[:, t, h * ML_DV:(h + 1) * ML_DV],
                                                 ALU.mult, ALU.mult).then_inc(s_y, 1)

            @block.scalar
            def _(act):
                act.wait_ge(s_lin, 1)
                g.act.step(act, act.activation(enm[:, :], g.fg[:, :], ACT.Abs))
                g.act.step(act, act.activation(enm[:, :], enm[:, :], ACT.Exp, scale=-1.0))
                act.activation(enm[:, :], enm[:, :], ACT.Ln, bias=1.0).then_inc(s_ln, 1)
                act.wait_ge(s_rows, 1)
                act.activation(enm[:, :], enm[:, :], ACT.Exp, scale=-1.0).then_inc(s_enm, 1)
                act.wait_ge(s_colsc, 2)
                for u in range(2 * ML_H):
                    h, d = u // 2, u % 2
                    act.wait_ge(s_diag, u + 1)
                    if u >= 2:
                        act.wait_ge(s_num, NT * (u - 1))
                    for st in range(NT):
                        g.act.do(act.activation(e[:, d, st, st * P:(st + 1) * P], diag[:, d, st, :], ACT.Exp))
                        for lo, hi in FULL[d][st]:
                            g.act.do(act.activation(e[:, d, st, lo * P:hi * P], g.ps[4 + d][:, lo * P:hi * P], ACT.Exp,
                                                    bias=gcol[:, st, ROW(d, h):ROW(d, h) + 1]))
                    g.act.join(act)
                    act.activation(g.small[:, 1:2], g.small[:, 2:3], ACT.Copy).then_inc(s_exp, 1)
                act.wait_ge(s_out, NT * 2 * ML_H)
                act.wait_ge(s_w, 2 * ML_H)
                for t in range(NT):
                    for h in range(ML_H):
                        g.act.do(act.activation(e[:, h % 2, t, 0:ML_DV], ym[:, t, h * ML_DV:(h + 1) * ML_DV], ACT.Square,
                                                accum_out=ssq[:, 0, 4 * t + h:4 * t + h + 1]))
                        if h % 2:
                            g.act.join(act)
                act.activation(ssq[:, 1, :], ssq[:, 0, :], ACT.Sqrt, bias=g.eps[:, 0:1], scale=1.0 / ML_DV).then_inc(s_rt, 1)
                act.activation(g.o[:, :, :], g.o[:, :, :], ACT.Sigmoid).then_inc(s_sig, 1)
                for c in range(DC):
                    act.wait_ge(s_tp, c + 1)
                    act.activation(g.mixT[:, c, :], g.ps[c % 4][:, :], ACT.Copy, scale=g.cols[:, COL_P4 + c:COL_P4 + c + 1]).then_inc(s_ev, 1)

            @block.tensor
            def _(pe):
                pe.wait_ge(s_rows, 1)
                for t in range(NT):
                    pe.transpose(g.ps[6][:, 36 * t:36 * t + 36], gg[:, t * P:(t + 1) * P], g.ident[0:36, 0:36]).then_inc(s_cols, 1)
                pe.wait_ge(s_enm, 1)
                for t in range(NT):
                    pe.transpose(g.ps[7][:, 36 * t:36 * t + 36], enm[:, t * P:(t + 1) * P], g.ident[0:36, 0:36]).then_inc(s_cols, 1)
                pe.wait_ge(s_colsc, 2)

                def spread(u):
                    h, d = u // 2, u % 2
                    if u >= 2:
                        pe.wait_ge(s_exp, u - 1)
                    r = ROW(d, h)
                    pe.matmul(g.ps[4 + d][:, :], g.ident[:, r:r + 1].broadcast_to([P, P]), negw[:, :], start=True, stop=True).then_inc(s_bc, 1)

                def scores(h):
                    if h:
                        pe.wait_ge(s_w, 2 * h)
                    for st in range(NT):
                        lo = 0 if st < 2 else SEG
                        mm = pe.matmul(g.ps[st][:, lo:T], g.kT[:, h, st * P:(st + 1) * P], g.qT[:, h, lo:T], start=True, stop=True)
                    mm.then_inc(s_score, 1)

                def numerators(u):
                    h, d = u // 2, u % 2
                    pe.wait_ge(s_w, u + 1)
                    for jt in range(NT):
                        n = NT * u + jt
                        if n >= 2:
                            pe.wait_ge(s_out, n - 1)
                        for st in SEES[d][jt]:
                            mm = pe.matmul(g.ps[6 + jt % 2][:, 0:ML_DV + 1], e[:, d, st, jt * P:(jt + 1) * P], g.v[:, st, h, :],
                                           start=(st == SEES[d][jt][0]), stop=(st == SEES[d][jt][-1]))
                        mm.then_inc(s_num, 1)

                spread(0)
                scores(0)
                for u in range(2 * ML_H):
                    if u + 1 < 2 * ML_H:
                        spread(u + 1)
                    if u % 2 == 1 and u + 1 < 2 * ML_H:
                        scores((u + 1) // 2)
                    numerators(u)
                for c in range(DC):
                    pe.wait_ge(s_y, NT * ML_H)
                    if c >= 4:
                        pe.wait_ge(s_ev, c - 3)
                    for t in range(NT):
                        mm = pe.transpose(g.ps[c % 4][:, t * P:(t + 1) * P], ym[:, t, c * P:(c + 1) * P], g.ident[:, :])
                    mm.then_inc(s_tp, 1)


def stage_ssd(g):
    nc, a = g.nc, g.a
    HW = SS_HG * SS_HD
    ROW = lambda d, h: 32 * d + h
    ORDER = ((0, 1, 2, 3), (1, 0, 3, 2))
    UNITS = [(d, h) for d in range(2) for h in range(SS_H)]
    with ExitStack() as ctx:
        sb = lambda name, shape: g.place(ctx, name, shape)
        xs = sb("ss_x", [P, NT, D])
        xd = sb("ss_xdt", [P, 2, NT, D])
        ys = sb("ss_y", [P, NT, D])
        bt = sb("ss_b", [P, NT, SS_G * SS_N])
        gm = sb("ss_gmask", [P, 2, SS_G, NT, P])
        e = sb("ss_exp", [P, 2, NT, P])
        w = sb("ss_w", [P, 2, NT, P])
        wend, one, res = (sb(f"ss_{n}", [48, T]) for n in ("wend", "t1", "t2"))
        acw = sb("ss_acum", [P, T])
        ac = acw[0:48, :]
        accol, dtcol, wcol, einc, eae = (sb(f"ss_{n}", [P, NT, 48]) for n in ("accol", "dtcol", "wcol", "einc", "eae"))
        aer = sb("ss_aend", [48, NT])
        bd = sb("ss_aend_diag", [48, NT, 48])
        par = sb("ss_par", [48, 4])
        dsk = sb("ss_dskip", [P, SS_H])
        hst = sb("ss_state", [P, SS_G, HW])
        tmp = sb("ss_tmp", [P, HW])
        ssq = sb("ss_ssq", [P, 3, 8])
        (s_par, s_z, s_abs, s_u, s_ln, s_wend, s_rows, s_col, s_colc, s_einc, s_ae) = (g.sem("ss_" + n) for n in (
            "params", "zeroed", "abs", "one_plus", "log", "wexp", "rows", "cols", "cols_out", "exps", "aend_spread"))
        (s_tp, s_tpv, s_tpa, s_g, s_gm, s_xd, s_yd, s_bc, s_df, s_ex, s_w, s_in, s_out) = (g.sem("ss_" + n) for n in (
            "x_transposed", "x_out_v", "x_out_a", "g_ready", "g_masked", "xdt", "y_init", "acum_spread", "diff", "exp", "weights", "intra", "intra_out"))
        (s_xp, s_loc, s_int, s_h, s_ya, s_silu, s_u2, s_sq, s_n, s_t2, s_e2) = (g.sem("ss_" + n) for n in (
            "xp", "local_state", "inter", "state", "inter_added", "silu", "gated", "squares", "normed", "y_transposed", "y_evicted"))
        with nc.Block() as block:
            @block.sync
            def _(sp):
                sp.wait_ge(s_z, 1)
                for d in range(2):
                    for k, n in enumerate(("ss_dt_bias", "ss_A_log")):
                        sp.dma_start(par[32 * d:32 * d + 16, k:k + 1], a[n][0, d, :].rearrange("(h o) -> h o", o=1)).then_inc(s_par, 16)
                sp.dma_start(dsk[:, :], a["ss_D"].broadcast_to([P, SS_H])).then_inc(s_par, 16)

            @block.vector
            def _(dve):
                dv = g.dve
                dv.do(dve.memset(par[:, :], 0.0))
                dv.do(dve.memset(acw[:, :], 0.0))
                dv.do(dve.memset(aer[:, :], 0.0))
                dv.join(dve)
                dve.memset(g.small[:, 0:1], 0.0).then_inc(s_z, 1)
                dve.wait_ge(s_par, 80)
                dve.tensor_scalar(g.dt[:, :], g.dt[:, :], par[:, 0:1], None, ALU.add).then_inc(s_abs, 1)
                dve.wait_ge(s_u, 1)
                dv.step(dve, dve.tensor_scalar(res[:, :], one[:, :], 1.0, None, ALU.add))
                dve.tensor_scalar(wend[:, :], res[:, :], 1.0, None, ALU.subtract).then_inc(s_u, 1)
                dve.wait_ge(s_u, 2)
                dve.wait_ge(s_ln, 1)
                dv.step(dve, dve.tensor_tensor(res[:, :], res[:, :], one[:, :], ALU.mult))
                dv.step(dve, dve.scalar_tensor_tensor(one[:, :], wend[:, :], 0.0, one[:, :], ALU.is_equal, ALU.mult))
                dv.step(dve, dve.tensor_scalar(wend[:, :], wend[:, :], 1.0e-30, None, ALU.max))
                dv.step(dve, dve.reciprocal(wend[:, :], wend[:, :]))
                dv.step(dve, dve.tensor_tensor(res[:, :], res[:, :], wend[:, :], ALU.mult))
                dv.step(dve, dve.tensor_tensor(res[:, :], res[:, :], one[:, :], ALU.add))
                dv.step(dve, dve.scalar_tensor_tensor(g.dt[:, :], g.dt[:, :], 0.0, res[:, :], ALU.max, ALU.add))
                dv.step(dve, dve.tensor_scalar(res[:, :], g.dt[:, :], par[:, 2:3], -1.0, ALU.mult, ALU.mult))
                dv.step(dve, dve.memset(one[:, :], 1.0))
                dv.do(dve.memset(one[0:16, 0::P], 0.0))
                dv.do(dve.memset(one[32:48, P - 1::P], 0.0))
                dv.join(dve)
                dv.do(dve.tensor_tensor_scan(ac[0:16, :], one[0:16, :], res[0:16, :], 0.0, ALU.mult, ALU.add))
                dv.do(dve.tensor_tensor_scan(ac[32:48, ::-1], one[32:48, ::-1], res[32:48, ::-1], 0.0, ALU.mult, ALU.add))
                dv.join(dve)
                dv.do(dve.tensor_copy(aer[0:16, :], ac[0:16, P - 1::P]))
                dv.do(dve.tensor_copy(aer[32:48, :], ac[32:48, 0::P]))
                dv.join(dve)
                for c in range(NT):
                    dv.do(dve.tensor_scalar(wend[:, c * P:(c + 1) * P], ac[:, c * P:(c + 1) * P], aer[:, c:c + 1], None, ALU.subtract))
                dv.join(dve)
                dve.tensor_tensor(bd[:, :, :], g.ident[0:48, 0:48].rearrange("p (o r) -> p o r", o=1).broadcast_to([48, NT, 48]),
                                  aer[:, :].rearrange("p (c o) -> p c o", o=1).broadcast_to([48, NT, 48]), ALU.mult).then_inc(s_rows, 1)
                for gr in range(SS_G):
                    dve.wait_ge(s_g, gr + 1)
                    for d, m in enumerate((g.upper, g.lower)):
                        dve.tensor_tensor(gm[:, d, gr, :, :], g.ps[gr][:, :].rearrange("p (c j) -> p c j", c=NT),
                                          m[:, :].rearrange("p (o j) -> p o j", o=1).broadcast_to([P, NT, P]), ALU.mult).then_inc(s_gm, 1)
                for k in range(0, 10, 2):
                    dve.wait_ge(s_tp, k + 1)
                    out = xs[:, k // 2, 0:512] if k < 8 else bt[:, 0:2, :]
                    dve.tensor_copy(out, g.ps[2 + k % 2][:, :] if k < 8 else g.ps[2][:, :].rearrange("p (c n) -> p c n", c=2)).then_inc(s_tpv, 1)
                for k, (dst, bank) in enumerate(((accol, 5), (dtcol, 6), (wcol, 7))):
                    dve.wait_ge(s_col, k + 1)
                    dve.tensor_copy(dst[:, :, :], g.ps[bank][:, 0:192].rearrange("p (c r) -> p c r", c=NT)).then_inc(s_colc, 1)
                dve.wait_ge(s_colc, 3)
                dve.wait_ge(s_tpv, 5)
                dve.wait_ge(s_tpa, 5)
                for t in range(NT):
                    dve.tensor_tensor(ys[:, t, :].rearrange("p (h k) -> p h k", h=SS_H), xs[:, t, :].rearrange("p (h k) -> p h k", h=SS_H),
                                      dsk[:, :].rearrange("p (h o) -> p h o", o=1).broadcast_to([P, SS_H, SS_HD]), ALU.mult).then_inc(s_yd, 1)
                dve.wait_ge(s_yd, NT)

                def difference(u):
                    d, h = UNITS[u]
                    dve.wait_ge(s_bc, u + 1)
                    if u >= 2:
                        dve.wait_ge(s_w, u - 1)
                    for c in range(NT):
                        ins = dve.tensor_scalar(e[:, u % 2, c, :], g.ps[u % 2][:, c * P:(c + 1) * P],
                                                accol[:, c, ROW(d, h):ROW(d, h) + 1], 0.0, ALU.subtract, ALU.min)
                    ins.then_inc(s_df, 1)

                def add_intra(u):
                    d, h = UNITS[u]
                    dve.wait_ge(s_in, u + 1)
                    if u >= SS_H:
                        dve.wait_ge(s_out, u - SS_H + 1)
                    y = ys[:, :, h * SS_HD:(h + 1) * SS_HD]
                    dve.tensor_tensor(y, g.ps[2 + u % 2][:, 0:NT * SS_HD].rearrange("p (c k) -> p c k", c=NT), y, ALU.add).then_inc(s_out, 1)

                for u in range(len(UNITS)):
                    difference(u)
                    if u:
                        add_intra(u - 1)
                add_intra(len(UNITS) - 1)
                dve.wait_ge(s_out, len(UNITS))
                heads = lambda x: x.rearrange("p (h k) -> p h k", h=SS_HG)
                spread = lambda x, c, d, gr: x[:, c, ROW(d, SS_HG * gr):ROW(d, SS_HG * gr) + SS_HG].rearrange("p (h o) -> p h o", o=1).broadcast_to([P, SS_HG, SS_HD])
                for d in range(2):
                    for k, c in enumerate(ORDER[d]):
                        n = 4 * d + k
                        if k < 3:
                            dve.wait_ge(s_loc, 3 * d + k + 1)
                            if k:
                                dve.wait_ge(s_int, 3 * d + k)
                                for gr in range(SS_G):
                                    dv.do(dve.tensor_tensor(heads(hst[:, gr, :]), heads(hst[:, gr, :]), spread(eae, c, d, gr), ALU.mult))
                                dv.join(dve)
                                for gr in range(SS_G):
                                    dv.do(dve.tensor_tensor(hst[:, gr, :], hst[:, gr, :], g.ps[4 + gr][:, :], ALU.add))
                            else:
                                if d:
                                    dve.wait_ge(s_int, 3)
                                for gr in range(SS_G):
                                    dv.do(dve.tensor_copy(hst[:, gr, :], g.ps[4 + gr][:, :]))
                            dv.join(dve)
                            dve.memset(g.small[:, 0:1], 0.0).then_inc(s_h, 1)
                        if k:
                            dve.wait_ge(s_int, 3 * d + k)
                            for gr in range(SS_G):
                                dv.step(dve, dve.tensor_tensor(heads(tmp[:, :]), heads(g.ps[6 + gr][:, :]), spread(einc, c, d, gr), ALU.mult))
                                y = ys[:, c, gr * HW:(gr + 1) * HW]
                                dv.step(dve, dve.tensor_tensor(y, tmp[:, :], y, ALU.add))
                            dve.memset(g.small[:, 0:1], 0.0).then_inc(s_ya, 1)
                dve.wait_ge(s_silu, 1)
                for t in range(NT):
                    dve.tensor_tensor(ys[:, t, :], ys[:, t, :], g.z[:, t, :], ALU.mult).then_inc(s_u2, 1)
                dve.wait_ge(s_sq, 1)
                dv.step(dve, dve.reciprocal(ssq[:, 2, :], ssq[:, 1, :]))
                for t in range(NT):
                    for gr in range(SS_G):
                        y = ys[:, t, gr * HW:(gr + 1) * HW]
                        dve.tensor_scalar(y, y, ssq[:, 2, 2 * t + gr:2 * t + gr + 1], None, ALU.mult).then_inc(s_n, 1)

            @block.scalar
            def _(act):
                ac_ = g.act
                act.wait_ge(s_abs, 1)
                ac_.step(act, act.activation(one[:, :], g.dt[:, :], ACT.Abs))
                act.activation(one[:, :], one[:, :], ACT.Exp, scale=-1.0).then_inc(s_u, 1)
                ac_.step(act, act.activation(par[:, 2:3], par[:, 1:2], ACT.Exp))
                act.wait_ge(s_u, 2)
                act.activation(res[:, :], res[:, :], ACT.Ln).then_inc(s_ln, 1)
                for k in range(1, 10, 2):
                    act.wait_ge(s_tp, k + 1)
                    out = xs[:, k // 2, 512:1024] if k < 8 else bt[:, 2:4, :]
                    act.activation(out, g.ps[3][:, :] if k < 8 else g.ps[3][:, :].rearrange("p (c n) -> p c n", c=2), ACT.Copy).then_inc(s_tpa, 1)
                act.wait_ge(s_rows, 1)
                act.activation(wend[:, :], wend[:, :], ACT.Exp, scale=-1.0).then_inc(s_wend, 1)
                act.wait_ge(s_colc, 1)
                act.activation(einc[:, :, :], accol[:, :, :], ACT.Exp).then_inc(s_einc, 1)
                act.wait_ge(s_ae, 1)
                act.activation(eae[:, :, :], g.ps[4][:, 0:192].rearrange("p (c r) -> p c r", c=NT), ACT.Exp).then_inc(s_einc, 1)
                for u in range(len(UNITS)):
                    act.wait_ge(s_df, u + 1)
                    act.activation(e[:, u % 2, :, :], e[:, u % 2, :, :], ACT.Exp).then_inc(s_ex, 1)
                act.activation(g.z[:, :, :], g.z[:, :, :], ACT.Silu).then_inc(s_silu, 1)
                act.wait_ge(s_in, len(UNITS))
                for t in range(NT):
                    act.wait_ge(s_u2, t + 1)
                    for gr in range(SS_G):
                        if t or gr:
                            ac_.join(act)
                        ac_.do(act.activation(e[:, 0, :, :].rearrange("p c j -> p (c j)"), ys[:, t, gr * HW:(gr + 1) * HW], ACT.Square,
                                              accum_out=ssq[:, 0, 2 * t + gr:2 * t + gr + 1]))
                ac_.join(act)
                act.activation(ssq[:, 1, :], ssq[:, 0, :], ACT.Sqrt, bias=g.eps[:, 0:1], scale=1.0 / HW).then_inc(s_sq, 1)
                for c in range(DC):
                    act.wait_ge(s_t2, c + 1)
                    act.activation(g.mixT[:, 8 + c, :], g.ps[c % 4][:, :], ACT.Copy, scale=g.cols[:, COL_P4 + 8 + c:COL_P4 + 9 + c]).then_inc(s_e2, 1)

            @block.gpsimd
            def _(pool):
                hd = lambda x: x.rearrange("p (h k) -> p h k", h=SS_H)
                sp_ = lambda x, c, d: x[:, c, 32 * d:32 * d + SS_H].rearrange("p (h o) -> p h o", o=1).broadcast_to([P, SS_H, SS_HD])
                pool.wait_ge(s_colc, 3)
                pool.wait_ge(s_tpv, 5)
                pool.wait_ge(s_tpa, 5)
                for d in range(2):
                    for t in range(NT):
                        pool.tensor_tensor(hd(xd[:, d, t, :]), hd(xs[:, t, :]), sp_(dtcol, t, d), ALU.mult).then_inc(s_xd, 1)
                pool.wait_ge(s_gm, 4)
                for u, (d, h) in enumerate(UNITS):
                    pool.wait_ge(s_ex, u + 1)
                    if u >= 2:
                        pool.wait_ge(s_in, u - 1)
                    pool.tensor_tensor(w[:, u % 2, :, :], e[:, u % 2, :, :], gm[:, d, h // SS_HG, :, :], ALU.mult).then_inc(s_w, 1)
                    if u < 8 and u % 2:
                        if u == 1:
                            pool.wait_ge(s_yd, NT)
                            pool.wait_ge(s_xd, 2 * NT)
                        t = u // 2
                        pool.tensor_tensor(hd(xs[:, t, :]), hd(xd[:, 0, t, :]), sp_(wcol, t, 0), ALU.mult).then_inc(s_xp, 1)
                pool.wait_ge(s_loc, 3)
                pool.wait_ge(s_xp, NT)
                for t in range(NT):
                    pool.tensor_tensor(hd(xs[:, t, :]), hd(xd[:, 1, t, :]), sp_(wcol, t, 1), ALU.mult).then_inc(s_xp, 1)

            @block.tensor
            def _(pe):
                for gr in range(SS_G):
                    for c in range(NT):
                        mm = pe.matmul(g.ps[gr][:, c * P:(c + 1) * P], g.xc[:, 8 + gr, c * P:(c + 1) * P], g.xc[:, 10 + gr, c * P:(c + 1) * P], start=True, stop=True)
                    mm.then_inc(s_g, 1)
                for k in range(10):
                    if k >= 2:
                        pe.wait_ge(s_tpa if k % 2 else s_tpv, k // 2)
                    for i in range(4):
                        if k < 8:
                            src = g.xc[:, 4 * (k % 2) + i, (k // 2) * P:(k // 2 + 1) * P]
                        else:
                            c = 2 * (k - 8) + i // 2
                            src = g.xc[:, 8 + i % 2, c * P:(c + 1) * P]
                        mm = pe.transpose(g.ps[2 + k % 2][:, i * P:(i + 1) * P], src, g.ident[:, :])
                    mm.then_inc(s_tp, 1)
                pe.wait_ge(s_rows, 1)
                cols = lambda bank, src: [pe.transpose(g.ps[bank][:, 48 * c:48 * c + 48], src[:, c * P:(c + 1) * P], g.ident[0:48, 0:48]) for c in range(NT)][-1]
                cols(5, ac).then_inc(s_col, 1)
                cols(6, g.dt).then_inc(s_col, 1)
                pe.matmul(g.ps[4][:, 0:192], g.ones[0:48, :], bd[:, :, :].rearrange("p c r -> p (c r)"), start=True, stop=True).then_inc(s_ae, 1)
                pe.wait_ge(s_wend, 1)
                cols(7, wend).then_inc(s_col, 1)

                def spread(u):
                    d, h = UNITS[u]
                    if u < 2:
                        pe.wait_ge(s_gm, 4)
                    else:
                        pe.wait_ge(s_df, u - 1)
                    r = ROW(d, h)
                    pe.matmul(g.ps[u % 2][:, :], g.ident[:, r:r + 1].broadcast_to([P, P]), acw[:, :], start=True, stop=True).then_inc(s_bc, 1)

                pe.wait_ge(s_tpv, 5)
                pe.wait_ge(s_tpa, 5)
                spread(0)
                for u, (d, h) in enumerate(UNITS):
                    if u + 1 < len(UNITS):
                        spread(u + 1)
                    pe.wait_ge(s_w, u + 1)
                    if h == 0:
                        pe.wait_ge(s_xd, NT * (d + 1))
                    if u >= 2:
                        pe.wait_ge(s_out, u - 1)
                    for c in range(NT):
                        mm = pe.matmul(g.ps[2 + u % 2][:, c * SS_HD:(c + 1) * SS_HD], w[:, u % 2, c, :], xd[:, d, c, h * SS_HD:(h + 1) * SS_HD], start=True, stop=True)
                    mm.then_inc(s_in, 1)
                pe.wait_ge(s_einc, 2)
                for d in range(2):
                    pe.wait_ge(s_xp, NT * (d + 1))
                    for k, c in enumerate(ORDER[d]):
                        if k:
                            pe.wait_ge(s_h, 3 * d + k)
                            if 3 * d + k >= 2:
                                pe.wait_ge(s_ya, 3 * d + k - 1)
                            for gr in range(SS_G):
                                mm = pe.matmul(g.ps[6 + gr][:, :], g.xc[:, 10 + gr, c * P:(c + 1) * P], hst[:, gr, :], start=True, stop=True)
                            mm.then_inc(s_int, 1)
                        if k < 3:
                            if 3 * d + k:
                                pe.wait_ge(s_h, 3 * d + k)
                            for gr in range(SS_G):
                                mm = pe.matmul(g.ps[4 + gr][:, :], bt[:, c, gr * SS_N:(gr + 1) * SS_N], xs[:, c, gr * HW:(gr + 1) * HW], start=True, stop=True)
                            mm.then_inc(s_loc, 1)
                pe.wait_ge(s_n, 8)
                for c in range(DC):
                    if c >= 4:
                        pe.wait_ge(s_e2, c - 3)
                    for t in range(NT):
                        mm = pe.transpose(g.ps[c % 4][:, t * P:(t + 1) * P], ys[:, t, c * P:(c + 1) * P], g.ident[:, :])
                    mm.then_inc(s_t2, 1)


class Tail:

    def __init__(self, g, ctx, layer, which, t0, tmp=None, gain=None):
        self.g, self.layer, self.which, self.t0 = g, layer, which, t0
        sb = lambda name, shape: g.place(ctx, name, shape)
        self.gain = gain if gain is not None else sb("tail_gain", [P, 2, D])
        self.tmp = sb("tail_tmp", [P, 2, 512]) if tmp is None else tmp
        self.ssq = sb("tail_ssq", [P, 4, 8])
        (self.s_gain, self.s_ready, self.s_sq, self.s_sum, self.s_root, self.s_tmp, self.s_add) = (g.sem("tail_" + n) for n in (
            "gain_loaded", "product_ready", "squared", "summed", "root", "scaled", "added"))

    def load(self, eng):
        for st in range(2):
            if st == 1 and self.t0:
                continue
            eng.dma_start(self.gain[:, st, :], self.g.modp[self.layer, st:st + 1, self.which * D:(self.which + 1) * D].broadcast_to([P, D])).then_inc(self.s_gain, 16)

    def scalar(self, act):
        g, t0 = self.g, self.t0
        for t in range(t0, NT):
            act.wait_ge(self.s_ready, t - t0 + 1)
            for h in range(2):
                if t > t0 or h:
                    g.act.join(act)
                g.act.do(act.activation(self.tmp[:, 0, :], g.ps[2 * (t - t0) + h][:, :], ACT.Square, accum_out=self.ssq[:, 0, 2 * t + h:2 * t + h + 1]))
        g.act.join(act)
        act.activation(self.ssq[:, 1, 0:1], self.ssq[:, 0, 2 * t0:2 * t0 + 1], ACT.Copy).then_inc(self.s_sq, 1)
        act.wait_ge(self.s_sum, 1)
        act.activation(self.ssq[:, 2, t0:NT], self.ssq[:, 1, t0:NT], ACT.Sqrt, bias=g.eps[:, 0:1], scale=1.0 / D).then_inc(self.s_root, 1)

    def vector(self, dve):
        g, t0 = self.g, self.t0
        dve.wait_ge(self.s_sq, 1)
        halves = self.ssq[:, 0, :].rearrange("p (t h) -> p t h", h=2)
        dve.tensor_tensor(self.ssq[:, 1, t0:NT], halves[:, t0:NT, 0], halves[:, t0:NT, 1], ALU.add).then_inc(self.s_sum, 1)
        dve.wait_ge(self.s_root, 1)
        g.dve.step(dve, dve.reciprocal(self.ssq[:, 3, t0:NT], self.ssq[:, 2, t0:NT]))
        dve.wait_ge(self.s_gain, 16 * (1 if t0 else 2))
        n = 0
        for t in range(t0, NT):
            for h in range(2):
                if n >= 2:
                    dve.wait_ge(self.s_add, n - 1)
                dve.scalar_tensor_tensor(self.tmp[:, n % 2, :], g.ps[2 * (t - t0) + h][:, :], self.ssq[:, 3, t:t + 1],
                                         self.gain[:, 1 if t < 2 else 0, 512 * h:512 * h + 512], ALU.mult, ALU.mult).then_inc(self.s_tmp, 1)
                n += 1

    def gpsimd(self, pool):
        n = 0
        for t in range(self.t0, NT):
            for h in range(2):
                x = self.g.x[:, t, 512 * h:512 * h + 512]
                pool.wait_ge(self.s_tmp, n + 1)
                pool.tensor_tensor(x, self.tmp[:, n % 2, :], x, ALU.add).then_inc(self.s_add, 1)
                n += 1


def stage_out(g, layer, w, kc, src, t0):
    nc = g.nc
    RING = 4
    with ExitStack() as ctx:
        slab = g.place(ctx, "wo_slab", [P, RING, D])
        tail = Tail(g, ctx, layer, 2, t0)
        s_w, s_used = [g.sem(f"wo_slab{i}") for i in range(RING)], g.sem("wo_used")
        with nc.Block() as block:
            @block.sync
            def _(sp):
                for k in range(kc):
                    if k >= RING:
                        sp.wait_ge(s_used, k - RING + 1)
                    sp.dma_start(slab[:, k % RING, :], w[k * P:(k + 1) * P, :]).then_inc(s_w[k % RING], 16)
                tail.load(sp)

            @block.tensor
            def _(pe):
                for k in range(kc):
                    pe.wait_ge(s_w[k % RING], 16 * (k // RING + 1))
                    for t in range(t0, NT):
                        for h in range(2):
                            mm = pe.matmul(g.ps[2 * (t - t0) + h][:, :], src[:, k, t * P:(t + 1) * P], slab[:, k % RING, 512 * h:512 * h + 512],
                                           start=(k == 0), stop=(k == kc - 1))
                        if k == kc - 1 and t < NT - 1:
                            mm.then_inc(tail.s_ready, 1)
                    mm.then_inc(tail.s_ready if k == kc - 1 else s_used, 1)

            @block.scalar
            def _(act):
                tail.scalar(act)

            @block.vector
            def _(dve):
                tail.vector(dve)

            @block.gpsimd
            def _(pool):
                tail.gpsimd(pool)


def stage_moe(g, layer, t0, out=None):
    nc, a = g.nc, g.a
    segs = (1,) if t0 else (0, 1)
    ns = len(segs)
    M = CAP * ns
    RA, RB = 6, RING_B
    SL = [(0, 512), (512, 1024), (1024, FF)]
    w1, w3, w2 = (a[n][layer] for n in ("exp_w1", "exp_w3", "exp_w2"))
    visits_a = lambda s: len(range(s, DC, RA))
    visits_b = lambda s: len(range(s, FC, RB))
    with ExitStack() as ctx:
        sb = lambda name, shape: g.place(ctx, name, shape)
        wa = sb("moe_w13", [P, RA, 2, FF])
        wb = sb("moe_w2", [P, RB, D])
        hm = sb("moe_h", [P, NT, D])
        oe = sb("moe_rows", [P, 2, NE // 4, D])
        selt = sb("moe_put", [P, 2, NE // 4, SEG])
        sel = sb("moe_pick", [P, 2, 2, NE * CAP + 4 * CAP])
        flat = lambda x: x[:, :, :, :].rearrange("p a b c -> p (a b c)")
        xg = sb("moe_xT", [P, 4, DC, M])
        xnx = sb("moe_xT_next", [P, 4, DC, M])
        s1 = sb("moe_silu", [M, FF])
        hidt = sb("moe_hidT", [P, FC, M])
        tail = Tail(g, ctx, layer, 5, t0, flat(xnx)[:, 0:1024].rearrange("p (k t) -> p k t", k=2),
                    None if t0 else flat(xg).rearrange("p (s d) -> p s d", s=2))
        hid = s1
        g.hT = oe[:, :, :, :].rearrange("p s b d -> p (s b d)")[:, 0:DC * T].rearrange("p (c t) -> p c t", c=DC)
        g.xn = hm
        s_wa, s_wb = [g.sem(f"moe_w13_{i}") for i in range(RA)], [g.sem(f"moe_w2_{i}") for i in range(RB)]
        (s_ua, s_ub, s_h, s_s, s_hid, s_ht, s_hto, s_y, s_o, s_gt, s_xq, s_x, s_store, s_apart) = (g.sem("moe_" + n) for n in (
            "w13_used", "w2_used", "h_ready", "silu_ready", "hid_ready", "hidT_ready", "hidT_out", "rows_ready", "rows_out", "picked", "next_xT", "xT_ready", "stored", "waits_apart"))
        s_rw = g.sem("route_weights")
        rw = sb("router_w", [P, DC, NE])
        with nc.Block() as block:
            @block.sync
            def _(sp):
                sp.dma_start(rw[:, :, :], a["router_w"][layer].rearrange("(c p) e -> p c e", p=P)).then_inc(s_rw, 16)
                for c in range(RA):
                    for k, w in enumerate((w1, w3)):
                        sp.dma_start(wa[:, c, k, :], w[0, c * P:(c + 1) * P, :]).then_inc(s_wa[c], 16)

        stage_norm(g, layer, 1, t0, ctx)
        with ExitStack() as rt:
            sr = lambda name, shape, dt=F32: g.place(rt, name, shape, dt)
            aff = sr("affinity", [P, 2, 48])
            lg = sr("router_tmp", [P, 4, NE])
            st8 = sr("router_stat", [P, 4, 4])
            atr = sr("affinity_rows", [48, SEG])
            mx = sr("top_values", [48, 8])
            ix = sr("top_index", [48, CAP], U32)
            ixf = sr("top_index_f", [48, CAP])
            own = sr("own_expert", [48, NE])
            bdx = flat(xnx)[0:48, 0:NE * CAP].rearrange("r (e c) -> r e c", e=NE)
            tok = sr("token_number", [P, 2])
            wsel = flat(xg)[:, 0:2 * NE * CAP].rearrange("p (k n) -> p k n", k=2)
            (s_lg, s_max, s_e, s_aff, s_at, s_row, s_bd, s_bc, s_own, s_sel, s_ws, s_st, s_sto, s_hb, s_hbo) = (g.sem("route_" + n) for n in (
                "logits", "max", "exp", "affinity", "rows", "diag", "diag2", "spread", "own", "pick", "weighed", "put", "put_out", "h_back", "h_out"))
            with nc.Block() as block:
                @block.gpsimd
                def _(pool):
                    g.pool.do(pool.memset(own[:, :], 0.0))
                    g.pool.do(pool.iota(tok[:, :], [[P, 2]], base=0, channel_multiplier=1, allow_small_or_imprecise_dtypes=True))
                    g.pool.join(pool)
                    for r in (0, 32):
                        g.pool.step(pool, pool.affine_select(out=own[:, :], in_=own[:, :], compare_op=ALU.not_equal, fill=1.0, base=-r, pattern=[[-1, NE]], channel_multiplier=1))
                    pool.memset(sel[:, :, :, NE * CAP:], 0.0).then_inc(s_own, 1)

                @block.tensor
                def _(pe):
                    pe.wait_ge(s_rw, 16)
                    for t in range(t0, NT):
                        for dc in range(DC):
                            mm = pe.matmul(g.ps[4][:, t * NE:(t + 1) * NE], g.hT[:, dc, t * P:(t + 1) * P], rw[:, dc, :], start=(dc == 0), stop=(dc == DC - 1))
                    mm.then_inc(s_lg, 1)
                    k = 0
                    for t in range(t0, NT):
                        for h in range(2):
                            if k >= 2:
                                pe.wait_ge(s_hbo, k - 1)
                            for i in range(4):
                                mm = pe.transpose(g.ps[6 + k % 2][:, i * P:(i + 1) * P], g.hT[:, 4 * h + i, t * P:(t + 1) * P], g.ident[:, :])
                            mm.then_inc(s_hb, 1)
                            k += 1
                    pe.wait_ge(s_aff, 1)
                    for j in range(2):
                        mm = pe.transpose(g.ps[5][0:48, j * P:(j + 1) * P], aff[:, j, :], g.ident[:, :])
                    mm.then_inc(s_at, 1)
                    pe.wait_ge(s_bd, 1)
                    for n, s in enumerate(segs):
                        pe.matmul(g.ps[n][:, :], g.ones[32 * s:32 * s + 16, :], bdx[32 * s:32 * s + 16, :, :].rearrange("r e c -> r (e c)"), start=True, stop=True).then_inc(s_bc, 1)
                    k = 0
                    for s in segs:
                        for j in range(2):
                            pe.wait_ge(s_ws, k + 1)
                            if k >= 2:
                                pe.wait_ge(s_sto, k - 1)
                            for b in range(4):
                                mm = pe.transpose(g.ps[2 + k % 2][:, b * P:(b + 1) * P], wsel[:, k % 2, b * P:(b + 1) * P], g.ident[:, :])
                            mm.then_inc(s_st, 1)
                            k += 1

                @block.scalar
                def _(act):
                    act.wait_ge(s_max, 1)
                    act.activation(lg[:, t0:NT, :], lg[:, t0:NT, :], ACT.Exp).then_inc(s_e, 1)
                    k = 0
                    for t in range(t0, NT):
                        for h in range(2):
                            act.wait_ge(s_hb, k + 1)
                            act.activation(hm[:, t, 512 * h:512 * h + 512], g.ps[6 + k % 2][:, :], ACT.Copy).then_inc(s_hbo, 1)
                            k += 1
                    for k in range(2 * ns):
                        act.wait_ge(s_st, k + 1)
                        s, j = segs[k // 2], k % 2
                        act.activation(selt[:, s, :, j * P:(j + 1) * P], g.ps[2 + k % 2][:, :].rearrange("p (b t) -> p b t", b=4), ACT.Copy).then_inc(s_sto, 1)

                @block.vector
                def _(dve):
                    dv = g.dve
                    n = NT - t0
                    dv.do(dve.memset(aff[:, :, :], 0.0))
                    dve.wait_ge(s_lg, 1)
                    psl = g.ps[4][:, t0 * NE:NT * NE].rearrange("p (t e) -> p t e", e=NE)
                    wide = lambda x: x.rearrange("p (t o) -> p t o", o=1).broadcast_to([P, n, NE])
                    dv.step(dve, dve.tensor_reduce(st8[:, 0, t0:NT], psl, AX.X, ALU.max))
                    dve.tensor_tensor(lg[:, t0:NT, :], psl, wide(st8[:, 0, t0:NT]), ALU.subtract).then_inc(s_max, 1)
                    dve.wait_ge(s_e, 1)
                    dv.step(dve, dve.tensor_reduce(st8[:, 1, t0:NT], lg[:, t0:NT, :], AX.X, ALU.add))
                    dv.step(dve, dve.reciprocal(st8[:, 2, t0:NT], st8[:, 1, t0:NT]))
                    for s in segs:
                        dv.do(dve.tensor_tensor(aff[:, :, 32 * s:32 * s + NE], lg[:, 2 * s:2 * s + 2, :],
                                                st8[:, 2, 2 * s:2 * s + 2].rearrange("p (t o) -> p t o", o=1).broadcast_to([P, 2, NE]), ALU.mult))
                    dv.join(dve)
                    dve.memset(g.small[:, 0:1], 0.0).then_inc(s_aff, 1)
                    dve.wait_ge(s_at, 1)
                    dv.step(dve, dve.tensor_copy(atr[:, :], g.ps[5][0:48, 0:SEG]))
                    for k in range(CAP // 8):
                        dv.step(dve, dve.max(mx[:, :], atr[:, :]))
                        dv.step(dve, dve.max_index(ix[:, 8 * k:8 * k + 8], mx[:, :], atr[:, :]))
                        if k < CAP // 8 - 1:
                            dv.step(dve, dve.match_replace(atr[:, :], mx[:, :], atr[:, :], -1.0))
                    dv.step(dve, dve.tensor_copy(ixf[:, :], ix[:, :]))
                    dve.wait_ge(s_own, 1)
                    dve.tensor_tensor(bdx[:, :, :], own[:, :].rearrange("r (e o) -> r e o", o=1).broadcast_to([48, NE, CAP]),
                                      ixf[:, :].rearrange("r (o c) -> r o c", o=1).broadcast_to([48, NE, CAP]), ALU.mult).then_inc(s_bd, 1)
                    k = 0
                    for n_, s in enumerate(segs):
                        dve.wait_ge(s_bc, n_ + 1)
                        for j in range(2):
                            dv.step(dve, dve.tensor_scalar(sel[:, s, j, 0:NE * CAP], g.ps[n_][:, :], tok[:, j:j + 1], None, ALU.is_equal))
                            if k >= 2:
                                dve.wait_ge(s_st, k - 1)
                            dve.tensor_tensor(wsel[:, k % 2, :].rearrange("p (e c) -> p e c", e=NE), sel[:, s, j, 0:NE * CAP].rearrange("p (e c) -> p e c", e=NE),
                                              aff[:, j, 32 * s:32 * s + NE].rearrange("p (e o) -> p e o", o=1).broadcast_to([P, NE, CAP]), ALU.mult).then_inc(s_ws, 1)
                            k += 1
        NB = NE // 4
        with nc.Block() as block:
            @block.sync
            def _(sp):
                def w13(i, j, first):
                    e = 4 * i + j if isinstance(i, int) else None
                    pick = lambda x: x[e] if e is not None else x[bass.ds(i * 4 + j, 1)].rearrange("o p f -> (o p) f")
                    for c in range(DC):
                        former = j * DC + max(x for x in range(-DC, c) if x % DC % RA == c % RA)
                        if first and former < 0:
                            continue
                        sp.wait_ge(s_ua, i * 4 * DC + former + 1)
                        for k, w in enumerate((w1, w3)):
                            sp.dma_start(wa[:, c % RA, k, :], pick(w)[c * P:(c + 1) * P, :]).then_inc(s_wa[c % RA], 16)

                for j in range(4):
                    w13(0, j, True)
                with sp.Fori(1, NB) as i:
                    for j in range(4):
                        w13(i, j, False)
                sp.wait_ge(s_x, 4 * (NB + 1))
                tail.load(sp)
                if out is not None:
                    for t in range(t0, NT):
                        sp.wait_ge(tail.s_add, 2 * (t - t0) + 2)
                        sp.dma_start(out[0, (t - t0) * P:(t - t0 + 1) * P, :], g.x[:, t, :]).then_inc(s_store, 16)
                    sp.wait_ge(s_store, 16 * (NT - t0))

            @block.tensor
            def _(pe):
                def pick(ib, q, wait):
                    if wait is not None:
                        pe.wait_ge(s_xq, wait)
                    for k in range(2):
                        dc = 2 * q + k
                        for n, s in enumerate(segs):
                            for j in range(2):
                                cols = slice(ib * 4 * CAP, (ib + 1) * 4 * CAP) if isinstance(ib, int) else bass.ds(ib * (4 * CAP), 4 * CAP)
                                mm = pe.matmul(g.ps[7][:, (k * ns + n) * P:(k * ns + n + 1) * P], hm[:, 2 * s + j, dc * P:(dc + 1) * P],
                                               sel[:, s, j, cols], start=(j == 0), stop=(j == 1))
                    mm.then_inc(s_gt, 1)

                def expert(i, j, first):
                    e = i * 4 + j
                    pe.wait_ge(s_x, e + 1)
                    if not first:
                        pe.wait_ge(s_hid, e)
                    for c in range(DC):
                        v = j * visits_a(c % RA) + c // RA + 1
                        pe.wait_ge(s_wa[c % RA], (i * (4 * visits_a(c % RA)) + v) * 32)
                        for k, (lo, hi) in enumerate(SL):
                            for m in range(2):
                                mm = pe.matmul(g.ps[k][64 * m:64 * m + M, 0:hi - lo], xg[:, j, c, :], wa[:, c % RA, m, lo:hi], start=(c == 0), stop=(c == DC - 1))
                        mm.then_inc(s_ua, 1)
                    if j < 2:
                        for q in (2 * j, 2 * j + 1):
                            pick(i + 1, q, 8 * (i + 1) + 2 * q)
                    pe.wait_ge(s_hid, e + 1)
                    if not first:
                        pe.wait_ge(s_hto, 2 * e)
                    pe.sem_inc(s_apart, 1)
                    for c in range(FC):
                        mm = pe.transpose(g.ps[3 + c // 8][:, (c % 8) * M:(c % 8 + 1) * M], hid[:, c * P:(c + 1) * P], g.ident[0:M, 0:M])
                        if c in (7, FC - 1):
                            mm.then_inc(s_ht, 1)
                    if not first:
                        pe.wait_ge(s_o, e)
                    for c in range(FC):
                        if c in (0, 8):
                            pe.wait_ge(s_hto, 2 * e + 1 + c // 8)
                        v = j * visits_b(c % RB) + c // RB + 1
                        pe.wait_ge(s_wb[c % RB], (i * (4 * visits_b(c % RB)) + v) * 16)
                        for m in range(2):
                            mm = pe.matmul(g.ps[5 + m][64 * m:64 * m + M, :], hidt[:, c, :], wb[:, c % RB, 512 * m:512 * m + 512], start=(c == 0), stop=(c == FC - 1))
                        mm.then_inc(s_ub, 1)

                for q in range(4):
                    pick(0, q, 2 * q if q else None)
                for j in range(4):
                    expert(0, j, j == 0)
                with pe.Fori(1, NB) as i:
                    for j in range(4):
                        expert(i, j, False)
                pe.wait_ge(s_o, NE)
                for t in range(t0, NT):
                    s = t // 2
                    for h in range(2):
                        for b in range(NB):
                            mm = pe.matmul(g.ps[2 * (t - t0) + h][:, :], selt[:, s, b, (t % 2) * P:(t % 2 + 1) * P], oe[:, s, b, 512 * h:512 * h + 512],
                                           start=(b == 0), stop=(b == NB - 1))
                    mm.then_inc(tail.s_ready, 1)

            @block.scalar
            def _(act):
                def expert(i, j, first):
                    e = i * 4 + j
                    act.wait_ge(s_ua, (e + 1) * DC)
                    if not first:
                        act.wait_ge(s_ht, 2 * e)
                    for k, (lo, hi) in enumerate(SL):
                        ins = act.activation(s1[:, lo:hi], g.ps[k][0:M, 0:hi - lo], ACT.Silu)
                        ins.then_inc(s_s, 1)
                    if not first:
                        act.wait_ge(s_ub, e * FC)
                    for k, (lo, hi) in enumerate(((0, 8), (8, FC))):
                        act.wait_ge(s_ht, 2 * e + 1 + k)
                        act.activation(hidt[:, lo:hi, :], g.ps[3 + k][:, 0:(hi - lo) * M].rearrange("p (c m) -> p c m", m=M), ACT.Copy).then_inc(s_hto, 1)

                for j in range(4):
                    expert(0, j, j == 0)
                with act.Fori(1, NB) as i:
                    for j in range(4):
                        expert(i, j, False)
                tail.scalar(act)

            @block.vector
            def _(dve):
                def rows_in(ib, q):
                    dve.wait_ge(s_gt, 4 * ib + q + 1)
                    for k in range(2):
                        dve.tensor_copy(xnx[:, :, 2 * q + k, :].rearrange("p e (s c) -> p e s c", s=ns),
                                        g.ps[7][:, k * ns * P:(k + 1) * ns * P].rearrange("p (s e c) -> p e s c", s=ns, e=4)).then_inc(s_xq, 1)

                def rows_on(j):
                    dve.tensor_copy(xg[:, j, :, :], xnx[:, j, :, :]).then_inc(s_x, 1)

                def expert(i, j, first):
                    e = i * 4 + j
                    if j < 2:
                        if j == 0:
                            dve.wait_ge(s_x, 4 * (i + 1))
                        rows_in(i + 1, 2 * j)
                        rows_in(i + 1, 2 * j + 1)
                    for k, (lo, hi) in enumerate(SL):
                        dve.wait_ge(s_s, 3 * e + k + 1)
                        ins = dve.tensor_tensor(hid[:, lo:hi], g.ps[k][64:64 + M, 0:hi - lo], s1[:, lo:hi], ALU.mult)
                    ins.then_inc(s_hid, 1)
                    if j == 1:
                        dve.wait_ge(s_xq, 8 * (i + 2))
                        rows_on(0)
                    if j:
                        rows_on(j)
                    dve.wait_ge(s_ub, (e + 1) * FC)
                    at = slice(i, i + 1) if isinstance(i, int) else bass.ds(i, 1)
                    for n, s in enumerate(segs):
                        for m in range(2):
                            ins = dve.tensor_copy(oe[32 * j:32 * j + 32, s, at, 512 * m:512 * m + 512],
                                                  g.ps[5 + m][64 * m + 32 * n:64 * m + 32 * n + 32, :].rearrange("p (o d) -> p o d", o=1))
                    ins.then_inc(s_o, 1)

                for q in range(4):
                    rows_in(0, q)
                dve.wait_ge(s_xq, 8)
                for j in range(4):
                    rows_on(j)
                for j in range(4):
                    expert(0, j, j == 0)
                with dve.Fori(1, NB) as i:
                    for j in range(4):
                        expert(i, j, False)
                tail.vector(dve)

            @block.gpsimd
            def _(pool):
                def w2_in(i, j, first):
                    e = 4 * i + j if isinstance(i, int) else None
                    pick = lambda x: x[e] if e is not None else x[bass.ds(i * 4 + j, 1)].rearrange("o p f -> (o p) f")
                    for c in range(FC):
                        former = j * FC + max(x for x in range(-FC, c) if x % FC % RB == c % RB)
                        if not (first and former < 0):
                            pool.wait_ge(s_ub, i * 4 * FC + former + 1)
                        pool.dma_start(wb[:, c % RB, :], pick(w2)[c * P:(c + 1) * P, :]).then_inc(s_wb[c % RB], 16)

                for j in range(4):
                    w2_in(0, j, True)
                with pool.Fori(1, NB) as i:
                    for j in range(4):
                        w2_in(i, j, False)
                tail.gpsimd(pool)


def stage_rwkv_project(g):
    nc, a = g.nc, g.a
    RING = 2
    MU = COL_P2
    order = ((1, "w"), (4, "a"), (5, "g"), (2, "k"), (3, "v"), (0, "r"))
    lo_of = {"g": SEG, "r": SEG}
    W = {"k": a["rw_wk"], "v": a["rw_wv"], "r": a["rw_wr"]}
    with ExitStack() as ctx:
        sb = lambda name, shape: g.place(ctx, name, shape)
        xx = sb("shift", [P, DC, T])
        mix = sb("mixture", [P, 2, DC, T])
        slab = sb("rw_slab", [P, RING, DC, 256])
        lora = sb("rw_lora", [P, DC, 128 + 64 + 160])
        s_lora, s_slab, s_free, s_mix, s_used, s_mm, s_ev = g.sem("lora_loaded"), [g.sem(f"rw_slab{i}") for i in range(RING)], g.sem("rw_slab_free"), g.sem("mixed"), g.sem("mix_used"), g.sem("rw_product"), g.sem("rw_out")
        s_kept = g.sem("rw_kept")
        with nc.Block() as block:
            @block.sync
            def _(sp):
                for d in range(2):
                    sp.dma_start(lora[:, :, 64 * d:64 * d + 64], a["rw_w1"][0, d].rearrange("(c p) r -> p c r", p=P)).then_inc(s_lora, 16)
                sp.dma_start(lora[:, :, 128:192], a["rw_a1"][0].rearrange("(c p) r -> p c r", p=P)).then_inc(s_lora, 16)
                sp.dma_start(lora[:, :, 192:352], a["rw_g1"][0].rearrange("(c p) r -> p c r", p=P)).then_inc(s_lora, 16)
                n = 0
                for name in "kvr":
                    for q in range(4):
                        if n >= RING:
                            sp.wait_ge(s_free, n - RING + 1)
                        sp.dma_start(slab[:, n % RING, :, :], W[name][0, :, 256 * q:256 * q + 256].rearrange("(c p) n -> p c n", p=P)).then_inc(s_slab[n % RING], 16)
                        n += 1
                for n, (src, dst) in enumerate(((g.kT, g.rwk), (g.vT, g.rwv), (g.rT, g.rwr))):
                    sp.wait_ge(s_ev, 4 + 8 * (n + 1))
                    sp.dma_start(dst, src[:, :, :]).then_inc(s_kept, 16)
                sp.wait_ge(s_kept, 48)

            @block.vector
            def _(dve):
                for s in range(2):
                    lo, hi = SEG * s, SEG * (s + 1)
                    for c in range(DC):
                        g.dve.do(dve.tensor_tensor(xx[:, c, lo + 1:hi - 1], g.hT[:, c, lo:hi - 2], g.hT[:, c, lo + 2:hi], ALU.add))
                        g.dve.do(dve.tensor_copy(xx[:, c, lo:hi:SEG - 1], g.hT[:, c, lo + 1:hi - 1:SEG - 3]))
                g.dve.join(dve)
                for c in range(DC):
                    g.dve.do(dve.scalar_tensor_tensor(xx[:, c, :], xx[:, c, :], 0.5, g.hT[:, c, :], ALU.mult, ALU.subtract))
                g.dve.join(dve)
                for n, (m, name) in enumerate(order):
                    lo = lo_of.get(name, 0)
                    if n >= 2:
                        dve.wait_ge(s_used, n - 1)
                    for c in range(DC):
                        ins = dve.scalar_tensor_tensor(mix[:, n % 2, c, lo:T], xx[:, c, lo:T], g.cols[:, MU + 8 * m + c:MU + 8 * m + c + 1], g.hT[:, c, lo:T], ALU.mult, ALU.add)
                    ins.then_inc(s_mix, 1)

            @block.tensor
            def _(pe):
                k = 0
                pe.wait_ge(s_lora, 64)
                for n, (m, name) in enumerate(order):
                    lo = lo_of.get(name, 0)
                    pe.wait_ge(s_mix, n + 1)
                    parts = {"w": [(0, 128)], "a": [(128, 192)], "g": [(192, 320), (320, 352)]}.get(name, [None] * 8)
                    for q, part in enumerate(parts):
                        if k >= 8:
                            pe.wait_ge(s_ev, k - 7)
                        if part is None:
                            ns = 4 * (n - 3) + q // 2
                            if q % 2 == 0:
                                pe.wait_ge(s_slab[ns % RING], 16 * (ns // RING + 1))
                        rows = part[1] - part[0] if part else P
                        for c in range(DC):
                            lhs = lora[:, c, part[0]:part[1]] if part else slab[:, ns % RING, c, P * (q % 2):P * (q % 2) + P]
                            mm = pe.matmul(g.ps[k % 8][0:rows, 0:T - lo], lhs, mix[:, n % 2, c, lo:T], start=(c == 0), stop=(c == DC - 1))
                        mm.then_inc(s_mm, 1)
                        k += 1
                        pe.wait_ge(s_mm, k)
                        if part is None and q % 2:
                            pe.nop().then_inc(s_free, 1)
                    pe.nop().then_inc(s_used, 1)

            @block.scalar
            def _(act):
                act.wait_ge(s_mm, 1)
                act.activation(g.tw[:, :], g.ps[0][:, :], ACT.Tanh).then_inc(s_ev, 1)
                act.wait_ge(s_mm, 2)
                act.activation(g.ta[0:64, :], g.ps[1][0:64, :], ACT.Copy).then_inc(s_ev, 1)
                act.wait_ge(s_mm, 3)
                act.activation(g.tg[:, 0, :], g.ps[2][:, 0:SEG], ACT.Sigmoid).then_inc(s_ev, 1)
                act.wait_ge(s_mm, 4)
                act.activation(g.tg[0:32, 1, :], g.ps[3][0:32, 0:SEG], ACT.Sigmoid).then_inc(s_ev, 1)
                for k in range(4, 28):
                    q = (k - 4) % 8
                    dst = (g.kT, g.vT, g.rT)[(k - 4) // 8]
                    act.wait_ge(s_mm, k + 1)
                    act.activation(dst[:, q, :], g.ps[k % 8][:, 0:SEG] if dst is g.rT else g.ps[k % 8][:, :], ACT.Copy).then_inc(s_ev, 1)


def stage_rwkv_masks(g):
    nc = g.nc
    s_a, s_b = g.sem("mask_filled"), g.sem("mask_cut")
    with nc.Block() as block:
        @block.gpsimd
        def _(pool):
            pool.memset(g.lev[:, :, :, :], 0.0)
            pool.memset(g.i64[:, :], 0.0)
            pool.memset(g.bones[:, :], 0.0)
            pool.memset(g.inc[:, :, :], 1.0)
            pool.memset(g.strict[:, :, :], 1.0).then_inc(s_a, 1)
            pool.wait_ge(s_a, 1)
            n = 0
            for h in range(2):
                r = slice(64 * h, 64 * h + 64)
                ins = [pool.memset(g.bones[r, 64 * h:64 * h + 64], 1.0),
                       pool.affine_select(out=g.i64[r, :], in_=g.i64[r, :], compare_op=ALU.not_equal, fill=1.0, base=0, pattern=[[-1, 64]], channel_multiplier=1)]
                for d, sgn in ((0, 1), (1, -1)):
                    ins.append(pool.affine_select(out=g.inc[r, d, :], in_=g.inc[r, d, :], compare_op=ALU.is_ge, fill=0.0, base=0, pattern=[[sgn, 64]], channel_multiplier=-sgn))
                    ins.append(pool.affine_select(out=g.strict[r, d, :], in_=g.strict[r, d, :], compare_op=ALU.is_gt, fill=0.0, base=0, pattern=[[sgn, 64]], channel_multiplier=-sgn))
                for i in ins:
                    i.then_inc(s_b, 1)
                n += len(ins)
                for lv in range(6):
                    m = 1 << lv
                    for k in range(2):
                        view = g.lev[r, k, lv, :].rearrange("p (b h r) -> p b h r", h=2, r=m)[:, :, 1 - k, :]
                        pool.memset(view, 1.0).then_inc(s_b, 1)
                        n += 1
                        pool.wait_ge(s_b, n)
                        pool.affine_select(out=view, in_=view, compare_op=ALU.is_ge, fill=0.0, base=-k * m, pattern=[[-2 * m, 32 // m], [0, m]], channel_multiplier=1).then_inc(s_b, 1)
                        n += 1
                        pool.wait_ge(s_b, n)
                        pool.affine_select(out=view, in_=view, compare_op=ALU.is_ge, fill=0.0, base=k * m + m - 1, pattern=[[2 * m, 32 // m], [0, m]], channel_multiplier=-1).then_inc(s_b, 1)
                        n += 1


def stage_rwkv(g):
    nc = g.nc
    K = 0.6065306597126334
    C3 = lambda x: x.rearrange("p (c t) -> p c t", t=LC)
    ORDER = ((0, 1, 2, 3, 4, 5, 6, 7), (3, 2, 1, 0, 7, 6, 5, 4))
    LAT = NCH // 2
    HALF = (slice(0, 64), slice(64, 128))
    with ExitStack() as ctx:
        sb = lambda name, shape: g.place(ctx, name, shape)
        two = lambda name, shape: [sb(f"{name}{d}", shape) for d in range(2)]
        par = sb("pair_cols", [P, 8])
        w2s, a2s, g2s = sb("w2_pair", [P, 2, P]), sb("a2_pair", [P, P]), sb("g2_pair", [P, 2, P])
        k0, v0, r0 = sb("k_pair", [P, T]), sb("v_pair", [P, T]), sb("r_pair", [P, SEG])
        kk, al, bb, km, t2 = (sb(n, [P, T]) for n in ("kk", "iclr", "bvec", "kmod", "rw_t2"))
        gp, bon = sb("gate_pair", [P, SEG]), sb("bonus", [P, SEG])
        one = sb("chunk_starts", [P, T])
        levb = sb("level_masks_blk", [P, 2, 5, 2, LC])
        sg, cs, ex = two("rw_sig", [P, T]), two("rw_cum", [P, T]), two("rw_exc", [P, T])
        em, ep = sg, cs
        bh, kh, bbar, kbar = (two(n, [P, T]) for n in ("b_hat", "k_hat", "b_bar", "k_bar"))
        ah, rh, pp = two("a_hat_blk", [P, NCH, 2, LC]), two("r_hat_blk", [P, LAT, 2, LC]), two("p_prod_blk", [P, NCH, 2, LC])
        nlev = two("n_levels_blk", [P, 2, NCH, 2, LC])
        vt = sb("v_tok_blk", [P, NCH, 2, LC])
        ecl = two("e_cend", [P, NCH])
        nt = two("n_t", [P, NCH, LC])
        t1 = nt[0][:, :, :].rearrange("p c t -> p (c t)")
        brr = two("b_tok_r_products", [P, NCH, 3, LC])
        rhs = two("a_and_nkv", [P, NCH, 2, LC])
        x, xt = two("x_inv_blk", [P, NCH, 2, LC]), two("x_inv_t_blk", [P, NCH, 2, LC])
        nk, kt, st = (two(n, [P, NCH, LC]) for n in ("nk_t", "k_tok", "state"))
        bt = [b[:, :, 0, :] for b in brr]
        gt, rt, dg = x, [p[:, 0:LAT, :, :] for p in pp], nt
        au = [n[:, :, :, :, :].rearrange("p l c h t -> p (l c h t)").rearrange("p (c k h t) -> p c k h t", k=2, h=2, t=LC) for n in nlev]
        yn, ysq = rhs[0][:, 0:2, :, :].rearrange("p a b t -> p (a b) t"), rhs[1][:, 0:2, :, :].rearrange("p a b t -> p (a b) t")
        ystat = sb("y_stat", [P, 4, LAT])
        yc = sb("y_chan", [P, SEG])
        par_t, gp_t, bon_t = sb("pair_cols_kept", [P, 8]), sb("gate_kept", [P, SEG]), sb("bonus_kept", [P, SEG])
        names = ("starts", "freed", "tail_kept", "apart", "pass_end", "staged", "lora_mm", "sig", "iclr", "gate", "kksq", "kksum", "kkroot", "kmod", "bonus_in", "bonus_mm", "cum", "exps", "hats", "bars",
                 "mm1", "nt", "x0", "mask", "nlev", "pmm", "pcopy", "xmm", "xadd", "tokmm", "tok", "nkvmm", "nkv", "aumm", "au", "au_late", "gmm", "gt", "dg", "smm", "scopy", "ymm", "ystat1", "ysq", "yvar", "yroot", "yn", "ytmm", "yout")
        S = {n: g.sem("rw_" + n) for n in names}
        with nc.Block() as block:
            @block.gpsimd
            def _(pool):
                for b in ah + rh:
                    pool.memset(b[:, :, :, :], 0.0)
                pool.memset(vt[:, :, :, :], 0.0)
                pool.memset(w2s[:, :, :], 0.0)
                pool.memset(a2s[:, :], 0.0)
                pool.memset(g2s[:, :, :], 0.0)
                pool.memset(one[:, :], 1.0).then_inc(S["starts"], 1)
                pool.wait_ge(S["starts"], 1)
                pool.memset(one[:, 0::LC], 0.0)

            @block.vector
            def _(dve):
                for b in pp + x + xt:
                    dve.memset(b[:, :, :, :], 0.0)
                for b in brr:
                    dve.memset(b[:, 0:LAT, 1, :], 0.0)
                for b in nlev:
                    dve.memset(b[:, :, :, :, :], 0.0)
                dv = g.dve
                dv.step(dve, dve.memset(levb[:, :, :, :, :], 0.0))
                for h, r in enumerate(HALF):
                    dve.tensor_copy(levb[r, :, :, h, :], g.lev[r, :, 1:6, :])

        with nc.Block() as block:
            def W(eng, name, i, per, k):
                eng.wait_ge(S[name], i * per + k)

            UNITS = [(d, c) for d in range(2) for c in (0, LAT)]
            NU = 5 * len(UNITS)
            unit = lambda n: (n // 4,) + UNITS[n % 4]
            UX = lambda bank: g.ps[bank][:, :].rearrange("p (c h t) -> p c h t", h=2, t=LC)

            QUARTERS = [(h, p) for h in range(2) for p in range(2)]
            quarter = lambda bank, h, p: g.ps[bank][HALF[p], :].rearrange("r (q h t) -> r q h t", h=2, t=LC)[:, :, h, :]

            @block.sync
            def _(sp):
                def pair(i):
                    one_ = (lambda x: x[:, i, :]) if isinstance(i, int) else (lambda x: x[:, bass.ds(i, 1), :].rearrange("p o t -> p (o t)"))
                    cols = slice(0, P) if isinstance(i, int) else bass.ds(i * P, P)
                    for dst, src in ((k0[:, :], one_(g.rwk)), (v0[:, :], one_(g.rwv)), (r0[:, :], one_(g.rwr)),
                                     (w2s[0:64, 0, :], g.a["rw_w2"][0, 0, :, cols]), (w2s[64:128, 1, :], g.a["rw_w2"][0, 1, :, cols]), (a2s[0:64, :], g.a["rw_a2"][0, :, cols]),
                                     (g2s[:, 0, :], g.a["rw_g2"][0, 0:P, cols]), (g2s[0:32, 1, :], g.a["rw_g2"][0, P:160, cols])):
                        sp.dma_start(dst, src).then_inc(S["staged"], 16)

                pair(0)
                with sp.Fori(0, DC - 1) as i:
                    for name, per in (("hats", 2), ("lora_mm", 4), ("kmod", 1)):
                        W(sp, name, i, per, per)
                        sp.sem_inc(S["freed"], 1)
                    W(sp, "tokmm", i, 7, 1)
                    sp.sem_inc(S["freed"], 1)
                    pair(i + 1)

            @block.gpsimd
            def _(pool):
                with pool.Fori(0, DC) as i:
                    def bars(d):
                        W(pool, "hats", i, 2, d + 1)
                        e3 = lambda: ecl[d][:, :].rearrange("p (c o) -> p c o", o=1).broadcast_to([P, NCH, LC])
                        pool.tensor_tensor(C3(bbar[d][:, :]), C3(bh[d][:, :]), e3(), ALU.mult).then_inc(S["bars"], 1)
                        pool.tensor_tensor(C3(kbar[d][:, :]), C3(kh[d][:, :]), e3(), ALU.mult).then_inc(S["bars"], 1)

                    bars(0)
                    for lv in range(5):
                        for d in range(2):
                            if (lv, d) == (2, 0):
                                bars(1)
                            if lv == 0:
                                W(pool, "nt", i, 2, d + 1)
                            if lv >= 2:
                                W(pool, "pmm", i, NU, 4 * (lv - 2) + 2 * d + 2)
                            pool.tensor_tensor(nlev[d][:, lv % 2, :, :, :], nt[d][:, :, :].rearrange("p c (o t) -> p c o t", o=1).broadcast_to([P, NCH, 2, LC]),
                                               levb[:, d, lv, :, :].rearrange("p (o h) t -> p o h t", o=1).broadcast_to([P, NCH, 2, LC]), ALU.mult).then_inc(S["nlev"], 1)
                    W(pool, "nlev", i, 10, 10)
                    W(pool, "x0", i, 2, 2)
                    W(pool, "kmod", i, 1, 1)
                    W(pool, "gate", i, 1, 1)
                    pool.sem_inc(S["freed"], 1)
                    for dst, src in ((par_t, par), (gp_t, gp), (bon_t, bon)):
                        pool.tensor_copy(dst[:, :], src[:, :]).then_inc(S["tail_kept"], 1)
                    for d in range(2):
                        pool.tensor_tensor(dg[d][:, :, :], g.i64[:, :].rearrange("p (o t) -> p o t", o=1).broadcast_to([P, NCH, LC]),
                                           ecl[d][:, :].rearrange("p (c o) -> p c o", o=1).broadcast_to([P, NCH, LC]), ALU.mult).then_inc(S["dg"], 1)
                    pool.wait_ge(S["pass_end"], i + 1)

            @block.vector
            def _(dve):
                dv = g.dve
                inc8 = lambda m, n: m.rearrange("p (o t) -> p o t", o=1).broadcast_to([P, n, LC])
                def columns(i, first=False):
                    if not first:
                        W(dve, "tail_kept", i - 1, 3, 3)
                    dv.do(dve.tensor_copy(par[:, :].rearrange("p (k o) -> p k o", o=1), g.cols[:, COL_P2 + 48:COL_P2 + 112].rearrange("p (k r) -> p k r", r=8)[:, :, slice(0, 1) if first else bass.ds(i, 1)]))
                    dv.join(dve)
                    W(dve, "staged", i, 128, 128)
                    dve.tensor_scalar(kk[:, :], k0[:, :], par[:, 3:4], None, ALU.mult).then_inc(S["cum"], 1)

                def sums(i, d):
                    W(dve, "sig", i, 2, d + 1)
                    order = slice(None) if d == 0 else slice(None, None, -1)
                    dv.step(dve, dve.tensor_tensor_scan(cs[d][:, order], one[:, :], sg[d][:, order], 0.0, ALU.mult, ALU.add))
                    dve.tensor_tensor(ex[d][:, :], cs[d][:, :], sg[d][:, :], ALU.subtract).then_inc(S["cum"], 1)

                def keys(i):
                    W(dve, "iclr", i, 1, 1)
                    dv.step(dve, dve.tensor_scalar(t1[:, :], al[:, :], 1.0, par[:, 4:5], ALU.subtract, ALU.mult))
                    dv.step(dve, dve.scalar_tensor_tensor(km[:, :], t1[:, :], 1.0, k0[:, :], ALU.add, ALU.mult))
                    dv.step(dve, dve.tensor_tensor(bon[:, :], r0[:, :], km[:, SEG:T], ALU.mult))
                    dve.tensor_scalar(bon[:, :], bon[:, :], par[:, 5:6], None, ALU.mult).then_inc(S["bonus_in"], 1)

                def roots(i):
                    W(dve, "kkroot", i, 1, 1)
                    dv.step(dve, dve.reciprocal(t2[:, :], t2[:, :]))

                def unit_keys(i):
                    dv.step(dve, dve.tensor_tensor(kk[:, :], kk[:, :], t2[:, :], ALU.mult))
                    dv.step(dve, dve.tensor_tensor(bb[:, :], kk[:, :], al[:, :], ALU.mult))

                def hats(i, d):
                    W(dve, "exps", i, 2, d + 1)
                    end = ep[d][:, LC - 1::LC] if d == 0 else ep[d][:, 0::LC]
                    dv.do(dve.tensor_copy(ecl[d][:, :], end))
                    for h, r in enumerate(HALF):
                        dv.do(dve.scalar_tensor_tensor(ah[d][r, :, h, :], C3(kk[r, :]), -1.0, C3(ex[d][r, :]), ALU.mult, ALU.mult))
                        dv.do(dve.tensor_tensor(rh[d][r, :, h, :], C3(r0[r, :]), C3(ep[d][r, SEG:T]), ALU.mult))
                    dv.do(dve.tensor_tensor(bh[d][:, :], bb[:, :], em[d][:, :], ALU.mult))
                    dv.do(dve.tensor_tensor(kh[d][:, :], km[:, :], em[d][:, :], ALU.mult))
                    dv.join(dve)
                    dve.memset(g.small[:, 0:1], 0.0).then_inc(S["hats"], 1)

                def bonus(i):
                    W(dve, "bonus_mm", i, 1, 1)
                    dv.step(dve, dve.tensor_tensor(bon[:, :], g.ps[6][:, 0:SEG], v0[:, SEG:T], ALU.mult))
                    dve.memset(g.small[:, 0:1], 0.0).then_inc(S["kmod"], 1)

                def masked(bank, dst, m):
                    for h, p in QUARTERS:
                        ins = dve.tensor_tensor(dst[HALF[h], p::2, :], quarter(bank, h, p), m[HALF[h], :].rearrange("p (o t) -> p o t", o=1).broadcast_to([64, LAT, LC]), ALU.mult)
                    ins.then_inc(S["mask"], 1)

                def core(i, nxt):
                    for d in range(2):
                        B = 4 * d
                        W(dve, "nt", i, 2, d + 1)
                        W(dve, "mm1", i, 8, 4 * d + 2)
                        cut = lambda m, r: m[r, :].rearrange("p (o t) -> p o t", o=1).broadcast_to([64, NCH, LC])
                        for h, r in enumerate(HALF):
                            dv.do(dve.tensor_tensor(x[d][r, :, h, :], C3(g.ps[B + 1][r, :]), cut(g.lev[:, 1 - d, 0, :], r), ALU.mult))
                            dv.do(dve.tensor_tensor(xt[d][r, :, h, :], nt[d][r, :, :], cut(g.lev[:, d, 0, :], r), ALU.mult))
                        dv.join(dve)
                        for h, r in enumerate(HALF):
                            dv.do(dve.tensor_tensor(x[d][r, :, h, :], x[d][r, :, h, :], cut(g.i64, r), ALU.add))
                            dv.do(dve.tensor_tensor(xt[d][r, :, h, :], xt[d][r, :, h, :], cut(g.i64, r), ALU.add))
                        dv.join(dve)
                        dve.memset(g.small[:, 0:1], 0.0).then_inc(S["x0"], 1)
                        W(dve, "mm1", i, 8, 4 * d + 3)
                        masked(B + 2, nk[d], g.strict[:, d, :])
                    for d in range(2):
                        W(dve, "mm1", i, 8, 4 * d + 4)
                        for h, p in QUARTERS:
                            ins = dve.tensor_tensor(brr[d][HALF[h], LAT + p::2, 1:3, :], quarter(4 * d + 3, h, p).rearrange("r (s q) t -> r q s t", s=2),
                                                    g.inc[HALF[h], d, :].rearrange("p (a b t) -> p a b t", a=1, b=1).broadcast_to([64, LAT // 2, 2, LC]), ALU.mult)
                        ins.then_inc(S["mask"], 1)
                    for n in range(NU):
                        lv, d, c = unit(n)
                        W(dve, "xmm", i, NU, n + 1)
                        if lv < 4:
                            dve.tensor_tensor(x[d][:, c:c + LAT, :, :], UX(2 + 2 * (n % 2)), x[d][:, c:c + LAT, :, :], ALU.add).then_inc(S["xadd"], 1)
                        dve.tensor_tensor(xt[d][:, c:c + LAT, :, :], UX(5 + n % 2), xt[d][:, c:c + LAT, :, :], ALU.add).then_inc(S["xadd"], 2 if lv == 4 else 1)
                    for d in range(2):
                        B = 4 * d
                        W(dve, "aumm", i, 2, d + 1)
                        for h, r in enumerate(HALF):
                            dve.tensor_copy(au[d][r, LAT:NCH, :, h, :], g.ps[B + 1][r, :].rearrange("p (c k t) -> p c k t", k=2, t=LC)).then_inc(S["au_late"], 1)
                    for d in range(2):
                        B = 4 * d
                        W(dve, "gmm", i, 2, d + 1)
                        W(dve, "dg", i, 2, d + 1)
                        for h, r in enumerate(HALF):
                            wide = lambda bank, k: g.ps[bank][r, :].rearrange("p (c k t) -> p c k t", k=2, t=LC)[:, :, k, :]
                            dve.tensor_tensor(gt[d][r, 0:LAT, h, :], wide(B + 2, 0), dg[d][r, 0:LAT, :], ALU.add).then_inc(S["gt"], 1)
                            dve.tensor_tensor(gt[d][r, LAT:NCH, h, :], wide(B + 3, 0), dg[d][r, LAT:NCH, :], ALU.add).then_inc(S["gt"], 1)
                            dve.tensor_tensor(rt[d][r, :, h, :], wide(B + 3, 1), rh[d][r, :, h, :], ALU.add).then_inc(S["gt"], 1)
                    W(dve, "gt", i, 12, 12)
                    between = [] if nxt is None else [lambda: columns(nxt), lambda: sums(nxt, 0), lambda: sums(nxt, 1), lambda: keys(nxt),
                                                      lambda: roots(nxt), lambda: unit_keys(nxt), lambda: hats(nxt, 0)]
                    for k in range(NCH - 1):
                        c = ORDER[0][k + 1]
                        W(dve, "smm", i, 14, 2 * k + 1)
                        dve.tensor_copy(st[0][:, c, :], g.ps[k % 2][:, k * LC:(k + 1) * LC]).then_inc(S["scopy"], 1)
                        if between:
                            between[k]()
                    W(dve, "ymm", i, 1, 1)
                    y = C3(g.ps[3][:, 0:SEG])
                    wide = lambda v: v.rearrange("p (c o) -> p c o", o=1).broadcast_to([P, LAT, LC])
                    dv.step(dve, dve.tensor_reduce(ystat[:, 0, :], y, AX.X, ALU.add))
                    dv.step(dve, dve.tensor_scalar(ystat[:, 0, :], ystat[:, 0, :], 1.0 / LC, None, ALU.mult))
                    dve.tensor_tensor(yn[:, :, :], y, wide(ystat[:, 0, :]), ALU.subtract).then_inc(S["ystat1"], 1)
                    if nxt is not None:
                        bonus(nxt)
                    W(dve, "ysq", i, 1, 1)
                    dve.tensor_reduce(ystat[:, 1, :], ysq[:, :, :], AX.X, ALU.add).then_inc(S["yvar"], 1)
                    if nxt is not None:
                        hats(nxt, 1)
                    W(dve, "yroot", i, 1, 1)
                    dv.step(dve, dve.reciprocal(ystat[:, 3, :], ystat[:, 2, :]))
                    dve.tensor_tensor(yn[:, :, :], yn[:, :, :], wide(ystat[:, 3, :]), ALU.mult).then_inc(S["yn"], 1)
                    W(dve, "ytmm", i, 1, 1)
                    dv.step(dve, dve.tensor_scalar(yc[:, :], g.ps[2][:, 0:SEG], par_t[:, 6:7], par_t[:, 7:8], ALU.mult, ALU.add))
                    dv.step(dve, dve.tensor_tensor(yc[:, :], yc[:, :], bon_t[:, :], ALU.add))
                    at = slice(i, i + 1) if isinstance(i, int) else bass.ds(i, 1)
                    dve.tensor_tensor(g.yT[:, at, :], yc[:, :].rearrange("p (o t) -> p o t", o=1), gp_t[:, :].rearrange("p (o t) -> p o t", o=1), ALU.mult).then_inc(S["pass_end"], 1)
                    dve.wait_ge(S["pass_end"], i + 1)

                columns(0, True)
                sums(0, 0)
                sums(0, 1)
                keys(0)
                roots(0)
                unit_keys(0)
                hats(0, 0)
                bonus(0)
                hats(0, 1)
                with dve.Fori(0, DC - 1) as i:
                    dv.enter(i, g.rw_steps)
                    core(i, i + 1)
                    dv.leave(DC - 1)
                core(DC - 1, None)

            @block.scalar
            def _(act):
                def squares(i):
                    W(act, "cum", i, 3, 1)
                    act.activation(t2[:, :], kk[:, :], ACT.Square).then_inc(S["kksq"], 1)

                def decays(i, d):
                    W(act, "lora_mm", i, 4, d + 1)
                    act.activation(sg[d][:, :], g.ps[6 + d][:, :], ACT.Sigmoid, bias=par[:, d:d + 1]).then_inc(S["sig"], 1)

                def rates(i):
                    W(act, "lora_mm", i, 4, 3)
                    act.activation(al[:, :], g.ps[2][:, :], ACT.Sigmoid, bias=par[:, 2:3]).then_inc(S["iclr"], 1)

                def gates(i):
                    W(act, "lora_mm", i, 4, 4)
                    act.activation(gp[:, :], g.ps[6][:, 0:SEG], ACT.Copy).then_inc(S["gate"], 1)

                def roots(i):
                    W(act, "kksum", i, 1, 1)
                    act.activation(t2[:, :], g.ps[7][:, :], ACT.Sqrt, bias=g.eps2[:, 0:1]).then_inc(S["kkroot"], 1)

                def exps(i, d):
                    W(act, "cum", i, 3, 2 + d)
                    act.activation(em[d][:, :], cs[d][:, :], ACT.Exp, scale=K)
                    act.activation(ep[d][:, :], cs[d][:, :], ACT.Exp, scale=-K)
                    act.activation(ex[d][:, :], ex[d][:, :], ACT.Exp, scale=-K).then_inc(S["exps"], 1)

                def core(i, nxt):
                    for d in range(2):
                        W(act, "mm1", i, 8, 4 * d + 1)
                        for h, p in QUARTERS:
                            ins = act.activation(nt[d][HALF[h], p::2, :], quarter(4 * d, h, p), ACT.Copy)
                        ins.then_inc(S["nt"], 1)
                    def tok(k, dst, bank):
                        W(act, "tokmm", i, 7, k)
                        act.activation(dst, C3(g.ps[bank][:, :]), ACT.Copy).then_inc(S["tok"], 1)

                    def pcopy(lo, hi):
                        for n in range(lo, hi):
                            lv, d, c = unit(n)
                            W(act, "pmm", i, NU, n + 1)
                            if n >= 4:
                                W(act, "xmm", i, NU, n - 3)
                            act.activation(pp[d][:, c:c + LAT, :, :], UX(n % 2), ACT.Copy).then_inc(S["pcopy"], 1)

                    def tokq(k, dst, bank, units=()):
                        W(act, "tokmm", i, 7, k)
                        for m, (h, p) in enumerate(QUARTERS):
                            ins = act.activation(dst(h, p), quarter(bank, h, p), ACT.Copy)
                            if m < len(units):
                                pcopy(units[m], units[m] + 1)
                        ins.then_inc(S["tok"], 1)

                    rows = lambda x: (lambda h, p: x[HALF[h], p::2, :])
                    pcopy(0, 2)
                    tokq(1, lambda h, p: vt[HALF[h], p::2, h, :], 3, (2,))
                    tok(2, rhs[0][:, :, 0, :], 7)
                    pcopy(3, 4)
                    tok(3, rhs[1][:, :, 0, :], 3)
                    tokq(4, rows(bt[0]), 7, (4, 5))
                    tokq(5, rows(bt[1]), 3, (6, 7))
                    tokq(6, rows(kt[0]), 7, (8, 9))
                    tokq(7, rows(kt[1]), 3, (10, 11))
                    pcopy(12, 14)
                    for d in range(2):
                        W(act, "nkvmm", i, 2, d + 1)
                        for h, p in QUARTERS:
                            ins = act.activation(rhs[d][HALF[h], p::2, 1, :], quarter(4 * d + 3, h, p), ACT.Copy)
                        ins.then_inc(S["nkv"], 1)
                    pcopy(14, NU)
                    for d in range(2):
                        W(act, "aumm", i, 2, d + 1)
                        for h, r in enumerate(HALF):
                            act.activation(au[d][r, 0:LAT, :, h, :], g.ps[4 * d][r, :].rearrange("p (c k t) -> p c k t", k=2, t=LC), ACT.Copy).then_inc(S["au"], 1)
                    between = [] if nxt is None else [[lambda: squares(nxt), lambda: decays(nxt, 0)], [lambda: decays(nxt, 1), lambda: rates(nxt)], [lambda: gates(nxt)],
                                                      [lambda: roots(nxt)], [lambda: exps(nxt, 0)], [lambda: exps(nxt, 1)], []]
                    for k in range(NCH - 1):
                        c = ORDER[1][k + 1]
                        W(act, "smm", i, 14, 2 * k + 2)
                        act.activation(st[1][:, c, :], g.ps[4 + k % 2][:, k * LC:(k + 1) * LC], ACT.Copy).then_inc(S["scopy"], 1)
                        if between:
                            for part in between[k]:
                                part()
                    W(act, "ystat1", i, 1, 1)
                    act.activation(ysq[:, :, :], yn[:, :, :], ACT.Square).then_inc(S["ysq"], 1)
                    W(act, "yvar", i, 1, 1)
                    act.activation(ystat[:, 2, :], ystat[:, 1, :], ACT.Sqrt, bias=g.eps[:, 1:2], scale=1.0 / LC).then_inc(S["yroot"], 1)
                    act.wait_ge(S["pass_end"], i + 1)

                squares(0)
                decays(0, 0)
                decays(0, 1)
                rates(0)
                gates(0)
                roots(0)
                exps(0, 0)
                exps(0, 1)
                with act.Fori(0, DC - 1) as i:
                    core(i, i + 1)
                core(DC - 1, None)

            @block.tensor
            def _(pe):
                def apart():
                    pe.sem_inc(S["apart"], 1)

                def each(bank, col0, lhs, rhs_, chunks, width=LC):
                    apart()
                    jobs = [(h, n, c) for h in range(2) for n, c in enumerate(chunks)]
                    if width > LC:
                        jobs.sort(key=lambda j: j[1])
                    for h, n, c in jobs:
                        o = col0 + n * width
                        mm = pe.matmul(g.ps[bank][HALF[h], o:o + width], lhs(c, h), rhs_(c, h), start=True, stop=True)
                    return mm

                def paired(bank, lhs, rhs_, chunks, col0=0):
                    apart()
                    for n, c in enumerate(chunks):
                        o = col0 + n // 2 * P
                        mm = pe.matmul(g.ps[bank][HALF[n % 2], o:o + P], lhs(c, 0), rhs_(c), start=True, stop=True)
                    return mm

                both = lambda x, c0=0: (lambda c: full(x, c - c0))
                tk = lambda x: (lambda c, h: x[:, c * LC:(c + 1) * LC])
                ch = lambda x: (lambda c, h: x[:, c, :])
                blk = lambda x, c0=0: (lambda c, h: x[:, c - c0, h, :])
                ALL, LATS = range(NCH), range(LAT, NCH)
                eye = lambda c, h: g.ident[:, HALF[h]]
                full = lambda x, c: x[:, c, :, :].rearrange("p h t -> p (h t)")
                def lora(i):
                    W(pe, "staged", i, 128, 128)
                    for d in range(2):
                        pe.matmul(g.ps[6 + d][:, :], w2s[:, d, :], g.tw[:, :], start=True, stop=True).then_inc(S["lora_mm"], 1)
                    pe.matmul(g.ps[2][:, :], a2s[:, :], g.ta[:, :], start=True, stop=True).then_inc(S["lora_mm"], 1)

                def gate_sums(i):
                    W(pe, "sig", i, 2, 2)
                    pe.matmul(g.ps[6][:, 0:SEG], g2s[:, 0, :], g.tg[:, 0, :], start=True, stop=False)
                    pe.matmul(g.ps[6][:, 0:SEG], g2s[:, 1, :], g.tg[:, 1, :], start=False, stop=True).then_inc(S["lora_mm"], 1)
                    W(pe, "kksq", i, 1, 1)
                    pe.matmul(g.ps[7][:, :], g.bones[:, :], t2[:, :], start=True, stop=True).then_inc(S["kksum"], 1)

                def bonus_sums(i):
                    W(pe, "gate", i, 1, 1)
                    W(pe, "bonus_in", i, 1, 1)
                    pe.matmul(g.ps[6][:, 0:SEG], g.bones[:, :], bon[:, :], start=True, stop=True).then_inc(S["bonus_mm"], 1)

                def core(i, nxt):
                    W(pe, "kmod", i, 1, 1)
                    W(pe, "iclr", i, 1, 1)
                    W(pe, "kkroot", i, 1, 1)
                    for d in range(2):
                        B = 4 * d
                        W(pe, "hats", i, 2, d + 1)
                        paired(B, tk(bh[d]), both(ah[d]), ALL).then_inc(S["mm1"], 1)
                        each(B + 1, 0, blk(ah[d]), tk(bh[d]), ALL).then_inc(S["mm1"], 1)
                        paired(B + 2, tk(kh[d]), both(ah[d]), ALL).then_inc(S["mm1"], 1)
                        paired(B + 3, tk(bh[d]), both(rh[d], LAT), LATS)
                        paired(B + 3, tk(kh[d]), both(rh[d], LAT), LATS, SEG).then_inc(S["mm1"], 1)

                    def pmm(n):
                        lv, d, c0 = unit(n)
                        if n == NU:
                            return
                        if n >= 4:
                            W(pe, "xadd", i, 2 * NU, 2 * (n - 3))
                        elif n % 2 == 0:
                            W(pe, "x0", i, 2, d + 1)
                        if n % 2 == 0:
                            W(pe, "nlev", i, 10, 2 * lv + d + 1)
                        if n >= 2:
                            W(pe, "pcopy", i, NU, n - 1)
                        apart()
                        for c in range(LAT):
                            mm = pe.matmul(g.ps[n % 2][:, c * P:(c + 1) * P], nlev[d][:, lv % 2, c0 + c, :, :].rearrange("p h t -> p (h t)"), full(x[d], c0 + c), start=True, stop=True)
                        mm.then_inc(S["pmm"], 1)

                    def xmm(n):
                        lv, d, c0 = unit(n)
                        W(pe, "pcopy", i, NU, n + 1)
                        if n >= 2:
                            W(pe, "xadd", i, 2 * NU, 2 * (n - 1))
                        apart()
                        for c in range(LAT):
                            if lv < 4:
                                pe.matmul(g.ps[2 + 2 * (n % 2)][:, c * P:(c + 1) * P], full(xt[d], c0 + c), full(pp[d], c0 + c), start=True, stop=True)
                        for c in range(LAT):
                            mm = pe.matmul(g.ps[5 + n % 2][:, c * P:(c + 1) * P], full(pp[d], c0 + c), full(xt[d], c0 + c), start=True, stop=True)
                        mm.then_inc(S["xmm"], 1)

                    def steps(lo, hi):
                        for n in range(lo, hi):
                            pmm(n + 1)
                            xmm(n)

                    def tok(src, bank, former):
                        if former is not None:
                            W(pe, "tok", i, 7, former)
                        if src in ah:
                            each(bank, 0, blk(src), lambda c, h: g.i64[:, :], ALL).then_inc(S["tokmm"], 1)
                        else:
                            paired(bank, tk(src), lambda c: g.ident[:, :], ALL).then_inc(S["tokmm"], 1)

                    pmm(0)
                    W(pe, "x0", i, 2, 2)
                    W(pe, "mask", i, 4, 1)
                    steps(0, 1)
                    W(pe, "mask", i, 4, 2)
                    steps(1, 2)
                    W(pe, "mask", i, 4, 3)
                    tok(v0, 3, None)
                    W(pe, "mask", i, 4, 4)
                    tok(ah[0], 7, None)
                    steps(2, 3)
                    tok(ah[1], 3, 1)
                    steps(3, 4)
                    W(pe, "bars", i, 4, 4)
                    tok(bbar[0], 7, 2)
                    steps(4, 6)
                    tok(bbar[1], 3, 3)
                    steps(6, 8)
                    tok(kbar[0], 7, 4)
                    steps(8, 10)
                    tok(kbar[1], 3, 5)
                    steps(10, 13)
                    W(pe, "tok", i, 7, 7)
                    for d in range(2):
                        paired(4 * d + 3, ch(nk[d]), both(vt), ALL).then_inc(S["nkvmm"], 1)
                    steps(13, NU)
                    for d in range(2):
                        B = 4 * d
                        W(pe, "xadd", i, 2 * NU, 2 * NU - 4 * (1 - d))
                        W(pe, "nkv", i, 2, d + 1)
                        apart()
                        for c in ALL:
                            mm = pe.matmul(g.ps[B + c // LAT][:, c % LAT * P:(c % LAT + 1) * P], full(xt[d], c), rhs[d][:, c, :, :].rearrange("p k t -> p (k t)"), start=True, stop=True)
                        mm.then_inc(S["aumm"], 1)
                    for d in range(2):
                        B = 4 * d
                        W(pe, "au", i, 4, 2 * d + 2)
                        W(pe, "au_late", i, 4, 2 * d + 2)
                        apart()
                        for c in ALL:
                            mm = pe.matmul(g.ps[B + 2 + c // LAT][:, c % LAT * P:(c % LAT + 1) * P], au[d][:, c, 0, :, :].rearrange("p h t -> p (h t)"),
                                           brr[d][:, c, 0:2, :].rearrange("p k t -> p (k t)"), start=True, stop=True)
                        mm.then_inc(S["gmm"], 1)
                    def own(k):
                        for d in range(2):
                            c = ORDER[d][k]
                            for h, r in enumerate(HALF):
                                o = g.ps[4 * d + k % 2][r, k * LC:(k + 1) * LC]
                                pe.matmul(o, bt[d][:, c, :], au[d][:, c, 1, h, :], start=True, stop=False)
                                mm = pe.matmul(o, kt[d][:, c, :], vt[:, c, h, :], start=False, stop=(k == 0))
                            if k == 0:
                                mm.then_inc(S["smm"], 1)

                    apart()
                    own(0)
                    W(pe, "gt", i, 12, 12)
                    if nxt is not None:
                        lora(nxt)
                    between = {1: gate_sums, 5: bonus_sums} if nxt is not None else {}
                    for k in range(1, NCH - 1):
                        own(k)
                        W(pe, "scopy", i, 14, 2 * k)
                        apart()
                        for d in range(2):
                            c = ORDER[d][k]
                            for h, r in enumerate(HALF):
                                mm = pe.matmul(g.ps[4 * d + k % 2][r, k * LC:(k + 1) * LC], gt[d][:, c, h, :], st[d][:, c, :], start=False, stop=True)
                            mm.then_inc(S["smm"], 1)
                        if k in between:
                            between[k](nxt)
                    W(pe, "scopy", i, 14, 14)
                    apart()
                    for c in LATS:
                        for h, r in enumerate(HALF):
                            o = g.ps[3][r, (c - LAT) * LC:(c - LAT + 1) * LC]
                            for d in range(2):
                                pe.matmul(o, rt[d][:, c - LAT, h, :], st[d][:, c, :], start=(d == 0), stop=False)
                                pe.matmul(o, brr[d][:, c, 1, :], au[d][:, c, 1, h, :], start=False, stop=False)
                                mm = pe.matmul(o, brr[d][:, c, 2, :], vt[:, c, h, :], start=False, stop=(d == 1))
                    mm.then_inc(S["ymm"], 1)
                    W(pe, "yn", i, 1, 1)
                    if nxt is not None:
                        W(pe, "iclr", nxt, 1, 1)
                    each(2, 0, ch(yn), eye, range(LAT)).then_inc(S["ytmm"], 1)
                    pe.wait_ge(S["pass_end"], i + 1)

                lora(0)
                gate_sums(0)
                bonus_sums(0)
                with pe.Fori(0, DC - 1) as i:
                    core(i, i + 1)
                core(DC - 1, None)


def program(nc, a, out):
    with ExitStack() as ctx:
        g = setup(nc, ctx, a)
        g.eps = g.place(ctx, "eps", [P, 2])
        g.eps2 = g.place(ctx, "eps_kk", [P, 1])
        with nc.Block() as block:
            @block.vector
            def _(dve):
                dve.memset(g.eps[:, 0:1], EPS)
                dve.memset(g.eps[:, 1:2], RW_EPS)
                dve.memset(g.eps2[:, 0:1], 1.0e-12)
        stage_constants_and_modulation(g)
        layer0(g)
        restart_semaphores(g)
        layer1(g, out)


def restart_semaphores(g):
    g.nc.clear_and_free_semaphores(g.passing)
    g.nc.all_engine_barrier()
    g.passing = []


def layer0(g):
    nc = g.nc
    with ExitStack() as ctx:
        sb = lambda name, shape: g.place(ctx, name, shape)
        g.mixT = sb("mixT", [P, 16, T])
        g.z = sb("z_gate", [P, NT, D])
        g.dt = sb("dt_raw", [48, T])
        g.xc = sb("conv_out", [P, CT, T])
        g.hT = g.mixT[:, 0:8, :]
        with ExitStack() as ml:
            sb = lambda name, shape: g.place(ml, name, shape)
            g.o = sb("o_gate", [P, NT, D])
            g.v = sb("v_ext", [P, NT, ML_H, ML_DV + 1])
            g.qT = sb("qT", [P, ML_H, T])
            g.kT = sb("kT", [P, ML_H, T])
            g.ig, g.fg = sb("ig", [36, T]), sb("fg", [36, T])
            g.xn = g.o
            stage_norm(g, 0, 0, 0, ctx)
            with nc.sbuf_tensor("conv_in", [P, CT, T], F32) as g.xbc:
                stage_project(g)
            stage_mlstm(g)
        stage_ssd(g)
        stage_out(g, 0, g.a["ab_w_out"][0], 16, g.mixT, 0)
    restart_semaphores(g)
    stage_moe(g, 0, 0)


def layer1(g, out):
    nc = g.nc
    with ExitStack() as ctx:
        sb = lambda name, shape: g.place(ctx, name, shape)
        g.yT = sb("rwkv_out", [P, DC, SEG])
        with ExitStack() as rw:
            sb = lambda name, shape: g.place(rw, name, shape)
            g.tw, g.ta, g.tg = sb("rw_tanh", [P, T]), sb("rw_a_in", [P, T]), sb("rw_g_in", [P, 2, SEG])
            with g.nc.Block() as block:
                @block.gpsimd
                def _(pool):
                    pool.memset(g.ta[:, :], 0.0)
                    pool.memset(g.tg[:, :, :], 0.0)
            with ExitStack() as pr:
                sp_ = lambda name, shape: g.place(pr, name, shape)
                g.kT, g.vT, g.rT = sp_("rw_k", [P, DC, T]), sp_("rw_v", [P, DC, T]), sp_("rw_r", [P, DC, SEG])
                g.hT = g.place(pr, "rw_hT", [P, DC, T])
                with ExitStack() as nr:
                    g.xn = g.place(nr, "rw_xn", [P, NT, D])
                    stage_norm(g, 1, 0, 0, nr)
                stage_rwkv_project(g)
            with ExitStack() as mk:
                m = lambda name, shape: g.place(mk, name, shape)
                g.lev, g.i64, g.bones = m("level_masks", [P, 2, 6, LC]), m("eye64", [P, LC]), m("block_ones", [P, P])
                g.inc, g.strict = m("mask_inc", [P, 2, LC]), m("mask_strict", [P, 2, LC])
                stage_rwkv_masks(g)
                stage_rwkv(g)
        stage_out(g, 1, g.a["rw_wo"][0], DC, LatOnly(g.yT), 2)
    stage_moe(g, 1, 2, out)


class LatOnly:

    def __init__(self, x):
        self.x = x

    def __getitem__(self, at):
        p, k, t = at
        return self.x[p, k, t.start - SEG:t.stop - SEG]


_INS = ["x", "c", "ctx", "c_ctx", "ada_w", "ada_b", "norm_g", "router_w", "exp_w1", "exp_w3", "exp_w2",
        "ab_w_in", "ab_w_out", "ml_gate_b", "ml_norm_g", "ss_conv_w", "ss_conv_b", "ss_dt_bias", "ss_A_log", "ss_D", "ss_norm_g",
        "rw_mu", "rw_wr", "rw_wk", "rw_wv", "rw_wo", "rw_w0", "rw_w1", "rw_w2", "rw_a0", "rw_a1", "rw_a2", "rw_g1", "rw_g2",
        "rw_kk", "rw_ka", "rw_rk", "rw_lnx_g", "rw_lnx_b"]


def kernel(**inputs):
    import numpy as _np
    import concourse.bacc as _bacc
    from concourse import mybir as _mybir
    from concourse.bass_utils import run_bass_kernel_spmd as _run

    nc = _bacc.Bacc("TRN2", target_bir_lowering=False, num_devices=1)
    arrays, args = {}, {}
    for name in _INS:
        a = _np.ascontiguousarray(inputs[name])
        arrays[f"in_{name}"] = a
        args[name] = nc.dram_tensor(f"in_{name}", a.shape, _mybir.dt.from_np(a.dtype), kind="ExternalInput").ap()
    out = nc.dram_tensor("out_0", (1, SEG, D), F32, kind="ExternalOutput").ap()
    program(nc, args, out)
    r = _run(nc, [arrays], core_ids=[0])
    return r.results[0]["out_0"]
```
